# Optimizing a Trainium2 kernel written in Bass

```python
import jax, jax.numpy as jnp
from jax import lax
import numpy as np
import math

D_MODEL = 1024
BATCH = 1
SEQ = 256
DEPTH = 1

GRID_W = 64
CTX_LEN = 256
ATT_HEADS = 8
ATT_KV_HEADS = 2
ATT_GROUP = ATT_HEADS // ATT_KV_HEADS
ATT_HEAD_DIM = 64
ATT_WIDTH = ATT_HEADS * ATT_HEAD_DIM
ATT_KV_WIDTH = ATT_KV_HEADS * ATT_HEAD_DIM
WINDOW = 128
BLOCK = 128
ROPE_BASE = 10000.0
HG_WIDTH = D_MODEL // 2
HG_EXPAND = 128
HG_HEADS = HG_WIDTH // HG_EXPAND
CHUNK = 64
D_FF = 2816
N_MOD = 9
IN_WIDTH = ATT_WIDTH + 2 * ATT_KV_WIDTH + 5 * HG_WIDTH + 2 * D_MODEL
EPS = 1e-6
NEG_INF = -1e30


def rmsnorm(x, g):
    x32 = x.astype(jnp.float32)
    y = x32 * lax.rsqrt(jnp.mean(x32 * x32, axis=-1, keepdims=True) + EPS)
    return (y * g.astype(jnp.float32)).astype(x.dtype)

def swiglu(h, w_in, w_out):
    gate, up = jnp.split(h @ w_in, 2, axis=-1)
    return (jax.nn.silu(gate) * up) @ w_out

def ada_pre(z, g, shift, scale):
    return rmsnorm(z, g) * (1 + scale) + shift

def ada_post(z, y, g, gate, w):
    return z + w * gate * rmsnorm(y, g)

def rope_1d(x, pos):
    half = x.shape[-1] // 2
    freqs = ROPE_BASE ** (-jnp.arange(half, dtype=jnp.float32) / half)
    ang = pos.astype(jnp.float32)[:, None] * freqs[None, :]
    cos, sin = jnp.cos(ang).astype(x.dtype), jnp.sin(ang).astype(x.dtype)
    x1, x2 = x[..., :half], x[..., half:]
    return jnp.concatenate([x1 * cos - x2 * sin, x1 * sin + x2 * cos], axis=-1)

def rope_2d(x, row, col):
    h = x.shape[-1] // 2
    return jnp.concatenate([rope_1d(x[..., :h], row), rope_1d(x[..., h:], col)], axis=-1)

def split_in(p):
    sizes = (ATT_WIDTH, ATT_KV_WIDTH, ATT_KV_WIDTH, HG_WIDTH, HG_WIDTH, HG_WIDTH, HG_WIDTH, HG_WIDTH, D_MODEL, D_MODEL)
    points = [int(v) for v in np.cumsum(sizes)[:-1]]
    return jnp.split(p, points, axis=-1)

def q_heads(z):
    B, T, _ = z.shape
    return z.reshape(B, T, ATT_KV_HEADS, ATT_GROUP, ATT_HEAD_DIM).transpose(0, 2, 3, 1, 4)

def kv_heads(z):
    B, T, _ = z.shape
    return z.reshape(B, T, ATT_KV_HEADS, ATT_HEAD_DIM).transpose(0, 2, 1, 3)

def hg_heads(z):
    B, T, _ = z.shape
    return z.reshape(B, T, HG_HEADS, HG_EXPAND).transpose(0, 2, 1, 3)

def hg_merge(o):
    B, H, T, d = o.shape
    return o.transpose(0, 2, 1, 3).reshape(B, T, H * d)

def softmax_with_sink(logits, sink):
    sink_col = jnp.broadcast_to(sink, logits.shape[:-1] + (1,))
    p = jax.nn.softmax(jnp.concatenate([logits, sink_col], axis=-1), axis=-1)
    return p[..., :-1]

def window_attention(q, k, v, kc, vc, sink):
    B, KVH, G, T, hd = q.shape
    nb = T // BLOCK
    scale = hd ** -0.5
    qb = q.reshape(B, KVH, G, nb, BLOCK, hd)

    def band(z):
        zp = jnp.pad(z, ((0, 0), (0, 0), (BLOCK, BLOCK), (0, 0))).reshape(B, KVH, nb + 2, BLOCK, hd)
        return jnp.concatenate([zp[:, :, :nb], zp[:, :, 1:nb + 1], zp[:, :, 2:]], axis=3)

    kb, vb = band(k), band(v)
    blk = jnp.arange(nb)[:, None, None] * BLOCK
    qpos = blk + jnp.arange(BLOCK)[None, :, None]
    kpos = blk - BLOCK + jnp.arange(3 * BLOCK)[None, None, :]
    valid = (jnp.abs(kpos - qpos) <= WINDOW) & (kpos >= 0) & (kpos < T)
    s_band = jnp.einsum('bkgnqd,bknsd->bkgnqs', qb, kb).astype(jnp.float32) * scale
    s_band = jnp.where(valid, s_band, NEG_INF)
    s_ctx = jnp.einsum('bkgnqd,bksd->bkgnqs', qb, kc).astype(jnp.float32) * scale
    sink_b = sink.astype(jnp.float32).reshape(KVH, G)[None, :, :, None, None, None]
    p = softmax_with_sink(jnp.concatenate([s_band, s_ctx], axis=-1), sink_b).astype(v.dtype)
    o = (jnp.einsum('bkgnqs,bknsd->bkgnqd', p[..., :3 * BLOCK], vb)
         + jnp.einsum('bkgnqs,bksd->bkgnqd', p[..., 3 * BLOCK:], vc))
    return o.reshape(B, KVH, G, T, hd).transpose(0, 3, 1, 2, 4).reshape(B, T, KVH * G * hd)

def context_attention(qc, kc, vc, sink):
    B, KVH, G, L, hd = qc.shape
    s = jnp.einsum('bkgqd,bksd->bkgqs', qc, kc).astype(jnp.float32) * (hd ** -0.5)
    sink_b = sink.astype(jnp.float32).reshape(KVH, G)[None, :, :, None, None]
    p = softmax_with_sink(s, sink_b).astype(vc.dtype)
    o = jnp.einsum('bkgqs,bksd->bkgqd', p, vc)
    return o.transpose(0, 3, 1, 2, 4).reshape(B, L, KVH * G * hd)

def gated_scan(q, k, v, logf, s0):
    B, H, T, dk = q.shape
    dv = v.shape[-1]
    n = T // CHUNK

    def chunks(z):
        return jnp.moveaxis(z.reshape(B, H, n, CHUNK, z.shape[-1]), 2, 0)

    tril = jnp.tril(jnp.ones((CHUNK, CHUNK), dtype=bool))

    def step(S, inp):
        qc, kc, vc, lf = inp
        b = jnp.cumsum(lf, axis=-2)
        o_inter = jnp.einsum('bhtd,bhde->bhte', qc * jnp.exp(b), S)
        diff = b[:, :, :, None, :] - b[:, :, None, :, :]
        decay = jnp.where(tril[:, :, None], jnp.exp(jnp.minimum(diff, 0.0)), 0.0)
        scores = jnp.einsum('bhtsd,bhsd->bhts', qc[:, :, :, None, :] * decay, kc)
        o_intra = jnp.einsum('bhts,bhse->bhte', scores, vc)
        b_last = b[:, :, -1:, :]
        k_dec = kc * jnp.exp(b_last - b)
        S_new = jnp.exp(b_last[:, :, 0, :])[..., None] * S + jnp.einsum('bhsd,bhse->bhde', k_dec, vc)
        return S_new, o_inter + o_intra

    S_fin, o = lax.scan(step, s0, (chunks(q), chunks(k), chunks(v), chunks(logf)))
    return jnp.moveaxis(o, 0, 2).reshape(B, H, T, dv), S_fin

def hgrn_bidir(q, v, lf_f, k_f, lf_b, k_b, s0_f, s0_b):
    flip = lambda z: jnp.flip(z, axis=2)
    o_f, s_f = gated_scan(q, k_f, v, lf_f, s0_f)
    o_b, s_b = gated_scan(flip(q), flip(k_b), flip(v), flip(lf_b), s0_b)
    return o_f + flip(o_b), s_f, s_b

def hg_forget(z, lb):
    f = lb + (1.0 - lb) * jax.nn.sigmoid(z.astype(jnp.float32))
    return hg_heads(jnp.log(f)), hg_heads(1.0 - f)

def mixer(h, hc, w_in, sink, lb_f, lb_b, g_hnorm, w_o_attn, w_o_hgrn, w_out, need_ctx):
    B, T, _ = h.shape
    rows = T // GRID_W
    row = jnp.repeat(jnp.arange(rows, dtype=jnp.int32), GRID_W)
    col = jnp.tile(jnp.arange(GRID_W, dtype=jnp.int32), rows)
    f32 = jnp.float32
    aq, ak, av, hq, hff, hfb, hi, hg, ga, gh = split_in(h @ w_in)
    aqc, akc, avc, hqc, hffc, hfbc, hic, hgc, gac, ghc = split_in(hc @ w_in)
    q = rope_2d(q_heads(aq), row, col)
    k = rope_2d(kv_heads(ak), row, col)
    kc, vc = kv_heads(akc), kv_heads(avc)
    o_att = window_attention(q, k, kv_heads(av), kc, vc, sink)
    qhc = hg_heads(jax.nn.silu(hqc.astype(f32)))
    vhc = hg_heads(hic.astype(f32))
    lfc_f, kc_f = hg_forget(hffc, lb_f)
    lfc_b, kc_b = hg_forget(hfbc, lb_b)
    s0 = jnp.zeros((B, HG_HEADS, HG_EXPAND, HG_EXPAND), f32)
    o_hc, s_f, s_b = hgrn_bidir(qhc, vhc, lfc_f, kc_f, lfc_b, kc_b, s0, s0)
    qh = hg_heads(jax.nn.silu(hq.astype(f32)))
    vh = hg_heads(hi.astype(f32))
    lf_f, k_f = hg_forget(hff, lb_f)
    lf_b, k_b = hg_forget(hfb, lb_b)
    o_h, _, _ = hgrn_bidir(qh, vh, lf_f, k_f, lf_b, k_b, s_f, s_b)

    def readout(o, gate):
        return rmsnorm(hg_merge(o), g_hnorm).astype(gate.dtype) * jax.nn.silu(gate)

    def merge(o_a, o_r, g_a, g_r):
        return (jax.nn.sigmoid(g_a) * (o_a @ w_o_attn) + jax.nn.sigmoid(g_r) * (o_r @ w_o_hgrn)) @ w_out

    y = merge(o_att, readout(o_h, hg), ga, gh)
    if not need_ctx:
        return y, None
    o_attc = context_attention(q_heads(aqc), kc, vc, sink)
    yc = merge(o_attc, readout(o_hc, hgc), gac, ghc)
    return y, yc

def first_inputs(seed: int = 0) -> dict:
    key = jax.random.key(seed)
    ks = jax.random.split(key, 20)
    f32 = jnp.float32

    def nrm(k, shape, scale):
        return jax.random.normal(k, shape, f32) * scale

    D = D_MODEL
    return {
        'x': nrm(ks[0], (BATCH, SEQ, D), 1.0),
        'c': nrm(ks[1], (BATCH, D), 1.0),
        'ctx': nrm(ks[2], (BATCH, CTX_LEN, D), 1.0),
        'c_ctx': nrm(ks[3], (D,), 1.0),
        'w_ada': nrm(ks[4], (DEPTH, D, N_MOD * D), 0.5 * D ** -0.5),
        'b_ada': nrm(ks[5], (DEPTH, N_MOD * D), 0.02),
        'norm_pre': 1.0 + nrm(ks[6], (DEPTH, 3, D), 0.02),
        'norm_post': 1.0 + nrm(ks[7], (DEPTH, 3, D), 0.02),
        'ffn1_w_in': nrm(ks[8], (DEPTH, D, 2 * D_FF), D ** -0.5),
        'ffn1_w_out': nrm(ks[9], (DEPTH, D_FF, D), D_FF ** -0.5),
        'ffn2_w_in': nrm(ks[10], (DEPTH, D, 2 * D_FF), D ** -0.5),
        'ffn2_w_out': nrm(ks[11], (DEPTH, D_FF, D), D_FF ** -0.5),
        'mix_w_in': nrm(ks[12], (DEPTH, D, IN_WIDTH), D ** -0.5),
        'attn_sink': nrm(ks[13], (DEPTH, ATT_HEADS), 0.5),
        'hgrn_lb_fwd': nrm(ks[14], (DEPTH + 1, HG_WIDTH), 0.5),
        'hgrn_lb_bwd': nrm(ks[15], (DEPTH + 1, HG_WIDTH), 0.5),
        'hgrn_norm': 1.0 + nrm(ks[16], (DEPTH, HG_WIDTH), 0.02),
        'w_o_attn': nrm(ks[17], (DEPTH, ATT_WIDTH, D), ATT_WIDTH ** -0.5),
        'w_o_hgrn': nrm(ks[18], (DEPTH, HG_WIDTH, D), HG_WIDTH ** -0.5),
        'w_out': nrm(ks[19], (DEPTH, D, D), D ** -0.5),
    }

def first_block(x, c, ctx, c_ctx, w_ada, b_ada, norm_pre, norm_post, ffn1_w_in, ffn1_w_out,
              ffn2_w_in, ffn2_w_out, mix_w_in, attn_sink, hgrn_lb_fwd, hgrn_lb_bwd, hgrn_norm,
              w_o_attn, w_o_hgrn, w_out):
    B, T, D = x.shape
    lb_f_all = jnp.cumsum(jax.nn.softmax(hgrn_lb_fwd.astype(jnp.float32), axis=0), axis=0)
    lb_b_all = jnp.cumsum(jax.nn.softmax(hgrn_lb_bwd.astype(jnp.float32), axis=0), axis=0)
    xc = ctx
    for l in range(DEPTH):
        need_ctx = l < DEPTH - 1
        mod = (jax.nn.silu(c) @ w_ada[l] + b_ada[l]).reshape(B, N_MOD, 1, D)
        mod_c = (jax.nn.silu(c_ctx) @ w_ada[l] + b_ada[l]).reshape(N_MOD, D)
        m = [mod[:, j] for j in range(N_MOD)]
        mc = [mod_c[j] for j in range(N_MOD)]
        h = ada_pre(x, norm_pre[l, 0], m[0], m[1])
        x = ada_post(x, swiglu(h, ffn1_w_in[l], ffn1_w_out[l]), norm_post[l, 0], m[2], 0.5)
        hc = ada_pre(xc, norm_pre[l, 0], mc[0], mc[1])
        xc = ada_post(xc, swiglu(hc, ffn1_w_in[l], ffn1_w_out[l]), norm_post[l, 0], mc[2], 0.5)
        h = ada_pre(x, norm_pre[l, 1], m[3], m[4])
        hc = ada_pre(xc, norm_pre[l, 1], mc[3], mc[4])
        y, yc = mixer(h, hc, mix_w_in[l], attn_sink[l], lb_f_all[l], lb_b_all[l], hgrn_norm[l],
                      w_o_attn[l], w_o_hgrn[l], w_out[l], need_ctx)
        x = ada_post(x, y, norm_post[l, 1], m[5], 1.0)
        h = ada_pre(x, norm_pre[l, 2], m[6], m[7])
        x = ada_post(x, swiglu(h, ffn2_w_in[l], ffn2_w_out[l]), norm_post[l, 2], m[8], 0.5)
        if need_ctx:
            xc = ada_post(xc, yc, norm_post[l, 1], mc[5], 1.0)
            hc = ada_pre(xc, norm_pre[l, 2], mc[6], mc[7])
            xc = ada_post(xc, swiglu(hc, ffn2_w_in[l], ffn2_w_out[l]), norm_post[l, 2], mc[8], 0.5)
    return x


DEPTH_2 = 2

Q_BLOCK = 128
NEG_INF_2 = -1e30
LN_EPS = 1e-5
RMS_EPS = 1e-6

MLA_HEADS = 4
MLA_Q_RANK = 256
MLA_KV_RANK = 128
MLA_NOPE = 64
MLA_ROPE = 32
MLA_V = 64
ROPE_THETA = 10000.0

SB_HEADS = 4
SB_DIM = 64

SW_Q_HEADS = 8
SW_KV_HEADS = 2
SW_DIM = 64
SW_WINDOW = 128

DF_HEADS = 4
DF_DIM = 32
DF_VDIM = 2 * DF_DIM

A_WIDTH = MLA_HEADS * MLA_V
B_WIDTH = SB_HEADS * SB_DIM
C_WIDTH = SW_Q_HEADS * SW_DIM
D_WIDTH = DF_HEADS * DF_VDIM
N_BRANCH = 4

IN_SPLITS = (MLA_Q_RANK, MLA_KV_RANK, MLA_ROPE, 3 * B_WIDTH, C_WIDTH, 2 * SW_KV_HEADS * SW_DIM, 2 * DF_HEADS * DF_DIM, 2 * DF_HEADS * DF_DIM, D_WIDTH)
IN_WIDTH_2 = sum(IN_SPLITS)

N_EXPERTS = 32
N_GROUPS = 8
EXPERTS_PER_GROUP = N_EXPERTS // N_GROUPS
GROUP_SCORE_TOP = 2
TOP_K = 2
D_EXPERT = 256
MOE_BLOCK = 256

DN_ALPHA = (2 * DEPTH_2) ** 0.25
DN_BETA = (8 * DEPTH_2) ** -0.25


def layer_norm(x, g, b):
    xf = x.astype(jnp.float32)
    mu = xf.mean(-1, keepdims=True)
    var = jnp.square(xf - mu).mean(-1, keepdims=True)
    return ((xf - mu) * lax.rsqrt(var + LN_EPS) * g.astype(jnp.float32) + b.astype(jnp.float32)).astype(x.dtype)

def rms_norm(x, g):
    xf = x.astype(jnp.float32)
    return (xf * lax.rsqrt(jnp.mean(xf * xf, -1, keepdims=True) + RMS_EPS) * g.astype(jnp.float32)).astype(x.dtype)

def apply_rope(t, positions):
    half = t.shape[-1] // 2
    inv_freq = ROPE_THETA ** (-jnp.arange(half, dtype=jnp.float32) / half)
    ang = positions.astype(jnp.float32)[:, None] * inv_freq[None, :]
    cos = jnp.cos(ang)[None, :, None, :]
    sin = jnp.sin(ang)[None, :, None, :]
    tf = t.astype(jnp.float32)
    t1, t2 = tf[..., :half], tf[..., half:]
    return jnp.concatenate([t1 * cos - t2 * sin, t1 * sin + t2 * cos], axis=-1).astype(t.dtype)

def alibi_slopes(n_heads):
    return 2.0 ** (-8.0 * jnp.arange(1, n_heads + 1, dtype=jnp.float32) / n_heads)

def _to_blocks(t):
    b, s = t.shape[:2]
    return t.reshape(b, s // Q_BLOCK, Q_BLOCK, *t.shape[2:]).swapaxes(0, 1)

def _from_blocks(o):
    nq, b, qb = o.shape[:3]
    return o.swapaxes(0, 1).reshape(b, nq * qb, *o.shape[3:])

def mla_attention(q_nope, q_rope, k_nope, k_rope, v):
    s_len = q_nope.shape[1]
    scale = (MLA_NOPE + MLA_ROPE) ** -0.5
    kidx = jnp.arange(s_len)

    def block(args):
        qn, qr, i = args
        qidx = i * Q_BLOCK + jnp.arange(Q_BLOCK)
        sc = (jnp.einsum('bqhd,bkhd->bhqk', qn, k_nope, preferred_element_type=jnp.float32)
              + jnp.einsum('bqhd,bkd->bhqk', qr, k_rope, preferred_element_type=jnp.float32)) * scale
        sc = jnp.where(kidx[None, :] <= qidx[:, None], sc, NEG_INF_2)
        p = jax.nn.softmax(sc, axis=-1)
        return jnp.einsum('bhqk,bkhd->bqhd', p.astype(v.dtype), v)

    out = lax.map(block, (_to_blocks(q_nope), _to_blocks(q_rope), jnp.arange(s_len // Q_BLOCK)))
    return _from_blocks(out)

def stick_breaking_attention(q, k, v):
    s_len = q.shape[1]
    scale = SB_DIM ** -0.5
    kidx = jnp.arange(s_len)

    def block(args):
        qb, i = args
        qidx = i * Q_BLOCK + jnp.arange(Q_BLOCK)
        z = jnp.einsum('bqhd,bkhd->bhqk', qb, k, preferred_element_type=jnp.float32) * scale
        mask = kidx[None, :] < qidx[:, None]
        log_beta = jax.nn.log_sigmoid(z)
        log_1m_beta = jnp.where(mask, log_beta - z, 0.0)
        suffix = lax.cumsum(log_1m_beta, axis=3, reverse=True) - log_1m_beta
        a = jnp.where(mask, jnp.exp(log_beta + suffix), 0.0)
        return jnp.einsum('bhqk,bkhd->bqhd', a.astype(v.dtype), v)

    out = lax.map(block, (_to_blocks(q), jnp.arange(s_len // Q_BLOCK)))
    return _from_blocks(out)

def sliding_window_attention(q, k, v, sinks, slopes, positions):
    b, s_len, _, d = q.shape
    w = SW_WINDOW
    nb = s_len // w
    g = SW_Q_HEADS // SW_KV_HEADS
    qb = q.reshape(b, nb, w, SW_KV_HEADS, g, d)

    def band(t):
        tb = t.reshape(b, nb, w, SW_KV_HEADS, d)
        prev = jnp.pad(tb[:, :-1], ((0, 0), (1, 0), (0, 0), (0, 0), (0, 0)))
        return jnp.concatenate([prev, tb], axis=2)

    kb, vb = band(k), band(v)
    pq = positions.astype(jnp.float32).reshape(nb, w)
    pk = jnp.concatenate([jnp.pad(pq[:-1], ((1, 0), (0, 0))), pq], axis=1)
    dist = pq[:, :, None] - pk[:, None, :]
    qi = jnp.arange(w)[:, None]
    kj = jnp.arange(2 * w)[None, :]
    offset = qi + w - kj
    in_window = (offset >= 0) & (offset < SW_WINDOW)
    key_exists = (jnp.arange(nb)[:, None, None] > 0) | (kj[None] >= w)
    mask = (in_window[None] & key_exists)[None, :, None, None]
    sc = jnp.einsum('bnqhgd,bnkhd->bnhgqk', qb, kb, preferred_element_type=jnp.float32) * (d ** -0.5)
    bias = -slopes.reshape(SW_KV_HEADS, g)[None, None, :, :, None, None] * dist[None, :, None, None]
    sc = jnp.where(mask, sc + bias, NEG_INF_2)
    sink = jnp.broadcast_to(sinks.astype(jnp.float32).reshape(SW_KV_HEADS, g)[None, None, :, :, None, None], sc.shape[:-1] + (1,))
    p = jax.nn.softmax(jnp.concatenate([sc, sink], axis=-1), axis=-1)[..., :-1]
    out = jnp.einsum('bnhgqk,bnkhd->bnqhgd', p.astype(v.dtype), vb)
    return out.reshape(b, s_len, SW_Q_HEADS, d)

def diff_attention(q1, q2, k1, k2, v, lam, slopes, positions):
    s_len, d = q1.shape[1], q1.shape[3]
    scale = d ** -0.5
    kidx = jnp.arange(s_len)
    kpos = positions.astype(jnp.float32)

    def block(args):
        a1, a2, i = args
        qidx = i * Q_BLOCK + jnp.arange(Q_BLOCK)
        qpos = lax.dynamic_slice(kpos, (i * Q_BLOCK,), (Q_BLOCK,))
        causal = kidx[None, :] <= qidx[:, None]
        bias = -slopes[:, None, None] * (qpos[:, None] - kpos[None, :])[None]

        def attn_map(a, kk):
            sc = jnp.einsum('bqhd,bkhd->bhqk', a, kk, preferred_element_type=jnp.float32) * scale + bias
            return jax.nn.softmax(jnp.where(causal, sc, NEG_INF_2), axis=-1)

        p = attn_map(a1, k1) - lam * attn_map(a2, k2)
        return jnp.einsum('bhqk,bkhd->bqhd', p.astype(v.dtype), v)

    out = lax.map(block, (_to_blocks(q1), _to_blocks(q2), jnp.arange(s_len // Q_BLOCK)))
    return _from_blocks(out)

def token_mixers(x, positions, lam_init, w_in, q_norm, kv_norm, w_uq, w_ukv, sinks,
                 lq1, lk1, lq2, lk2, subln, w_gate, b_gate, w_br_a, w_br_b, w_br_c, w_br_d, w_out):
    b, s_len, _ = x.shape
    h = jnp.einsum('bsd,de->bse', x, w_in)
    split_at = [int(c) for c in np.cumsum(IN_SPLITS)[:-1]]
    c_q, c_kv, k_rope_raw, sb_qkv, sw_q, sw_kv, df_q, df_k, df_v = jnp.split(h, split_at, axis=-1)

    q = jnp.einsum('bsr,re->bse', rms_norm(c_q, q_norm), w_uq).reshape(b, s_len, MLA_HEADS, MLA_NOPE + MLA_ROPE)
    q_nope = q[..., :MLA_NOPE]
    q_rope = apply_rope(q[..., MLA_NOPE:], positions)
    kv = jnp.einsum('bsr,re->bse', rms_norm(c_kv, kv_norm), w_ukv).reshape(b, s_len, MLA_HEADS, MLA_NOPE + MLA_V)
    k_nope, v_a = kv[..., :MLA_NOPE], kv[..., MLA_NOPE:]
    k_rope = apply_rope(k_rope_raw[:, :, None, :], positions)[:, :, 0]
    o_a = mla_attention(q_nope, q_rope, k_nope, k_rope, v_a).reshape(b, s_len, A_WIDTH)

    sb = sb_qkv.reshape(b, s_len, 3, SB_HEADS, SB_DIM)
    o_b = stick_breaking_attention(sb[:, :, 0], sb[:, :, 1], sb[:, :, 2]).reshape(b, s_len, B_WIDTH)

    swkv = sw_kv.reshape(b, s_len, 2, SW_KV_HEADS, SW_DIM)
    o_c = sliding_window_attention(sw_q.reshape(b, s_len, SW_Q_HEADS, SW_DIM), swkv[:, :, 0], swkv[:, :, 1],
                                   sinks, alibi_slopes(SW_Q_HEADS), positions).reshape(b, s_len, C_WIDTH)

    dq = df_q.reshape(b, s_len, DF_HEADS, 2, DF_DIM)
    dk = df_k.reshape(b, s_len, DF_HEADS, 2, DF_DIM)
    f32 = jnp.float32
    lam = (jnp.exp(jnp.sum(lq1.astype(f32) * lk1.astype(f32)))
           - jnp.exp(jnp.sum(lq2.astype(f32) * lk2.astype(f32))) + lam_init)
    o = diff_attention(dq[..., 0, :], dq[..., 1, :], dk[..., 0, :], dk[..., 1, :],
                       df_v.reshape(b, s_len, DF_HEADS, DF_VDIM), lam, alibi_slopes(DF_HEADS), positions)
    o_d = (rms_norm(o, subln) * (1.0 - lam_init)).reshape(b, s_len, D_WIDTH)

    gates = jax.nn.sigmoid(jnp.einsum('bsd,de->bse', x, w_gate) + b_gate).reshape(b, s_len, N_BRANCH, D_MODEL)
    merged = (gates[:, :, 0] * jnp.einsum('bsw,wd->bsd', o_a, w_br_a)
              + gates[:, :, 1] * jnp.einsum('bsw,wd->bsd', o_b, w_br_b)
              + gates[:, :, 2] * jnp.einsum('bsw,wd->bsd', o_c, w_br_c)
              + gates[:, :, 3] * jnp.einsum('bsw,wd->bsd', o_d, w_br_d))
    return jnp.einsum('bsd,de->bse', merged, w_out)

def grouped_moe(x, w_router, router_bias, w1, w3, w2):
    b, s_len, d = x.shape
    xt = x.reshape(b * s_len, d)
    t = xt.shape[0]
    scores = jax.nn.sigmoid(jnp.dot(xt.astype(jnp.float32), w_router.astype(jnp.float32)))
    biased = (scores + router_bias.astype(jnp.float32)).reshape(t, N_GROUPS, EXPERTS_PER_GROUP)
    group_score = lax.top_k(biased, GROUP_SCORE_TOP)[0].sum(-1)
    g_sel = jnp.argmax(group_score, axis=-1).astype(jnp.int32)
    in_group = jnp.take_along_axis(biased, g_sel[:, None, None], axis=1)[:, 0]
    local = lax.top_k(in_group, TOP_K)[1]
    e_idx = (g_sel[:, None] * EXPERTS_PER_GROUP + local).astype(jnp.int32)
    gate = jnp.take_along_axis(scores, e_idx, axis=1)
    gate = gate / gate.sum(-1, keepdims=True)

    tk = t * TOP_K
    flat_e = e_idx.reshape(-1)
    order = jnp.argsort(flat_e)
    sorted_e = flat_e[order]
    tok = (order // TOP_K).astype(jnp.int32)
    counts = jnp.bincount(flat_e, length=N_EXPERTS)
    padded = (counts + MOE_BLOCK - 1) // MOE_BLOCK * MOE_BLOCK
    pad_end = jnp.cumsum(padded)
    pad_start = pad_end - padded
    start = jnp.cumsum(counts) - counts
    dest = (pad_start[sorted_e] + jnp.arange(tk) - start[sorted_e]).astype(jnp.int32)
    n_blocks = -(-tk // MOE_BLOCK) + N_EXPERTS
    rows = n_blocks * MOE_BLOCK
    row_tok = jnp.full((rows,), t, jnp.int32).at[dest].set(tok)
    x_pad = jnp.concatenate([xt, jnp.zeros((1, d), xt.dtype)], axis=0)
    xs = x_pad[row_tok].reshape(n_blocks, MOE_BLOCK, d)
    block_e = jnp.minimum(jnp.searchsorted(pad_end, jnp.arange(n_blocks) * MOE_BLOCK, side='right'), N_EXPERTS - 1)

    def expert_block(args):
        xb, e = args
        hid = jax.nn.silu(xb @ w1[e]) * (xb @ w3[e])
        return hid @ w2[e]

    ys = lax.map(expert_block, (xs, block_e)).reshape(rows, d)
    gate_sorted = gate.reshape(-1)[order].astype(x.dtype)
    y = jnp.zeros((t, d), x.dtype).at[tok].add(ys[dest] * gate_sorted[:, None])
    return y.reshape(b, s_len, d)

def second_inputs(seed: int = 0) -> dict:
    key = jax.random.key(seed)
    ks = iter(jax.random.split(key, 40))

    def nrm(shape, scale):
        return jax.random.normal(next(ks), shape, jnp.float32) * scale

    def gain(shape):
        return 1.0 + 0.02 * jax.random.normal(next(ks), shape, jnp.float32)

    L = DEPTH_2
    return {
        'x': nrm((BATCH, SEQ, D_MODEL), 1.0),
        'positions': jnp.arange(SEQ, dtype=jnp.int32),
        'w_in': nrm((L, D_MODEL, IN_WIDTH_2), D_MODEL ** -0.5),
        'mla_q_norm': gain((L, MLA_Q_RANK)),
        'mla_kv_norm': gain((L, MLA_KV_RANK)),
        'w_uq': nrm((L, MLA_Q_RANK, MLA_HEADS * (MLA_NOPE + MLA_ROPE)), MLA_Q_RANK ** -0.5),
        'w_ukv': nrm((L, MLA_KV_RANK, MLA_HEADS * (MLA_NOPE + MLA_V)), MLA_KV_RANK ** -0.5),
        'sw_sinks': nrm((L, SW_Q_HEADS), 0.5),
        'df_lq1': nrm((L, DF_DIM), 0.1),
        'df_lk1': nrm((L, DF_DIM), 0.1),
        'df_lq2': nrm((L, DF_DIM), 0.1),
        'df_lk2': nrm((L, DF_DIM), 0.1),
        'df_subln': gain((L, DF_VDIM)),
        'w_gate': nrm((L, D_MODEL, N_BRANCH * D_MODEL), D_MODEL ** -0.5),
        'b_gate': nrm((L, N_BRANCH * D_MODEL), 0.01),
        'w_br_a': nrm((L, A_WIDTH, D_MODEL), DN_BETA * A_WIDTH ** -0.5),
        'w_br_b': nrm((L, B_WIDTH, D_MODEL), DN_BETA * B_WIDTH ** -0.5),
        'w_br_c': nrm((L, C_WIDTH, D_MODEL), DN_BETA * C_WIDTH ** -0.5),
        'w_br_d': nrm((L, D_WIDTH, D_MODEL), DN_BETA * D_WIDTH ** -0.5),
        'w_out': nrm((L, D_MODEL, D_MODEL), DN_BETA * D_MODEL ** -0.5),
        'ln1_g': gain((L, D_MODEL)),
        'ln1_b': nrm((L, D_MODEL), 0.01),
        'w_router': nrm((D_MODEL, N_EXPERTS), D_MODEL ** -0.5),
        'router_bias': nrm((N_EXPERTS,), 0.01),
        'moe_w1': nrm((L, N_EXPERTS, D_MODEL, D_EXPERT), D_MODEL ** -0.5),
        'moe_w3': nrm((L, N_EXPERTS, D_MODEL, D_EXPERT), DN_BETA * D_MODEL ** -0.5),
        'moe_w2': nrm((L, N_EXPERTS, D_EXPERT, D_MODEL), DN_BETA * D_EXPERT ** -0.5),
        'ln2_g': gain((L, D_MODEL)),
        'ln2_b': nrm((L, D_MODEL), 0.01),
    }

def second_block(x, positions, w_in, mla_q_norm, mla_kv_norm, w_uq, w_ukv, sw_sinks,
              df_lq1, df_lk1, df_lq2, df_lk2, df_subln, w_gate, b_gate,
              w_br_a, w_br_b, w_br_c, w_br_d, w_out, ln1_g, ln1_b,
              w_router, router_bias, moe_w1, moe_w3, moe_w2, ln2_g, ln2_b):
    for l in range(DEPTH_2):
        lam_init = 0.8 - 0.6 * math.exp(-0.3 * l)
        mix = token_mixers(x, positions, lam_init, w_in[l], mla_q_norm[l], mla_kv_norm[l], w_uq[l], w_ukv[l],
                           sw_sinks[l], df_lq1[l], df_lk1[l], df_lq2[l], df_lk2[l], df_subln[l],
                           w_gate[l], b_gate[l], w_br_a[l], w_br_b[l], w_br_c[l], w_br_d[l], w_out[l])
        x = layer_norm(DN_ALPHA * x + mix, ln1_g[l], ln1_b[l])
        ffn = grouped_moe(x, w_router, router_bias, moe_w1[l], moe_w3[l], moe_w2[l])
        x = layer_norm(DN_ALPHA * x + ffn, ln2_g[l], ln2_b[l])
    return x


def setup_inputs(seed=0):
    out = dict(first_inputs(seed))
    for name, value in second_inputs(seed + 1).items():
        if name != "x":
            out[name + "_2"] = value
    return out


def reference(
    x, c, ctx, c_ctx, w_ada, b_ada, norm_pre, norm_post, ffn1_w_in, ffn1_w_out, ffn2_w_in,
    ffn2_w_out, mix_w_in, attn_sink, hgrn_lb_fwd, hgrn_lb_bwd, hgrn_norm, w_o_attn, w_o_hgrn,
    w_out, positions_2, w_in_2, mla_q_norm_2, mla_kv_norm_2, w_uq_2, w_ukv_2, sw_sinks_2,
    df_lq1_2, df_lk1_2, df_lq2_2, df_lk2_2, df_subln_2, w_gate_2, b_gate_2, w_br_a_2, w_br_b_2,
    w_br_c_2, w_br_d_2, w_out_2, ln1_g_2, ln1_b_2, w_router_2, router_bias_2, moe_w1_2,
    moe_w3_2, moe_w2_2, ln2_g_2, ln2_b_2,
):
    x = first_block(
        x, c, ctx, c_ctx, w_ada, b_ada, norm_pre, norm_post, ffn1_w_in, ffn1_w_out, ffn2_w_in,
        ffn2_w_out, mix_w_in, attn_sink, hgrn_lb_fwd, hgrn_lb_bwd, hgrn_norm, w_o_attn,
        w_o_hgrn, w_out,
    )
    return second_block(
        x, positions_2, w_in_2, mla_q_norm_2, mla_kv_norm_2, w_uq_2, w_ukv_2, sw_sinks_2,
        df_lq1_2, df_lk1_2, df_lq2_2, df_lk2_2, df_subln_2, w_gate_2, b_gate_2, w_br_a_2,
        w_br_b_2, w_br_c_2, w_br_d_2, w_out_2, ln1_g_2, ln1_b_2, w_router_2, router_bias_2,
        moe_w1_2, moe_w3_2, moe_w2_2, ln2_g_2, ln2_b_2,
    )


_drawn_inputs = setup_inputs


def setup_inputs(seed=0):
    import zlib

    import numpy as np

    out = dict(_drawn_inputs(seed))
    spreads = {}
    factors = {'norm_pre': 3.391,
     'norm_post': 3.667,
     'attn_sink': 8.0,
     'hgrn_lb_fwd': 4.74,
     'hgrn_lb_bwd': 3.657,
     'hgrn_norm': 4.477,
     'mla_q_norm_2': 8.0,
     'mla_kv_norm_2': 8.0,
     'sw_sinks_2': 7.076,
     'df_lq1_2': 5.989,
     'df_lk1_2': 4.456,
     'df_lq2_2': 8.0,
     'df_lk2_2': 8.0,
     'df_subln_2': 8.0,
     'b_gate_2': 8.0,
     'ln1_b_2': 2.895,
     'ln2_b_2': 3.519}
    for name, (base, spread) in spreads.items():
        noise = np.random.default_rng([zlib.crc32(name.encode()), seed]).standard_normal(out[name].shape)
        drawn = base * np.exp(spread * noise) if base else spread * noise
        out[name] = __import__('jax').numpy.asarray(drawn.astype(out[name].dtype))
    for name, factor in factors.items():
        out[name] = (out[name] * factor).astype(out[name].dtype)
    return out
```

```python
from contextlib import ExitStack

import concourse.bass as bass
import numpy as np
from concourse import mybir

P = 128
D = 1024
KD = D // P
T = 256
D_FF = 2816
FT = D_FF // P
EPS = 1e-6
LN_EPS = 1e-5
BANK = 512

HEADS, HD = 8, 64
HG_HEADS = 4
WINDOW = 128
GRID_W = 64
IN1 = dict(aq=0, ak=512, hq=768, hff=1280, hfb=1792, hi=2304, hg=2816, ga=3328, gh=4352)
LEVELS = [64, 32, 16, 8, 4, 2, 1]
NEG = -1e30

LAYERS = 2
ALPHA = (2 * LAYERS) ** 0.25
EXPERTS, GROUPS, PER_GROUP, D_EXPERT = 32, 8, 4, 256
MLA_HEADS, MLA_DIM = 4, 96
IN2_WIDTH = 2720
IN2 = dict(c=0, sbqk=416, sbv=928, swq=1184, swk=1696, swv=1824, dfqk=1952, dfv=2464)
BRANCH_TILES = (2, 2, 4, 2)
C_Q, C_KV, C_ROPE = 256, 128, 32
TWO_PI_PARTS = (6.28125, 0.0019350051879882812, 3.019916050561733e-07)
ROUND = 1.5 * 2.0 ** 23

COLS = {}
_at = 0
for _name, _n in (("c", 8), ("c_ctx", 8), ("b_ada", 72), ("norm_pre", 24), ("lb_f0", 4), ("lb_f1", 4),
                  ("lb_b0", 4), ("lb_b1", 4), ("hgrn_norm", 4), ("halves", 2), ("quarters", 4),
                  ("rev8", 8), ("tri", 16), ("layers", 72)):
    COLS[_name] = (_at, _n)
    _at += _n
N_COLS = _at
PER_LAYER_COLS = 36


class Jobs:

    def __init__(self, used):
        self.used = list(used)

    def take(self, *banks):
        jobs = []
        for b in banks:
            jobs.append((b, self.used[b]))
            self.used[b] += 1
        return jobs


class Units:

    SLOTS = 4

    def __init__(self):
        self.dmas = []

    def add(self, n, dmas=1):
        first = len(self.dmas)
        self.dmas += [dmas] * n
        return first

    def loaded(self, u):
        return 16 * sum(self.dmas[v] for v in range(u % self.SLOTS, u + 1, self.SLOTS))


def shape_constants():
    f32 = np.float32
    i = np.arange(P)
    s, t = i[:, None], i[None, :]
    masks = []
    for m in LEVELS:
        masks.append((s // (2 * m) == t // (2 * m)) & (s % (2 * m) < m) & (t % (2 * m) >= m))
    masks += [x.T for x in masks]
    masks.append(s == t)
    pair_masks = np.stack(masks, 1).astype(f32)
    q = np.arange(T)
    gap = q[:, None] - q[None, :]
    tok = lambda a: np.ascontiguousarray(a.reshape(2, P, -1).transpose(1, 0, 2).astype(f32))
    window = np.zeros((T, 2 * T), f32)
    window[:, :T] = np.where(np.abs(gap) <= WINDOW, 0.0, NEG)
    causal = tok(np.where(gap >= 0, 0.0, NEG))
    slide = tok(np.where((gap >= 0) & (gap < P), 0.0, NEG))
    freqs = f32(10000.0) ** (-np.arange(16, dtype=f32) / f32(16))
    row, col = q // GRID_W, q % GRID_W
    ang = np.concatenate([row[:, None].astype(f32) * freqs, col[:, None].astype(f32) * freqs], 1)
    rope = tok(np.concatenate([np.cos(ang), np.sin(ang)], 1))
    reset = np.ones((P, 4 * P), f32)
    reset[:, ::P] = 0.0
    keys_first = np.stack([(q[:, None] < q[None, :])[k * P:(k + 1) * P] for k in range(2)], 1)
    halves = np.stack([i < 64, i >= 64], 1)
    quarters = np.stack([i // 32 == n for n in range(4)], 1)
    rev8 = np.tile(8.0 - np.arange(8), (P, 1))
    tri = np.tile(np.tril(np.ones((4, 4)), -1).reshape(1, 16), (P, 1))
    lam_init = np.array([0.8 - 0.6 * np.exp(-0.3 * l) for l in range(LAYERS)], f32)
    return dict(
        pair_masks=pair_masks, window=tok(window), causal=causal, slide=slide, rope=rope, reset=reset,
        ident=np.eye(P, dtype=f32), later=(s > t).astype(f32), sb_mask=keys_first.astype(f32),
        halves=halves.astype(f32), quarters=quarters.astype(f32),
        inv_freq=np.tile(freqs, (P, 1)), lam_init=np.tile(lam_init, (P, 1)),
        rev8=rev8.astype(f32), tri=tri.astype(f32),
    )


def build_program(nc, io, stop=None):
    fp32 = mybir.dt.float32
    u8 = mybir.dt.uint8
    i32 = mybir.dt.int32
    ALU = mybir.AluOpType
    ACT = mybir.ActivationFunctionType
    X_AXIS = mybir.AxisListType.X
    mm = nc.tensor.matmul
    tr = nc.tensor.transpose
    act = nc.scalar.activation
    tt = nc.vector.tensor_tensor
    ts = nc.vector.tensor_scalar
    stt = nc.vector.scalar_tensor_tensor
    copy = nc.vector.tensor_copy

    with ExitStack() as ctx:
        def sb(name, shape, dt=fp32):
            return ctx.enter_context(nc.sbuf_tensor(name, shape, dt))

        def sem(name):
            return ctx.enter_context(nc.semaphore(name))

        ring = sb("ring", [P, 4, 4096])
        X = sb("X", [P, 4, D])
        HT = sb("HT", [P, KD, 2 * T])
        G = sb("G", [P, 4, D])
        cols = sb("cols", [P, N_COLS])
        ident = sb("ident", [P, P])
        pair_mask = sb("pair_mask", [P, 2 * len(LEVELS) + 1, P], u8)
        masks = sb("masks", [P, 4, 2 * T])
        reset = masks[:, 0, :]
        window = masks[:, 1:3, :]
        causal = masks[:, 0, :].rearrange("p (t n) -> p t n", t=2)
        slide_gap = masks[:, 1, :].rearrange("p (t n) -> p t n", t=2)
        causal_gap = masks[:, 2, :].rearrange("p (t n) -> p t n", t=2)
        sb_mask = masks[:, 3, :].rearrange("p (t n) -> p t n", t=2)
        rope1 = sb("rope1", [P, 2, 2, 32])
        arena = sb("arena", [P, 20992])
        th = sb("th", [P, 2, BANK])
        tmp = sb("tmp", [P, 2, BANK])
        junk = sb("junk", [P, BANK])
        sc = sb("sc", [P, KD, 2])
        mod = sb("mod", [P, 9, KD, 2])
        gain = sb("gain", [P, 3, KD, 2])
        lbs = sb("lbs", [P, 2, 2, 4])
        lbt = sb("lbt", [P, 3, 8])
        ss = sb("ss", [P, 16, 8])
        rs = sb("rs", [P, 16, 8])
        neghalf = sb("neghalf", [P, 8])
        inv_width = sb("inv_width", [P, 8])
        neg_inv_d = sb("neg_inv_d", [P, 2])
        tot = sb("tot", [P, 2, 4, 4])
        dec = sb("dec", [P, 2, 4, 4])
        mx = sb("mx", [P, 16])
        negmx = sb("negmx", [P, 16])
        den = sb("den", [P, 16])
        sinkx = sb("sinkx", [P, 16])
        sink1 = sb("sink1", [P, HEADS])
        later = sb("later", [P, P])
        ones = sb("ones", [P, P])
        w_router = sb("w_router", [P, KD, EXPERTS])
        router_bias = sb("router_bias", [P, EXPERTS])
        rope2 = sb("rope2", [P, 2, 2, 16])
        inv_freq = sb("inv_freq", [P, 16])
        pos_i = sb("pos_i", [P, 2], i32)
        pos = sb("pos", [P, 2])
        lam_init = sb("lam_init", [P, LAYERS])
        lam_sum = sb("lam_sum", [P, 2, LAYERS])
        neg_lam = sb("neg_lam", [P, LAYERS])
        sub_gain = sb("sub_gain", [P, LAYERS])
        half_bias = sb("half_bias", [P, LAYERS, 32])
        sink2 = sb("sink2", [P, LAYERS, 8])
        mx2 = sb("mx2", [P, 2, 8])
        neg2 = sb("neg2", [P, 2, 8])
        den2 = sb("den2", [P, 2, 8])
        sinkx2 = sb("sinkx2", [P, 2, 8])
        row_sum = sb("row_sum", [P, 2, 4])
        row_rs = sb("row_rs", [P, 4, 4])

        def region(start, *dims):
            n = int(np.prod(dims))
            v = arena[:, start:start + n]
            if len(dims) == 1:
                return v
            names = "abcd"[:len(dims)]
            return v.rearrange(f"p ({' '.join(names)}) -> p {' '.join(names)}", **dict(zip(names, dims)))

        PS = [ctx.enter_context(nc.psum_tensor(f"bank{b}", [P, BANK], fp32)) for b in range(8)]

        bank_full = [sem(f"bank_full{b}") for b in range(8)]
        bank_free = [sem(f"bank_free{b}") for b in range(8)]
        slot_loaded = [sem(f"slot_loaded{s}") for s in range(4)]
        slot_free = [sem(f"slot_free{s}") for s in range(4)]
        cols_loaded = sem("cols_loaded")
        consts_loaded = sem("consts_loaded")
        c_tanh_ready = sem("c_tanh_ready")
        silu_c_ready = sem("silu_c_ready")
        sumsq_ready = sem("sumsq_ready")
        rstd_ready = sem("rstd_ready")
        xn_ready = sem("xn_ready")
        x_ready = sem("x_ready")
        th_ready = sem("th_ready")
        gain_ready = sem("gain_ready")
        f_ready = sem("f_ready")
        lf_ready = sem("lf_ready")
        cum_ready = sem("cum_ready")
        kexp_ready = sem("kexp_ready")
        kdec_ready = sem("kdec_ready")
        state_ready = sem("state_ready")
        qexp_ready = sem("qexp_ready")
        qdec_ready = sem("qdec_ready")
        gap_ready = sem("gap_ready")
        decay_ready = sem("decay_ready")
        qlev_ready = sem("qlev_ready")
        klev_ready = sem("klev_ready")
        negmax_ready = sem("negmax_ready")
        probs_ready = sem("probs_ready")
        pv_done = sem("pv_done")
        merged_ready = sem("merged_ready")
        out_stored = sem("out_stored")
        lb_max_ready = sem("lb_max_ready")
        lb_exp_ready = sem("lb_exp_ready")
        silu_ready = sem("silu_ready")
        gate_ready = sem("gate_ready")
        gate_tanh_ready = sem("gate_tanh_ready")
        lam_ready = sem("lam_ready")
        lam_exp_ready = sem("lam_exp_ready")
        consts2_loaded = sem("consts2_loaded")
        angle_ready = sem("angle_ready")
        rope2_ready = sem("rope2_ready")
        layer_loaded = sem("layer_loaded")
        c_squares_ready = sem("c_squares_ready")
        c_rstd_ready = sem("c_rstd_ready")
        df_squares_ready = sem("df_squares_ready")
        df_rstd_ready = sem("df_rstd_ready")
        neg2_ready = sem("neg2_ready")
        probs2_ready = sem("probs2_ready")
        mixed_ready = sem("mixed_ready")
        pv2_done = sem("pv2_done")
        df_scaled_ready = sem("df_scaled_ready")
        r_ready = sem("r_ready")
        sum_ready = sem("sum_ready")
        mean_ready = sem("mean_ready")
        square_ready = sem("square_ready")
        ln_rstd_ready = sem("ln_rstd_ready")
        merged2_ready = sem("merged2_ready")
        moe_th_ready = sem("moe_th_ready")
        router_exp_ready = sem("router_exp_ready")
        gates_ready = sem("gates_ready")
        sb_log_ready = sem("sb_log_ready")
        sb_beta_ready = sem("sb_beta_ready")
        sb_l_ready = sem("sb_l_ready")
        sb_a_ready = sem("sb_a_ready")
        sb_exp_ready = sem("sb_exp_ready")
        mtok_ready = sem("mtok_ready")
        o_ready = sem("o_ready")
        sbo_ready = sem("sbo_ready")
        gate_half_ready = sem("gate_half_ready")
        ln_done = sem("ln_done")
        layer_start = sem("layer_start")

        def acquire(eng, job):
            bank, use = job
            if not (isinstance(use, int) and use == 0):
                eng.wait_ge(bank_free[bank], use)
            return PS[bank]

        def filled(eng, job):
            bank, use = job
            eng.wait_ge(bank_full[bank], use + 1)
            return PS[bank]

        def emptied(eng, job):
            bank, use = job
            eng.wait_ge(bank_free[bank], use + 1)

        def full(job):
            return bank_full[job[0]], 1

        def free(job):
            return bank_free[job[0]], 1

        def cat(job, a, b):
            return PS[job[0]][:, :].rearrange("p (a b) -> p a b", a=a)

        units = Units()
        U_ADA = units.add(18)
        U_FF1A = units.add(11, 2)
        U_FF1B = units.add(6)
        MIX = ["hq", "hff", "hi", "ak", "aq", "hg", "ga", "ga2", "hfb", "gh", "gh2"]
        U_MIX = units.add(11)
        U_WOA = units.add(1)
        U_WOH = units.add(1)
        U_WOUT = units.add(2)
        U_FF2A = units.add(11, 2)
        U_FF2B = units.add(6)
        U_LAYERS = len(units.dmas)

        jobs = Jobs([0] * 8)
        J_ADA = []
        for u in range(18):
            j = u // 2
            J_ADA.append(jobs.take(*([u % 4] if j != 2 else [u % 4, (u + 2) % 4])))

        def norm_jobs():
            return [jobs.take(k % 8)[0] for k in range(KD)]

        class Loop:

            def __init__(self, n, banks):
                self.first = [jobs.used[b] for b in banks]
                self.banks = banks
                for _ in range(n):
                    jobs.take(*banks)

            def __call__(self, i, k):
                return self.banks[k], self.first[k] + i

        J_N1 = norm_jobs()
        J_FF1A = Loop(11, [0, 1, 2, 3])
        J_FF1B = jobs.take(4, 5, 6, 7, 0, 1, 2, 3)
        J_N2 = norm_jobs()
        J_HQ = jobs.take(0, 1)
        J_HF = [jobs.take(2, 3, 4, 5)]
        J_HI = jobs.take(6, 7, 0, 1)
        J_AK = jobs.take(2, 3)
        J_AQ = jobs.take(4, 5)
        J_HG = jobs.take(6, 7)
        J_KT, J_KV, J_LEV, J_DIAG, J_GATE = [], [], [], [], []
        for d in range(2):
            if d == 1:
                J_HF.append(jobs.take(2, 3, 4, 5))
            J_KT.append([])
            J_KV.append([])
            for i in range(3):
                J_KT[d].append(jobs.take(2 * (i % 2))[0])
                J_KV[d].append(jobs.take(2 * (i % 2) + 1)[0])
            J_LEV.append([])
            for li in range(len(LEVELS)):
                J_LEV[d].append(jobs.take(*((0, 1) if li % 2 == 0 else (2, 3))))
                if li < 4:
                    J_GATE.append(jobs.take(4 + li)[0])
            J_DIAG.append(jobs.take(4, 5))
        J_O = jobs.take(0, 1)
        J_ORT = jobs.take(2, 3)
        J_QT = jobs.take(4, 5)
        J_KZ = jobs.take(6, 7)
        J_S, J_PT, J_PV, J_OT = [], [], [], []
        for b in range(2):
            J_S.append([jobs.take(h % 4)[0] for h in range(HEADS)])
            J_PV.append(jobs.take(6)[0])
            J_PT.append([jobs.take(4 + h % 2)[0] for h in range(HEADS)])
            J_OT.append(jobs.take(7)[0])
        J_WOA = jobs.take(0, 1, 2, 3)
        J_WOH = jobs.take(4, 5, 6, 7)
        J_WOUT = jobs.take(0, 1, 2, 3)
        J_N3 = norm_jobs()
        J_FF2A = Loop(11, [0, 1, 2, 3])
        J_FF2B = jobs.take(4, 5, 6, 7)

        U_IN = units.add(4)
        units.dmas[U_IN + 2] = 2
        U_IN4 = units.add(1, 5)
        U_IN5 = units.add(1)
        U_GATES = units.add(8)
        U_BR = units.add(4)
        U_OUT2 = units.add(2)
        U_MOE = len(units.dmas)
        for _ in range(EXPERTS):
            units.add(1, 2)
            units.add(1)
        LAYER_TURNS = (len(units.dmas) - U_LAYERS) // 4
        assert (len(units.dmas) - U_LAYERS) % 4 == 0
        LAYER_DMAS = [16 * sum(units.dmas[u] for u in range(U_LAYERS, len(units.dmas)) if u % 4 == s) for s in range(4)]

        before_layers = list(jobs.used)
        J_XT = jobs.take(0, 1, 2, 3)
        J_C = jobs.take(4, 5)
        J_CT = jobs.take(6, 7)
        J_SBQK = jobs.take(0, 1)
        J_MQ = jobs.take(2, 3)
        J_MKV = jobs.take(4, 5)
        J_VTOK = jobs.take(6, 7)
        J_SWQ = jobs.take(0, 1)
        J_SWK = jobs.take(2)
        J_DFV = jobs.take(3)
        J_DFQK = jobs.take(4, 5)
        J_MQT = jobs.take(6, 7)
        J_MKT = jobs.take(0, 1)
        J_SBZ = jobs.take(2, 3, 4, 5)
        J_G2 = jobs.take(6, 7, 6, 7)
        J_SBS = jobs.take(2, 3, 4, 5)
        J_G2 += jobs.take(6, 7)
        J_SM, J_PB, J_OV, J_OX = [], [], [], []
        J_SBO = jobs.take(6)
        J_SBX = jobs.take(6)
        for n, (kind, _) in enumerate((("mla", 0), ("mla", 1), ("sw", 0), ("sw", 1), ("df", 0), ("df", 1))):
            J_SM.append(jobs.take(*range({"mla": 2}.get(kind, 4))))
            J_G2 += jobs.take(7, 7)[:2 if n < 5 else 0] if n < 5 else []
            J_PB.append(jobs.take(*[4 + i % 2 for i in range(4 if kind == "sw" else 2)]))
            J_OV.append(jobs.take(6)[0])
            J_OX.append(jobs.take(6)[0])
        J_BR = [jobs.take(*((0, 1, 2, 3) if j % 2 == 0 else (4, 5, 6, 7))) for j in range(4)]
        J_OUT2 = jobs.take(0, 1, 2, 3)
        J_XT2 = jobs.take(4, 5, 6, 7)
        J_ROUTE = jobs.take(3)
        J_Y = jobs.take(4, 5, 6, 7)
        J_EXP = Loop(EXPERTS, [0, 1, 2])
        LAYER_USES = [n - m for n, m in zip(jobs.used, before_layers)]

        def at(L, job):
            bank, use = job
            return bank, L * LAYER_USES[bank] + use

        def repeat(eng, n, body):
            turns = n // 4
            with eng.Fori(0, turns) as g:
                for r in range(4):
                    body(g * 4 + r, r, g)
            for r in range(n - 4 * turns):
                body(4 * turns + r, 4 * turns + r, 0)

        def loaded(eng, u, g=0):
            value = units.loaded(u)
            if not isinstance(g, int):
                value = g * (16 * units.dmas[u]) + value
            eng.wait_ge(slot_loaded[u % 4], value)
            return ring[:, u % 4, :]

        def released(eng, u, g=0):
            value = u // 4 + g
            if not (isinstance(value, int) and value == 0):
                eng.wait_ge(slot_free[u % 4], value)
            return ring[:, u % 4, :]

        def release(u):
            nc.tensor.drain().then_inc(slot_free[u % 4], 1)

        XN = region(0, 4, D)
        NORM_POST = region(4096, 3, D)
        MASK_F = region(8192, 15, P)
        HID = region(0, FT, 2 * T)
        HQ = region(0, 4, T)
        BB = region(1024, 4, 4 * P)
        KK = region(3072, 4, 4 * P)
        VHG = region(5120, 4, 4 * P)
        STATE = region(7168, 4, 4, P)
        KDEC = region(9216, 4, P)
        KDT = region(9728, 4, P)
        EB = region(10240, 4, T)
        QLEV = region(11264, 4, T)
        KLEV = region(12288, 4, T)
        SHIFT = region(10240, 4, 4, P)
        QDEC = region(13312, 8, T)
        SCORE = region(15360, 2, 4, P)
        HGT = region(16384, 4, T)
        ORT = region(17408, 4, T)
        VTOK = region(18432, 4, P)
        QTOK = region(18944, 2, 8, HD)
        KTOK = region(19968, 4, 4, HD)
        ROPE_T = region(10240, 4, 256)
        ONT = region(10240, 2, 4 * P)
        SGA = X[:, 2:4, :].rearrange("p t (a n) -> p (t a) n", n=T)
        SGH = G[:, 0:2, :].rearrange("p t (a n) -> p (t a) n", n=T)
        PROB = region(0, HEADS, 4 * P)
        PT = region(4096, 2, 4 * P)
        OTOK = region(5120, 2, 4 * P)
        OT = region(6144, 4, T)
        QT = region(7168, 4, T)
        KZ = region(8192, 4, 4 * P)
        MERGED = region(10240, KD, T)
        YT2 = region(13312, 2, D)

        def col(name, i=0, n=1):
            first = COLS[name][0] + i
            return cols[:, first:first + n]

        N_CONSTS = 23
        TILES = ((2, 3, 0), (3, 2, 1))

        block = ctx.enter_context(nc.Block())

        SG = region(0, 4 * KD, T)
        CTOK = region(0, 2, C_Q + C_KV + C_ROPE)
        CT = region(1024, 3, T)
        W_UQ = region(2048, 2, MLA_HEADS * MLA_DIM)
        W_UKV = region(3072, MLA_HEADS * P)
        MQTOK = region(4096, 2, MLA_HEADS, MLA_DIM)
        MKTOK = region(5120, 2, MLA_HEADS, MLA_DIM)
        ROT = region(6144, 4, P)
        OTS = [region(8192, 2, T), region(8704, 2, T), region(9216, 4, T), region(10240, 2, T)]
        MQT = region(10752, MLA_HEADS, T)
        MKT = region(11776, MLA_HEADS, T)
        MV = region(12800, 2, MLA_HEADS, HD)
        SBV = region(13312, 2, T)
        SWV = region(13824, 2, P)
        DFV = region(14080, 2, T)
        SBQT = region(14592, 2, T)
        SBKZ = region(15104, 4, T)
        SWQT = region(16128, 4, T)
        SWKZ = region(17152, 4, T)
        DFQT = region(18176, 2, T)
        DFKZ = region(18688, 8, T)
        LCOLS = region(20736, PER_LAYER_COLS)
        HBIAS = region(20800, 32)
        SINK2 = region(20864, 8)
        SUBG = region(20880, 1)
        NEG_LAM = region(20884, 1)
        POS_ROW_I = region(0, T).bitcast(i32)
        POS_ROW = region(512, T)
        POS_ROW_GAP = region(1024, 2, T)
        LAMS = region(2048, 4, LAYERS, 32)
        angle = region(2560, 2, 2, 16)
        turns = region(2688, 2, 2, 16)
        PB = [X[:, 2:4, :].rearrange("p t (a n) -> p (t a) n", n=T), HT[:, :, T:2 * T]]
        SB_E, SB_L = PB
        MERGED2 = region(10752, KD, T)
        SQ = PB[0]
        HIDG = region(0, 2, T)
        HIDT = region(512, 2, T)
        ROUTE = region(1024, 64)
        BIASED = region(1152, 16, 4)
        PAIR = region(1280, 16, 8)
        GROUP = region(1408, 16)
        GMAX = region(1440, 8)
        PICK = region(1472, 16)
        CMP = region(1536, 16, 4, 4)
        CMP2 = region(1792, 16, 4, 4)
        RANK = region(2048, 16, 4)
        GW = region(2176, 2, EXPERTS)

        SOFT = [("mla", 0), ("mla", 1), ("sw", 0), ("sw", 1), ("df", 0), ("df", 1)]
        MAPS = dict(mla=4, sw=8, df=8)
        OUT_HEADS = dict(mla=4, sw=8, df=4)
        SCALE = dict(mla=MLA_DIM ** -0.5, sw=HD ** -0.5, df=32.0 ** -0.5)
        BRANCH = dict(mla=0, sb=1, sw=2, df=3)

        def probs_before(n):
            return sum(OUT_HEADS[kind] // 2 for kind, _ in SOFT[:n])

        def maps_before(n):
            return sum(MAPS[kind] for kind, _ in SOFT[:n])

        N_MAPS, N_PAIRS = maps_before(6), probs_before(6)

        @block.sync
        def _(sp):
            def columns(w, first, n):
                return w[:, first:first + n].rearrange("(k p) n -> p k n", p=P)

            def load(u, dst, src, g=0):
                sp.dma_start(dst, src).then_inc(slot_loaded[u % 4], 16)

            def slot(v, k, n):
                return v[:, 0:k * n].rearrange("p (k n) -> p k n", k=k)

            for u in range(18):
                v = released(sp, U_ADA + u)
                load(U_ADA + u, slot(v, KD, BANK), columns(io["w_ada"], u * BANK, BANK))

            def ffn_in(first, w):
                def body(i, r, g):
                    v = released(sp, first + r, g).rearrange("p (a k n) -> p a k n", a=2, k=KD)
                    for part in range(2):
                        src = w[:, bass.ds(i * 256 + part * D_FF, 256)]
                        load(first + r, v[:, part, :, :], src.rearrange("(k p) n -> p k n", p=P))
                repeat(sp, 11, body)

            def ffn_out(first, w):
                for half in range(2):
                    for part in range(3):
                        f0, f1 = part * 8, min(part * 8 + 8, FT)
                        u = first + half * 3 + part
                        v = released(sp, u)
                        load(u, slot(v, f1 - f0, BANK),
                             w[f0 * P:f1 * P, half * BANK:half * BANK + BANK].rearrange("(k p) n -> p k n", p=P))

            ffn_in(U_FF1A, io["ffn1_w_in"])
            ffn_out(U_FF1B, io["ffn1_w_out"])
            for n, name in enumerate(MIX):
                first = IN1[name[:2] if name.endswith("2") else name] + (BANK if name.endswith("2") else 0)
                width = 256 if name == "ak" else BANK
                v = released(sp, U_MIX + n)
                load(U_MIX + n, slot(v, KD, width), columns(io["mix_w_in"], first, width))
            for u, w in ((U_WOA, io["w_o_attn"]), (U_WOH, io["w_o_hgrn"])):
                v = released(sp, u)
                load(u, slot(v, 4, D), w.rearrange("(k p) n -> p k n", p=P))
            for half in range(2):
                v = released(sp, U_WOUT + half)
                load(U_WOUT + half, slot(v, KD, BANK), columns(io["w_out"], half * BANK, BANK))
            ffn_in(U_FF2A, io["ffn2_w_in"])
            ffn_out(U_FF2B, io["ffn2_w_out"])
            with sp.Fori(0, LAYERS) as L:
                def free_slot(u, g=0):
                    sp.wait_ge(slot_free[u % 4], L * LAYER_TURNS + g + u // 4)
                    return ring[:, u % 4, :]

                def rows(name, n):
                    return io["l_" + name][bass.ds(L * n, n), :]

                def cut(name, n, first, width):
                    return io["l_" + name][bass.ds(L * n, n), first:first + width].rearrange("(k p) n -> p k n", p=P)

                for i, (name, width) in enumerate((("c", 416), ("sbqk", BANK), ("sbv", 384), ("swq", BANK))):
                    v = slot(free_slot(U_IN + i), KD, width)
                    if name == "sbv":
                        load(U_IN + i, v[:, :, 0:256], cut("w_in", D, IN2["sbv"], 256))
                        load(U_IN + i, v[:, :, 256:384], cut("w_in", D, IN2["swv"], P))
                    else:
                        load(U_IN + i, v, cut("w_in", D, IN2[name], width))
                v = slot(free_slot(U_IN4), KD, BANK)
                for i in range(4):
                    load(U_IN4, v[:, :, i * HD:i * HD + HD], cut("w_in", D, IN2["swk"] + i // 2 * HD, HD))
                load(U_IN4, v[:, :, 256:BANK], cut("w_in", D, IN2["dfv"], 256))
                load(U_IN5, slot(free_slot(U_IN5), KD, BANK), cut("w_in", D, IN2["dfqk"], BANK))
                for i in range(8):
                    load(U_GATES + i, slot(free_slot(U_GATES + i), KD, BANK), cut("w_gate", D, i * BANK, BANK))
                for j, name in enumerate(("w_br_a", "w_br_b", "w_br_c", "w_br_d")):
                    n = BRANCH_TILES[j]
                    load(U_BR + j, slot(free_slot(U_BR + j), n, D), cut(name, n * P, 0, D))
                for half in range(2):
                    load(U_OUT2 + half, slot(free_slot(U_OUT2 + half), KD, BANK), cut("w_out", D, half * BANK, BANK))
                with sp.Fori(0, EXPERTS // 2) as g:
                    for r in range(2):
                        u = U_MOE + 2 * r
                        v = slot(free_slot(u, g), KD, BANK)
                        for i, name in enumerate(("moe_w1", "moe_w3")):
                            src = io["l_" + name][bass.ds(L * (EXPERTS * D) + g * (2 * D) + r * D, D), :]
                            load(u, v[:, :, i * 256:i * 256 + 256], src.rearrange("(k p) n -> p k n", p=P))
                        v = slot(free_slot(u + 1, g), 2, D)
                        src = io["l_moe_w2"][bass.ds(L * (EXPERTS * D_EXPERT) + g * (2 * D_EXPERT) + r * D_EXPERT, D_EXPERT), :]
                        load(u + 1, v, src.rearrange("(k p) n -> p k n", p=P))
            sp.wait_ge(ln_done, 2 * LAYERS)
            sp.dma_start(io["out"].rearrange("(t p) n -> p t n", p=P), X[:, 0:2, :]).then_inc(out_stored, 16)
            sp.wait_ge(out_stored, 16)

        @block.scalar
        def _(se):
            def const(dst, src):
                se.dma_start(dst, src).then_inc(consts_loaded, 16)

            se.dma_start(cols[:, :], io["cols"]).then_inc(cols_loaded, 16)
            const(ident[:, :], io["ident"])
            const(X[:, 0:2, :], io["x"].rearrange("(t p) n -> p t n", p=P))
            const(X[:, 2:4, :], io["ctx"].rearrange("(t p) n -> p t n", p=P))
            const(MASK_F, io["pair_masks"])
            const(reset[:, :], io["reset"])
            const(window[:, :, :], io["window"])
            const(rope1[:, :, :, :], io["rope"].rearrange("p t (a n) -> p t a n", a=2))
            for g, j in enumerate((2, 2, 5, 8)):
                const(G[:, g, :], io["b_ada"][j * D:(j + 1) * D].partition_broadcast(P))
            for n in range(3):
                const(NORM_POST[:, n, :], io["norm_post"][n, :].partition_broadcast(P))
            const(sink1[:, :], io["attn_sink"].partition_broadcast(P))
            const(later[:, :], io["later"])
            const(w_router[:, :, :], io["w_router"].rearrange("(k p) n -> p k n", p=P))
            const(router_bias[:, :], io["router_bias"].partition_broadcast(P))
            const(inv_freq[:, :], io["inv_freq"])
            const(lam_init[:, :], io["lam_init"])
            for l in range(LAYERS):
                const(sink2[:, l, :], io["sw_sinks"][l, :].partition_broadcast(P))
            const(pos_i[:, :], io["pos_cols"])
            se.wait_ge(cols_loaded, 16)
            act(sc[:, :, :], cols[:, 0:16].rearrange("p (w k) -> p k w", w=2), ACT.Tanh, scale=0.5).then_inc(c_tanh_ready, 1)
            se.wait_ge(lb_max_ready, 1)
            act(lbt[:, 0:2, :], lbt[:, 0:2, :], ACT.Exp).then_inc(lb_exp_ready, 1)
            se.wait_ge(consts_loaded, 16 * N_CONSTS)

            def sum_squares(ev, tiles, src, dst):
                for t in range(tiles):
                    last = act(dst(t), src(t), ACT.Square, accum_out=ss[:, ev, t:t + 1])
                last.then_inc(sumsq_ready, 1)

            def transposed(n, tiles, J):
                for k in range(1, KD, 2):
                    ps = filled(se, J[k])
                    for w in range(tiles // 2):
                        last = act(HT[:, k, w * T:(w + 1) * T], ps[:, w * T:(w + 1) * T], ACT.Identity,
                                   scale=gain[:, n, k, w:w + 1], bias=mod[:, 3 * n, k, w:w + 1])
                    last.then_inc(*free(J[k]))

            def ffn_in(J, width):
                def body(i, r, g):
                    for j in range(2):
                        ps = filled(se, J(i, 2 * j))
                        act(th[:, j, 0:width], ps[:, 0:width], ACT.Tanh, scale=0.5).then_inc(th_ready, 1)
                repeat(se, 11, body)

            def post_squares(ev, tiles, J):
                for half in range(2):
                    for t in range(tiles):
                        ps = filled(se, J[half * tiles + t])
                        if half or t:
                            se.drain()
                        last = act(junk[:, :], ps[:, :], ACT.Square, accum_out=ss[:, ev, half * tiles + t:half * tiles + t + 1])
                last.then_inc(sumsq_ready, 1)

            sum_squares(0, 4, lambda t: X[:, t, :], lambda t: XN[:, t, :])
            se.wait_ge(gain_ready, 1)
            transposed(0, 4, J_N1)
            ffn_in(J_FF1A, 2 * T)
            post_squares(1, 4, J_FF1B)

            se.wait_ge(x_ready, 1)
            sum_squares(2, 4, lambda t: X[:, t, :], lambda t: XN[:, t, :])
            transposed(1, 4, J_N2)
            for i in range(2):
                ps = filled(se, J_HQ[i])
                act(th[:, i, :], ps[:, :], ACT.Tanh, scale=0.5).then_inc(gate_tanh_ready, 1)

            def forget_exp(d):
                if d:
                    filled(se, J_DIAG[0][1])
                for h in range(HG_HEADS):
                    ps = filled(se, J_HF[d][h])
                    act(KK[:, h, :], ps[:, :], ACT.Exp, scale=-1.0).then_inc(*free(J_HF[d][h]))

            def recurrence(d):
                se.wait_ge(f_ready, d + 1)
                act(BB, KK, ACT.Ln).then_inc(lf_ready, 1)
                se.wait_ge(cum_ready, d + 1)
                act(dec[:, d, :, :], tot[:, d, :, :], ACT.Exp)
                for i, tile in enumerate(TILES[d]):
                    if i:
                        filled(se, J_KT[d][i - 1])
                    cut = slice(tile * P, tile * P + P)
                    if d == 0:
                        for h in range(HG_HEADS):
                            last = act(KDEC[:, h, :], BB[:, h, cut], ACT.Exp, scale=-1.0,
                                       bias=tot[:, d, h, tile:tile + 1])
                    else:
                        last = act(KDEC, BB[:, :, cut], ACT.Exp)
                    last.then_inc(kexp_ready, 1)
                    ps = filled(se, J_KT[d][i])
                    if i:
                        filled(se, J_KV[d][i - 1])
                    act(KDT, cat(J_KT[d][i], 4, P), ACT.Copy).then_inc(*free(J_KT[d][i]))
                if d == 0:
                    last = act(EB, BB[:, :, 0:T], ACT.Exp)
                else:
                    for h in range(HG_HEADS):
                        for tile in range(2):
                            cut = slice(tile * P, tile * P + P)
                            last = act(EB[:, h, cut], BB[:, h, cut], ACT.Exp, scale=-1.0,
                                       bias=tot[:, d, h, tile:tile + 1])
                last.then_inc(qexp_ready, 1)
                for li in range(len(LEVELS)):
                    n = d * len(LEVELS) + li
                    se.wait_ge(gap_ready, n + 1)
                    act(EB, EB, ACT.Abs)
                    se.drain()
                    act(EB, EB, ACT.Exp, scale=-1.0).then_inc(decay_ready, 1)
                    if li < 4:
                        gate(d * 4 + li)

            def gate(i):
                sg, job = (SGA, SGH)[i // 4], J_GATE[i]
                filled(se, job)
                act(sg[:, 2 * (i % 4):2 * (i % 4) + 2, :], cat(job, 2, T), ACT.Tanh, scale=0.5).then_inc(*free(job))

            forget_exp(0)
            for t in range(4):
                ps = filled(se, J_HI[t])
                act(VHG[:, t, :], ps[:, :], ACT.Copy).then_inc(*free(J_HI[t]))
            se.wait_ge(silu_ready, 1)
            for i in range(2):
                ps = filled(se, J_HG[i])
                act(th[:, i, :], ps[:, :], ACT.Tanh, scale=0.5).then_inc(gate_tanh_ready, 1)
            recurrence(0)
            forget_exp(1)
            recurrence(1)
            for t in range(2):
                ps = filled(se, J_O[t])
                if t:
                    se.drain()
                last = act(junk[:, :], ps[:, :], ACT.Square, accum_out=ss[:, 3, t:t + 1])
            last.then_inc(sumsq_ready, 1)

            emptied(se, J_ORT[1])
            for i in range(2):
                filled(se, J_QT[i])
                act(QT[:, 2 * i:2 * i + 2, :], cat(J_QT[i], 2, T), ACT.Copy).then_inc(*free(J_QT[i]))
            for b in range(2):
                se.wait_ge(negmax_ready, b + 1)
                act(sinkx[:, b * 8:b * 8 + 8], sinkx[:, b * 8:b * 8 + 8], ACT.Exp)
                for h in range(HEADS):
                    act(PROB[:, h, :], PROB[:, h, :], ACT.Exp, bias=negmx[:, b * 8 + h:b * 8 + h + 1],
                        scale=HD ** -0.5, accum_out=den[:, b * 8 + h:b * 8 + h + 1]).then_inc(probs_ready, 1)
                for h in range(0, HEADS, 2):
                    ps = filled(se, J_PT[b][h])
                    if h >= 2:
                        se.wait_ge(pv_done, b * 7 + h - 1)
                    elif b:
                        filled(se, J_PV[b - 1])
                    act(PT[:, 0, :], ps[:, :], ACT.Copy).then_inc(*free(J_PT[b][h]))
                filled(se, J_OT[b])
                act(OT[:, :, b * P:b * P + P], cat(J_OT[b], 4, P), ACT.Copy).then_inc(*free(J_OT[b]))
            post_squares(4, 2, J_WOUT)

            se.wait_ge(x_ready, 2)
            sum_squares(5, 2, lambda t: X[:, t, :], lambda t: XN[:, t, :])
            transposed(2, 2, J_N3)
            ffn_in(J_FF2A, T)
            post_squares(6, 2, J_FF2B)
            se.wait_ge(x_ready, 3)

            def const2(dst, src):
                se.dma_start(dst, src).then_inc(consts2_loaded, 16)

            const2(causal, io["causal"])
            const2(slide_gap, io["slide"])
            const2(sb_mask, io["sb_mask"])
            for i, n in enumerate(("df_lq1", "df_lk1", "df_lq2", "df_lk2")):
                const2(LAMS[:, i, :, :].rearrange("p l n -> p (l n)"), io[n].rearrange("l n -> (l n)").partition_broadcast(P))
            const2(POS_ROW_I, io["pos_row"].partition_broadcast(P))
            se.wait_ge(lam_ready, 1)
            act(lam_sum[:, :, :], lam_sum[:, :, :], ACT.Exp).then_inc(lam_exp_ready, 1)
            se.wait_ge(angle_ready, 1)
            act(rope2[:, :, :, :], angle[:, :, :, :], ACT.Sin).then_inc(rope2_ready, 1)

            with se.Fori(0, LAYERS) as L:
                se.wait_ge(layer_start, L + 1)
                se.dma_start(W_UQ, io["l_w_uq"][bass.ds(L * C_Q, C_Q), :].rearrange("(k p) n -> p k n", p=P)).then_inc(layer_loaded, 16)
                se.dma_start(W_UKV, io["l_w_ukv"][bass.ds(L * C_KV, C_KV), :]).then_inc(layer_loaded, 16)
                for i, n in enumerate(("ln1_g", "ln1_b", "ln2_g", "ln2_b")):
                    se.dma_start(G[:, i, :], io[n][bass.ds(L, 1), :].partition_broadcast(P)).then_inc(layer_loaded, 16)

                def evac(dst, job, src=None, func=ACT.Copy, **kw):
                    filled(se, at(L, job))
                    act(dst, src if src is not None else PS[job[0]][:, :], func, **kw).then_inc(*free(job))

                def to_features(J):
                    for i in range(4):
                        evac(HT[:, 2 * i:2 * i + 2, 0:T], J[i], cat(J[i], 2, T))

                to_features(J_XT)
                for t in range(2):
                    ps = filled(se, at(L, J_C[t]))
                    act(junk[:, 0:C_Q], ps[:, 0:C_Q], ACT.Square, accum_out=ss[:, 7, t:t + 1])
                    last = act(junk[:, C_Q:C_Q + C_KV], ps[:, C_Q:C_Q + C_KV], ACT.Square, accum_out=ss[:, 7, 2 + t:3 + t])
                    se.drain()
                se.drain().then_inc(c_squares_ready, 1)
                evac(SBQT, J_SBQK[0], cat(J_SBQK[0], 2, T))
                for t in range(2):
                    filled(se, at(L, J_VTOK[t]))
                    ps = PS[J_VTOK[t][0]]
                    act(SBV[:, t, :], ps[:, 0:256], ACT.Copy)
                    act(SWV[:, t, :], ps[:, 256:384], ACT.Copy).then_inc(*free(J_VTOK[t]))
                for i in range(2):
                    evac(SWQT[:, 2 * i:2 * i + 2, :], J_SWQ[i], cat(J_SWQ[i], 2, T))
                evac(DFV, J_DFV[0], cat(J_DFV[0], 2, T))
                evac(DFQT, J_DFQK[0], cat(J_DFQK[0], 2, T))
                for i in range(2):
                    evac(MQT[0:MLA_DIM, 2 * i:2 * i + 2, :], J_MQT[i], cat(J_MQT[i], 2, T)[0:MLA_DIM])
                for i in range(2):
                    evac(MKT[0:MLA_DIM, 2 * i:2 * i + 2, :], J_MKT[i], cat(J_MKT[i], 2, T)[0:MLA_DIM])

                def gate(i):
                    job = at(L, J_G2[i])
                    ps = filled(se, job)
                    for a in range(2):
                        last = act(SG[:, 2 * i + a, :], ps[:, a * T:(a + 1) * T], ACT.Tanh, scale=0.5,
                                   bias=HBIAS[:, 2 * i + a:2 * i + a + 1])
                    last.then_inc(*free(job))

                for h in range(4):
                    ps = filled(se, at(L, J_SBZ[h]))
                    act(SB_E[:, 2 * h:2 * h + 2, :], cat(J_SBZ[h], 2, T), ACT.Abs, scale=HD ** -0.5)
                se.drain()
                act(SB_E, SB_E, ACT.Exp, scale=-1.0)
                se.drain()
                act(SB_E, SB_E, ACT.Ln, bias=1.0).then_inc(sb_log_ready, 1)
                for i in range(4):
                    gate(i)
                se.wait_ge(sb_a_ready, L + 1)
                act(SB_E, SB_E, ACT.Exp).then_inc(sb_exp_ready, 1)
                for i in range(4, 6):
                    gate(i)

                def exps(n):
                    kind, b = SOFT[n]
                    maps = MAPS[kind]
                    se.wait_ge(neg2_ready, L * 6 + n + 1)
                    if kind == "sw":
                        act(sinkx2[:, n % 2, :], sinkx2[:, n % 2, :], ACT.Exp)
                    for h in range(maps):
                        act(PB[n % 2][:, h, :], PB[n % 2][:, h, :], ACT.Exp, scale=SCALE[kind],
                            bias=neg2[:, n % 2, h:h + 1], accum_out=den2[:, n % 2, h:h + 1]).then_inc(probs2_ready, 1)

                def outputs(n):
                    kind, b = SOFT[n]
                    for i in range(0, OUT_HEADS[kind] // 2, 2):
                        pair = probs_before(n) + i
                        if pair >= 2:
                            se.wait_ge(pv2_done, L * N_PAIRS + pair - 1)
                        evac(tmp[:, 0, :], J_PB[n][i])
                    tiles = OUT_HEADS[kind] // 2
                    dst = OTS[BRANCH[kind]][:, :, b * P:b * P + P]
                    src = PS[J_OX[n][0]][:, 0:tiles * P].rearrange("p (a n) -> p a n", a=tiles)
                    if kind == "df":
                        evac(dst, J_OX[n], src, ACT.Copy, scale=SUBG)
                    else:
                        evac(dst, J_OX[n], src)

                evac(OTS[1], J_SBX[0], cat(J_SBX[0], 2, T))
                exps(0)
                for n in range(6):
                    if n < 5:
                        gate(6 + 2 * n)
                        gate(7 + 2 * n)
                        exps(n + 1)
                    outputs(n)

                def moments(i):
                    se.wait_ge(r_ready, L * 2 + i + 1)
                    for t in range(2):
                        last = act(SQ[:, 4 * t:4 * t + 4, :], X[:, t, :].rearrange("p (a n) -> p a n", a=4), ACT.Copy,
                                   accum_out=ss[:, 8, t:t + 1])
                    last.then_inc(sum_ready, 1)
                    se.wait_ge(mean_ready, L * 2 + i + 1)
                    for t in range(2):
                        last = act(SQ[:, 4 * t:4 * t + 4, :], X[:, t, :].rearrange("p (a n) -> p a n", a=4), ACT.Square,
                                   bias=rs[:, 8, t:t + 1], accum_out=ss[:, 9, t:t + 1])
                    last.then_inc(square_ready, 1)

                moments(0)
                to_features(J_XT2)
                filled(se, at(L, J_ROUTE[0]))
                act(ROUTE, PS[J_ROUTE[0][0]][:, 0:64], ACT.Exp, scale=-1.0).then_inc(*free(J_ROUTE[0]))

                def expert(e, first):
                    for t in range(2):
                        ps = filled(se, at(L, J_EXP(e, t)))
                        act(th[:, t, 0:T], ps[:, 0:T], ACT.Tanh, scale=0.5).then_inc(moe_th_ready, 1)
                        if t == 0 and not first:
                            turn(e - 1)

                def turn(e):
                    evac(HIDT, J_EXP(e, 2), cat(J_EXP(e, 2), 2, T))

                expert(0, True)
                expert(1, False)
                with se.Fori(0, EXPERTS // 2 - 1) as g:
                    for r in range(2):
                        expert(g * 2 + (2 + r), False)
                turn(EXPERTS - 1)
                moments(1)

        @block.gpsimd
        def _(po):
            po.memset(neghalf[:, :], -0.5)
            po.memset(inv_width[:, 0:2], 1.0 / C_Q)
            po.memset(inv_width[:, 2:4], 1.0 / C_KV)
            po.memset(inv_width[:, 4:8], 1.0 / HD)
            po.memset(neg_inv_d[:, :], -1.0 / D)
            po.drain()

            def rstd(ev, n, width, halves):
                po.wait_ge(sumsq_ready, ev + 1)
                if halves:
                    po.tensor_tensor(ss[:, ev, 0:n], ss[:, ev, 0:n], ss[:, ev, n:2 * n], ALU.add)
                    po.drain()
                po.tensor_scalar(ss[:, ev, 0:n], ss[:, ev, 0:n], 1.0 / width, EPS, ALU.mult, ALU.add)
                po.drain()
                po.tensor_tensor(rs[:, ev, 0:n], ss[:, ev, 0:n], neghalf[:, 0:n], ALU.pow).then_inc(rstd_ready, 1)

            rstd(0, 4, D, False)
            rstd(1, 4, D, True)
            rstd(2, 4, D, False)
            for d in range(2):
                for li in range(len(LEVELS)):
                    n = d * len(LEVELS) + li
                    po.wait_ge(decay_ready, n + 1)
                    if li:
                        filled(po, J_LEV[d][li - 1][1])
                    po.tensor_tensor(QLEV, HQ, EB, ALU.mult).then_inc(qlev_ready, 1)
                    if li < 4:
                        i = d * 4 + li
                        sg = (SGA, SGH)[i // 4][:, 2 * (i % 4):2 * (i % 4) + 2, :]
                        emptied(po, J_GATE[i])
                        po.tensor_scalar(sg, sg, 0.5, 0.5, ALU.mult, ALU.add).then_inc(gate_ready, 1)
            rstd(3, 2, 4 * P, False)
            rstd(4, 2, D, True)
            rstd(5, 2, D, False)
            rstd(6, 2, D, True)
            with po.Fori(0, LAYERS) as L:
                po.wait_ge(c_squares_ready, L + 1)
                po.tensor_tensor(row_rs[:, 0, :], ss[:, 7, 0:4], inv_width[:, 0:4], ALU.mult)
                po.drain()
                po.tensor_scalar(row_rs[:, 0, :], row_rs[:, 0, :], 1.0, EPS, ALU.mult, ALU.add)
                po.drain()
                po.tensor_tensor(row_rs[:, 1, :], row_rs[:, 0, :], neghalf[:, 0:4], ALU.pow).then_inc(c_rstd_ready, 1)
                for b in range(2):
                    po.wait_ge(df_squares_ready, L * 2 + b + 1)
                    po.tensor_tensor(row_rs[:, 0, :], row_sum[:, b, :], inv_width[:, 4:8], ALU.mult)
                    po.drain()
                    po.tensor_scalar(row_rs[:, 0, :], row_rs[:, 0, :], 1.0, EPS, ALU.mult, ALU.add)
                    po.drain()
                    po.tensor_tensor(row_rs[:, 2 + b, :], row_rs[:, 0, :], neghalf[:, 0:4], ALU.pow).then_inc(df_rstd_ready, 1)
                for i in range(2):
                    po.wait_ge(sum_ready, L * 2 + i + 1)
                    po.tensor_tensor(rs[:, 8, 0:2], ss[:, 8, 0:2], neg_inv_d[:, 0:2], ALU.mult).then_inc(mean_ready, 1)
                    po.wait_ge(square_ready, L * 2 + i + 1)
                    po.tensor_tensor(ss[:, 9, 0:2], ss[:, 9, 0:2], neg_inv_d[:, 0:2], ALU.mult)
                    po.drain()
                    po.tensor_scalar(ss[:, 9, 0:2], ss[:, 9, 0:2], -1.0, LN_EPS, ALU.mult, ALU.add)
                    po.drain()
                    po.tensor_tensor(rs[:, 9, 0:2], ss[:, 9, 0:2], neghalf[:, 0:2], ALU.pow).then_inc(ln_rstd_ready, 1)

        @block.vector
        def _(ve):
            ve.wait_ge(cols_loaded, 16)
            c_kw = cols[:, 0:16].rearrange("p (w k) -> p k w", w=2)
            ve.wait_ge(c_tanh_ready, 1)
            stt(sc[:, :, :], sc[:, :, :], 1.0, c_kw, ALU.add, ALU.mult)
            ve.drain()
            ts(sc[:, :, :], sc[:, :, :], 0.5, None, ALU.mult).then_inc(silu_c_ready, 1)
            for d, (a, b) in enumerate((("lb_f0", "lb_f1"), ("lb_b0", "lb_b1"))):
                tt(lbt[:, 2, 4 * d:4 * d + 4], col(a, 0, 4), col(b, 0, 4), ALU.max)
            ve.drain()
            for d, names in enumerate((("lb_f0", "lb_f1"), ("lb_b0", "lb_b1"))):
                for r in range(2):
                    last = tt(lbt[:, r, 4 * d:4 * d + 4], col(names[r], 0, 4), lbt[:, 2, 4 * d:4 * d + 4], ALU.subtract)
            last.then_inc(lb_max_ready, 1)
            ve.wait_ge(lb_exp_ready, 1)
            tt(lbt[:, 2, :], lbt[:, 0, :], lbt[:, 1, :], ALU.add)
            ve.drain()
            nc.vector.reciprocal(lbt[:, 2, :], lbt[:, 2, :])
            ve.drain()
            for d in range(2):
                tt(lbs[:, d, 0, :], lbt[:, 0, 4 * d:4 * d + 4], lbt[:, 2, 4 * d:4 * d + 4], ALU.mult)
            ve.drain()
            for d in range(2):
                ts(lbs[:, d, 1, :], lbs[:, d, 0, :], -1.0, 1.0, ALU.mult, ALU.add)

            ve.wait_ge(consts_loaded, 16 * N_CONSTS)
            copy(pair_mask[:, :, :], MASK_F)
            nc.vector.memset(ones[:, :], 1.0)
            for u in range(18):
                j, half = u // 2, u % 2
                if j % 3 != 2:
                    ps = filled(ve, J_ADA[u][0])
                    bias = col("b_ada", 4 * u, 4).rearrange("p (k o) -> p k o", o=1).to_broadcast([P, 4, 2])
                    tt(mod[:, j, 4 * half:4 * half + 4, :], ps[:, 0:8].rearrange("p (k w) -> p k w", w=2),
                       bias, ALU.add).then_inc(*free(J_ADA[u][0]))
                else:
                    for w, job in enumerate(J_ADA[u]):
                        g = w if j == 2 else j // 3 + 1
                        ps = filled(ve, job)
                        part = G[:, g, half * BANK:half * BANK + BANK]
                        tt(part, part, ps[:, :], ALU.add).then_inc(*free(job))
            ve.drain()
            for n in range(3):
                pre = col("norm_pre", 8 * n, 8).rearrange("p (k o) -> p k o", o=1).to_broadcast([P, KD, 2])
                stt(gain[:, n, :, :], mod[:, 3 * n + 1, :, :], 1.0, pre, ALU.add, ALU.mult)
            for g, (n, w) in enumerate(((0, 0.5), (0, 0.5), (1, 1.0), (2, 0.5))):
                stt(G[:, g, :], G[:, g, :], w, NORM_POST[:, n, :], ALU.mult, ALU.mult)
            ve.drain().then_inc(gain_ready, 1)

            def normalise(ev, tiles):
                ve.wait_ge(rstd_ready, ev + 1)
                for t in range(tiles):
                    last = ts(XN[:, t, :], X[:, t, :], rs[:, ev, t:t + 1], None, ALU.mult)
                last.then_inc(xn_ready, 1)

            def transposed(n, tiles, J):
                for k in range(0, KD, 2):
                    ps = filled(ve, J[k])
                    for w in range(tiles // 2):
                        last = ts(HT[:, k, w * T:(w + 1) * T], ps[:, w * T:(w + 1) * T],
                                  gain[:, n, k, w:w + 1], mod[:, 3 * n, k, w:w + 1], ALU.mult, ALU.add)
                    last.then_inc(*free(J[k]))

            def ffn_in(J, width, before):
                def body(i, r, g):
                    for j in range(2):
                        gate, up = J(i, 2 * j), J(i, 2 * j + 1)
                        ve.wait_ge(th_ready, i * 2 + (before + j + 1))
                        stt(tmp[:, j, 0:width], th[:, j, 0:width], 1.0, PS[gate[0]][:, 0:width],
                            ALU.add, ALU.mult).then_inc(*free(gate))
                        ve.drain()
                        ps = filled(ve, up)
                        stt(HID[:, i * 2 + j, 0:width], tmp[:, j, 0:width], 0.5, ps[:, 0:width],
                            ALU.mult, ALU.mult).then_inc(*free(up))
                repeat(ve, 11, body)

            def post(ev, tiles, J, gains, buf):
                ve.wait_ge(rstd_ready, ev + 1)
                for half in range(2):
                    cut = slice(half * BANK, half * BANK + BANK)
                    for t in range(tiles):
                        job = J[half * tiles + t]
                        ps = filled(ve, job)
                        stt(buf[:, t, cut], ps[:, :], rs[:, ev, t:t + 1], G[:, gains[t], cut],
                            ALU.mult, ALU.mult).then_inc(*free(job))
                ve.drain()
                tt(X[:, 0:tiles, :], X[:, 0:tiles, :], buf[:, 0:tiles, :], ALU.add).then_inc(x_ready, 1)

            normalise(0, 4)
            transposed(0, 4, J_N1)
            ffn_in(J_FF1A, 2 * T, 0)
            post(1, 4, J_FF1B, (0, 0, 1, 1), XN)

            ve.drain()
            normalise(2, 4)
            transposed(1, 4, J_N2)

            for i in range(2):
                ve.wait_ge(gate_tanh_ready, i + 1)
                ps = PS[J_HQ[i][0]]
                stt(tmp[:, i, :], th[:, i, :], 1.0, ps[:, :], ALU.add, ALU.mult).then_inc(*free(J_HQ[i]))
                ve.drain()
                last = ts(HQ[:, 2 * i:2 * i + 2, :], tmp[:, i, :].rearrange("p (a n) -> p a n", a=2), 0.5, None, ALU.mult)
            last.then_inc(silu_ready, 1)

            def rope(dst, src, table, heads):
                v = src.rearrange("p h (r a n) -> p h r a n", r=2, a=2)
                w = dst.rearrange("p h (r a n) -> p h r a n", r=2, a=2)
                c = table[:, 0, :].rearrange("p (o r n) -> p o r n", o=1, r=2).to_broadcast([P, heads, 2, 16])
                s = table[:, 1, :].rearrange("p (o r n) -> p o r n", o=1, r=2).to_broadcast([P, heads, 2, 16])
                t = [ROPE_T[:, i, 0:heads * 32].rearrange("p (h r n) -> p h r n", h=heads, r=2) for i in range(4)]
                tt(t[0], v[:, :, :, 0, :], c, ALU.mult)
                tt(t[1], v[:, :, :, 1, :], s, ALU.mult)
                tt(t[2], v[:, :, :, 0, :], s, ALU.mult)
                last = tt(t[3], v[:, :, :, 1, :], c, ALU.mult)
                ve.drain()
                tt(w[:, :, :, 0, :], t[0], t[1], ALU.subtract)
                tt(w[:, :, :, 1, :], t[2], t[3], ALU.add)
                ve.drain()

            def forget(d):
                for h in range(HG_HEADS):
                    emptied(ve, J_HF[d][h])
                    ts(KK[:, h, :], KK[:, h, :], 1.0, None, ALU.add)
                    ve.drain()
                    nc.vector.reciprocal(KK[:, h, :], KK[:, h, :])
                    ve.drain()
                    last = ts(KK[:, h, :], KK[:, h, :], lbs[:, d, 1, h:h + 1], lbs[:, d, 0, h:h + 1], ALU.mult, ALU.add)
                last.then_inc(f_ready, 1)

            def cumulate(d):
                ve.wait_ge(lf_ready, d + 1)
                ts(KK, KK, -1.0, 1.0, ALU.mult, ALU.add)
                for h in range(HG_HEADS):
                    nc.vector.tensor_tensor_scan(BB[:, h, :], reset[:, :], BB[:, h, :], 0.0, ALU.mult, ALU.add)
                ve.drain()
                tiles = BB.rearrange("p h (t n) -> p h t n", n=P)
                last = copy(tot[:, d, :, :], tiles[:, :, :, P - 1])
                if d:
                    nc.vector.memset(SHIFT[:, :, :, 0:1], 0.0)
                    for h in range(HG_HEADS):
                        copy(SHIFT[:, h, :, 1:P], tiles[:, h, :, 0:P - 1])
                    ve.drain()
                    last = copy(tiles, SHIFT)
                last.then_inc(cum_ready, 1)

            def states(d):
                for i, tile in enumerate(TILES[d]):
                    n = d * 3 + i
                    ve.wait_ge(kexp_ready, n + 1)
                    tt(KDEC, KDEC, KK[:, :, tile * P:tile * P + P], ALU.mult).then_inc(kdec_ready, 1)
                    job = J_KV[d][i]
                    filled(ve, job)
                    ps = cat(job, 4, P)
                    src, dst = STATE[:, 2 * d, :, :], STATE[:, 2 * d + (i == 2), :, :]
                    if i == 0:
                        dst = STATE[:, 2 * d:2 * d + 1, :, :]
                        copy(STATE[:, 2 * d, :, :], ps).then_inc(*free(job))
                    else:
                        ve.drain()
                        for h in range(HG_HEADS):
                            last = stt(dst[:, h, :], src[:, h, :], dec[:, d, h, tile:tile + 1], ps[:, h, :],
                                       ALU.mult, ALU.add)
                        last.then_inc(*free(job))

            def levels(d):
                ve.wait_ge(qexp_ready, d + 1)
                tt(QDEC[:, 4 * d:4 * d + 4, :], HQ, EB, ALU.mult).then_inc(qdec_ready, 1)

                def pick(li):
                    for tile in range(2):
                        job = J_LEV[d][li][tile]
                        filled(ve, job)
                        which = d * len(LEVELS) + li
                        nc.vector.copy_predicated(SCORE[:, tile, :, :],
                                                  pair_mask[:, which:which + 1, :].to_broadcast([P, 4, P]),
                                                  cat(job, 4, P)).then_inc(*free(job))

                for li, m in enumerate(LEVELS):
                    n = d * len(LEVELS) + li
                    ve.drain()
                    if n:
                        ve.wait_ge(qlev_ready, n)
                    for h in range(HG_HEADS):
                        b = BB[:, h, 0:T].rearrange("p (k n) -> p k n", n=2 * m)
                        e = EB[:, h, :].rearrange("p (k n) -> p k n", n=2 * m)
                        mid = b[:, :, m - 1:m].to_broadcast([P, T // (2 * m), 2 * m])
                        last = tt(e, b, mid, ALU.subtract)
                    last.then_inc(gap_ready, 1)
                    if li:
                        pick(li - 1)
                    ve.wait_ge(decay_ready, n + 1)
                    tt(KLEV, KK[:, :, 0:T], EB, ALU.mult).then_inc(klev_ready, 1)
                pick(len(LEVELS) - 1)
                ve.drain()
                for tile in range(2):
                    job = J_DIAG[d][tile]
                    filled(ve, job)
                    diag = pair_mask[:, 2 * len(LEVELS):, :].to_broadcast([P, 4, P])
                    if d == 0:
                        last = nc.vector.copy_predicated(SCORE[:, tile, :, :], diag, cat(job, 4, P))
                        last.then_inc(*free(job))
                    else:
                        e = EB[:, :, tile * P:tile * P + P]
                        tt(e, SCORE[:, tile, :, :], cat(job, 4, P), ALU.add)
                        ve.drain()
                        nc.vector.copy_predicated(SCORE[:, tile, :, :], diag, e).then_inc(*free(job))

            nc.vector.memset(SCORE, 0.0)
            forget(0)
            for i in range(2):
                job = J_AK[i]
                filled(ve, job)
                v = cat(job, 2, 256)
                for t in range(2):
                    k = v[:, t, 0:P].rearrange("p (h n) -> p h n", h=2)
                    dup = KTOK[:, 2 * i + t, :, :].rearrange("p (g c) n -> p g c n", c=2)
                    if i == 0:
                        rope(dup[:, :, 0, :], k, rope1[:, t, :, :], 2)
                        copy(dup[:, :, 1, :], dup[:, :, 0, :])
                    else:
                        copy(dup[:, :, 0, :], k)
                        copy(dup[:, :, 1, :], k)
                    last = copy(VTOK[:, 2 * i + t, :], v[:, t, P:2 * P])
                last.then_inc(*free(job))
            for t in range(2):
                filled(ve, J_AQ[t])
                rope(QTOK[:, t, :, :], cat(J_AQ[t], 8, HD), rope1[:, t, :, :], 8)
                ve.drain().then_inc(*free(J_AQ[t]))
            cumulate(0)
            for i in range(2):
                ve.wait_ge(gate_tanh_ready, 3 + i)
                ps = PS[J_HG[i][0]]
                stt(tmp[:, i, :], th[:, i, :], 1.0, ps[:, :], ALU.add, ALU.mult).then_inc(*free(J_HG[i]))
                ve.drain()
                for a in range(2):
                    ts(HGT[:, 2 * i + a, :], tmp[:, i, a * T:(a + 1) * T], col("hgrn_norm", 2 * i + a), 0.5, ALU.mult, ALU.mult)
            states(0)
            levels(0)
            forget(1)
            cumulate(1)
            states(1)
            levels(1)
            ve.drain().then_inc(state_ready, 1)
            ve.wait_ge(rstd_ready, 4)
            for t in range(2):
                ts(ONT[:, t, :], PS[J_O[t][0]][:, :], rs[:, 3, t:t + 1], None, ALU.mult).then_inc(*free(J_O[t]))
            for t in range(2):
                filled(ve, J_ORT[t])
                tt(ORT[:, :, t * P:t * P + P], cat(J_ORT[t], 4, P), HGT[:, :, t * P:t * P + P],
                   ALU.mult).then_inc(*free(J_ORT[t]))

            for g in range(2):
                ps = filled(ve, J_KZ[g])
                for half in range(2):
                    last = ts(KZ[:, 2 * g + half, :], ps[:, :], col("halves", half), None, ALU.mult)
                last.then_inc(*free(J_KZ[g]))
            for b in range(2):
                if b:
                    filled(ve, J_PT[0][HEADS - 1])
                for h in range(HEADS):
                    ps = filled(ve, J_S[b][h])
                    nc.vector.tensor_tensor_reduce(out=PROB[:, h, :], in0=ps[:, :], in1=window[:, b, :], scale=1.0,
                                                   scalar=-3e38, op0=ALU.add, op1=ALU.max,
                                                   accum_out=mx[:, b * 8 + h:b * 8 + h + 1]).then_inc(*free(J_S[b][h]))
                cut = slice(b * 8, b * 8 + 8)
                ve.drain()
                stt(negmx[:, cut], mx[:, cut], HD ** -0.5, sink1[:, :], ALU.mult, ALU.max)
                ve.drain()
                tt(sinkx[:, cut], sink1[:, :], negmx[:, cut], ALU.subtract)
                ve.drain()
                ts(negmx[:, cut], negmx[:, cut], -1.0, None, ALU.mult).then_inc(negmax_ready, 1)
                ve.wait_ge(probs_ready, 8 * (b + 1))
                tt(den[:, cut], den[:, cut], sinkx[:, cut], ALU.add)
                ve.drain()
                nc.vector.reciprocal(den[:, cut], den[:, cut])
                for h in range(1, HEADS, 2):
                    ps = filled(ve, J_PT[b][h])
                    if h >= 3:
                        ve.wait_ge(pv_done, b * 7 + h - 1)
                    copy(PT[:, 1, :], ps[:, :]).then_inc(*free(J_PT[b][h]))
                filled(ve, J_PV[b])
                ve.drain()
                tt(OTOK[:, b, :].rearrange("p (h n) -> p h n", h=HEADS), cat(J_PV[b], HEADS, HD),
                   den[:, cut].rearrange("p (h o) -> p h o", o=1).to_broadcast([P, HEADS, HD]),
                   ALU.mult).then_inc(*free(J_PV[b]))

            ve.wait_ge(gate_ready, 8)
            for i in range(4):
                filled(ve, J_WOA[i])
                tt(MERGED[:, 2 * i:2 * i + 2, :], cat(J_WOA[i], 2, T), SGA[:, 2 * i:2 * i + 2, :],
                   ALU.mult).then_inc(*free(J_WOA[i]))
            for i in range(4):
                filled(ve, J_WOH[i])
                part = tmp[:, i % 2, :].rearrange("p (a n) -> p a n", a=2)
                tt(part, cat(J_WOH[i], 2, T), SGH[:, 2 * i:2 * i + 2, :], ALU.mult).then_inc(*free(J_WOH[i]))
                ve.drain()
                last = tt(MERGED[:, 2 * i:2 * i + 2, :], MERGED[:, 2 * i:2 * i + 2, :], part, ALU.add)
            last.then_inc(merged_ready, 1)
            post(4, 2, J_WOUT, (2, 2), YT2)

            ve.drain()
            normalise(5, 2)
            transposed(2, 2, J_N3)
            ffn_in(J_FF2A, T, 22)
            post(6, 2, J_FF2B, (3, 3), XN)
            copy(pos[:, :], pos_i[:, :])
            ve.wait_ge(consts2_loaded, 16 * 8)
            copy(POS_ROW, POS_ROW_I)
            ve.drain()
            for t in range(2):
                ts(POS_ROW_GAP[:, t, :], POS_ROW, pos[:, t:t + 1], None, ALU.subtract)
            ve.drain()
            tt(slide_gap, slide_gap, POS_ROW_GAP, ALU.add)
            tt(causal_gap, causal, POS_ROW_GAP, ALU.add)
            for i in range(2):
                tt(LAMS[:, 2 * i, :, :], LAMS[:, 2 * i, :, :], LAMS[:, 2 * i + 1, :, :], ALU.mult)
            for t in range(2):
                for a in range(2):
                    ts(angle[:, t, a, :], inv_freq[:, :], pos[:, t:t + 1], None, ALU.mult)
            ve.drain()
            for i in range(2):
                last = nc.vector.reduce_sum(lam_sum[:, i, :], LAMS[:, 2 * i, :, :], X_AXIS)
            last.then_inc(lam_ready, 1)
            for a, quarter in ((0, 0.25), (1, 0.0)):
                ts(turns[:, :, a, :], angle[:, :, a, :], float(1 / (2 * np.pi)), quarter, ALU.mult, ALU.add)
            ve.drain()
            ts(turns[:, :, :, :], turns[:, :, :, :], ROUND, -ROUND, ALU.add, ALU.add)
            for part in TWO_PI_PARTS:
                ve.drain()
                stt(angle[:, :, :, :], turns[:, :, :, :], -part, angle[:, :, :, :], ALU.mult, ALU.add)
            ve.drain()
            ts(angle[:, :, 0, :], angle[:, :, 0, :], float(np.pi / 2), None, ALU.add)
            ve.drain()
            ts(angle[:, :, :, :], angle[:, :, :, :], 3.1415925, -3.1415925, ALU.min, ALU.max).then_inc(angle_ready, 1)
            ve.wait_ge(lam_exp_ready, 1)
            tt(neg_lam[:, :], lam_sum[:, 1, :], lam_sum[:, 0, :], ALU.subtract)
            ve.drain()
            ts(lam_sum[:, 0, :], lam_init[:, :], -1.0, 1.0, ALU.mult, ALU.add)
            ve.drain()
            tt(neg_lam[:, :], neg_lam[:, :], lam_init[:, :], ALU.subtract)
            for l in range(LAYERS):
                tt(sub_gain[:, l:l + 1], lam_sum[:, 0, l:l + 1], col("layers", l * PER_LAYER_COLS + 35), ALU.mult)
                ts(half_bias[:, l, :], col("layers", l * PER_LAYER_COLS, 32), 0.5, None, ALU.mult)
            ve.wait_ge(rope2_ready, 1)
            copy(turns[:, 0, 0, 0:1], rope2[:, 0, 0, 0:1])
            with ve.Fori(0, LAYERS) as L:
                ve.drain().then_inc(layer_start, 1)
                copy(LCOLS, cols[:, bass.ds(L * PER_LAYER_COLS + COLS["layers"][0], PER_LAYER_COLS)])
                copy(HBIAS, half_bias[:, bass.ds(L, 1), :])
                copy(SINK2, sink2[:, bass.ds(L, 1), :])
                copy(SUBG, sub_gain[:, bass.ds(L, 1)])
                copy(NEG_LAM, neg_lam[:, bass.ds(L, 1)])
                ve.drain().then_inc(mtok_ready, 1)

                def full_at(job):
                    return filled(ve, at(L, job))

                ve.wait_ge(c_rstd_ready, L + 1)
                for t in range(2):
                    ps = PS[J_C[t][0]]
                    ts(CTOK[:, t, 0:C_Q], ps[:, 0:C_Q], row_rs[:, 1, t:t + 1], None, ALU.mult)
                    ts(CTOK[:, t, C_Q:C_Q + C_KV], ps[:, C_Q:C_Q + C_KV], row_rs[:, 1, 2 + t:3 + t], None, ALU.mult)
                    copy(CTOK[:, t, C_Q + C_KV:], ps[:, C_Q + C_KV:C_Q + C_KV + C_ROPE]).then_inc(*free(J_C[t]))
                ve.drain()

                def rotate(dst, src, t, heads):
                    c = rope2[:, t, 0:1, :].to_broadcast([P, heads, 16])
                    s = rope2[:, t, 1:2, :].to_broadcast([P, heads, 16])
                    a, b = src[:, :, 0:16], src[:, :, 16:32]
                    r = [ROT[:, i, 0:heads * 16].rearrange("p (h n) -> p h n", h=heads) for i in range(4)]
                    tt(r[0], a, c, ALU.mult)
                    tt(r[1], b, s, ALU.mult)
                    tt(r[2], a, s, ALU.mult)
                    tt(r[3], b, c, ALU.mult)
                    ve.drain()
                    tt(dst[:, :, 0:16], r[0], r[1], ALU.subtract)
                    tt(dst[:, :, 16:32], r[2], r[3], ALU.add)
                    ve.drain()

                for t in range(2):
                    rotate(MKTOK[:, t, 0:1, HD:], CTOK[:, t:t + 1, C_Q + C_KV:], t, 1)
                    for h in range(1, MLA_HEADS):
                        copy(MKTOK[:, t, h, HD:], MKTOK[:, t, 0, HD:])
                ps = full_at(J_CT[0])
                for f in range(2):
                    last = ts(CT[:, f, :], ps[:, f * T:(f + 1) * T], LCOLS[:, 32 + f:33 + f], None, ALU.mult)
                last.then_inc(*free(J_CT[0]))
                ps = full_at(J_CT[1])
                ts(CT[:, 2, :], ps[:, 0:T], LCOLS[:, 34:35], None, ALU.mult).then_inc(*free(J_CT[1]))
                ps = full_at(J_SBQK[1])
                for h in range(4):
                    last = ts(SBKZ[:, h, :], ps[:, h // 2 * T:(h // 2 + 1) * T], col("halves", h % 2), None, ALU.mult)
                last.then_inc(*free(J_SBQK[1]))
                for t in range(2):
                    full_at(J_MQ[t])
                    q = PS[J_MQ[t][0]][:, 0:MLA_HEADS * MLA_DIM].rearrange("p (h n) -> p h n", h=MLA_HEADS)
                    copy(MQTOK[:, t, :, 0:HD], q[:, :, 0:HD])
                    rotate(MQTOK[:, t, :, HD:], q[:, :, HD:], t, MLA_HEADS)
                    ve.drain().then_inc(*free(J_MQ[t]))
                for t in range(2):
                    full_at(J_MKV[t])
                    kv = cat(J_MKV[t], MLA_HEADS, P)
                    copy(MKTOK[:, t, :, 0:HD], kv[:, :, 0:HD])
                    copy(MV[:, t, :, :], kv[:, :, HD:]).then_inc(*free(J_MKV[t]))
                ps = full_at(J_SWK[0])
                for g in range(2):
                    for half in range(2):
                        last = ts(SWKZ[:, 2 * g + half, :], ps[:, g * T:(g + 1) * T], col("halves", half), None, ALU.mult)
                last.then_inc(*free(J_SWK[0]))
                ps = full_at(J_DFQK[1])
                for m in range(8):
                    last = ts(DFKZ[:, m, :], ps[:, m // 4 * T:(m // 4 + 1) * T], col("quarters", m % 4), None, ALU.mult)
                last.then_inc(*free(J_DFQK[1]))

                ve.wait_ge(sb_log_ready, L + 1)
                for h in range(4):
                    e, l = SB_E[:, 2 * h:2 * h + 2, :], SB_L[:, 2 * h:2 * h + 2, :]
                    z = cat(J_SBZ[h], 2, T)
                    ts(l, z, HD ** -0.5, None, ALU.mult).then_inc(*free(J_SBZ[h]))
                    ve.drain()
                    stt(e, l, 0.0, e, ALU.min, ALU.subtract)
                    ve.drain()
                    tt(l, e, l, ALU.subtract)
                    ve.drain()
                    last = tt(l, l, sb_mask, ALU.mult)
                last.then_inc(sb_l_ready, 1)
                for h in range(4):
                    full_at(J_SBS[h])
                    e = SB_E[:, 2 * h:2 * h + 2, :]
                    tt(e, e, cat(J_SBS[h], 2, T), ALU.add).then_inc(*free(J_SBS[h]))
                ve.drain().then_inc(sb_a_ready, 1)
                ve.wait_ge(sb_exp_ready, L + 1)
                for h in range(4):
                    e = SB_E[:, 2 * h:2 * h + 2, :]
                    last = tt(e, e, sb_mask, ALU.mult)
                last.then_inc(sbo_ready, 1)
                full_at(J_SBO[0])
                copy(th[:, 0, :], PS[J_SBO[0][0]][:, :]).then_inc(*free(J_SBO[0]))

                def scores(n):
                    kind, b = SOFT[n]
                    buf, side = PB[n % 2], n % 2
                    if n == 1:
                        full_at(J_SBS[3])
                    elif n >= 2:
                        full_at(J_PB[n - 2][-1])
                    for i, job in enumerate(J_SM[n]):
                        full_at(job)
                        ps = cat(job, 2, T)
                        if kind == "mla":
                            tt(buf[:, 2 * i:2 * i + 2, :], ps, causal[:, b:b + 1, :].to_broadcast([P, 2, T]),
                               ALU.add).then_inc(*free(job))
                        else:
                            for a in range(2):
                                m = 2 * i + a
                                slope = 2.0 ** -(m + 1) if kind == "sw" else 2.0 ** (-2.0 * (m // 2 + 1))
                                gap = (slide_gap if kind == "sw" else causal_gap)[:, b, :]
                                last = stt(buf[:, m, :], gap, slope / SCALE[kind], ps[:, a, :], ALU.mult, ALU.add)
                            last.then_inc(*free(job))
                    ve.drain()
                    m = MAPS[kind]
                    nc.vector.reduce_max(mx2[:, side, 0:m], buf[:, 0:m, :], X_AXIS)
                    ve.drain()
                    if kind == "sw":
                        stt(mx2[:, side, :], mx2[:, side, :], SCALE[kind], SINK2, ALU.mult, ALU.max)
                        ve.drain()
                        tt(sinkx2[:, side, :], SINK2, mx2[:, side, :], ALU.subtract)
                        ts(neg2[:, side, :], mx2[:, side, :], -1.0, None, ALU.mult)
                    else:
                        ts(neg2[:, side, 0:m], mx2[:, side, 0:m], -SCALE[kind], None, ALU.mult)
                    ve.drain().then_inc(neg2_ready, 1)

                def weights(n):
                    kind, b = SOFT[n]
                    side, m = n % 2, MAPS[kind]
                    ve.wait_ge(probs2_ready, L * N_MAPS + maps_before(n) + m)
                    if kind == "sw":
                        tt(den2[:, side, :], den2[:, side, :], sinkx2[:, side, :], ALU.add)
                        ve.drain()
                    nc.vector.reciprocal(den2[:, side, 0:m], den2[:, side, 0:m])
                    ve.drain()
                    if kind == "df":
                        for h in range(4):
                            ts(den2[:, side, 2 * h + 1:2 * h + 2], den2[:, side, 2 * h + 1:2 * h + 2], NEG_LAM, None, ALU.mult)
                            p = PB[side][:, 2 * h, :]
                            ts(p, p, den2[:, side, 2 * h:2 * h + 1], None, ALU.mult)
                        ve.drain()
                        for h in range(4):
                            p = PB[side][:, 2 * h, :]
                            stt(p, PB[side][:, 2 * h + 1, :], den2[:, side, 2 * h + 1:2 * h + 2], p, ALU.mult, ALU.add)
                        ve.drain().then_inc(mixed_ready, 1)

                def outputs(n):
                    kind, b = SOFT[n]
                    side, heads = n % 2, OUT_HEADS[kind]
                    for i in range(1, heads // 2, 2):
                        pair = probs_before(n) + i
                        if pair >= 2:
                            ve.wait_ge(pv2_done, L * N_PAIRS + pair - 1)
                        full_at(J_PB[n][i])
                        copy(tmp[:, 1, :], PS[J_PB[n][i][0]][:, :]).then_inc(*free(J_PB[n][i]))
                    if n:
                        full_at(J_OX[n - 1])
                    else:
                        full_at(J_SBX[0])
                    full_at(J_OV[n])
                    out = PS[J_OV[n][0]][:, 0:heads * HD].rearrange("p (h n) -> p h n", h=heads)
                    o = th[:, 0, 0:heads * HD].rearrange("p (h n) -> p h n", h=heads)
                    if kind != "df":
                        r = den2[:, side, 0:heads].rearrange("p (h o) -> p h o", o=1).to_broadcast([P, heads, HD])
                        tt(o, out, r, ALU.mult).then_inc(*free(J_OV[n]))
                    else:
                        copy(o, out)
                        ve.drain()
                        q = th[:, 1, 0:heads * HD].rearrange("p (h n) -> p h n", h=heads)
                        tt(q, o, o, ALU.mult)
                        ve.drain()
                        nc.vector.reduce_sum(row_sum[:, b, :], q, X_AXIS).then_inc(df_squares_ready, 1)
                        ve.wait_ge(df_rstd_ready, L * 2 + b + 1)
                        r = row_rs[:, 2 + b, :].rearrange("p (h o) -> p h o", o=1).to_broadcast([P, heads, HD])
                        tt(o, o, r, ALU.mult).then_inc(*free(J_OV[n]))

                scores(0)
                weights(0)
                for n in range(6):
                    if n < 5:
                        scores(n + 1)
                    outputs(n)
                    if n < 5:
                        weights(n + 1)

                for i in range(16):
                    ve.wait_ge(bank_free[J_G2[i][0]], at(L, J_G2[i])[1] + 1)
                    sg = SG[:, 2 * i:2 * i + 2, :]
                    ts(sg, sg, 0.5, 0.5, ALU.mult, ALU.add)
                ve.drain()
                for j in range(4):
                    for i in range(4):
                        job = J_BR[j][i]
                        full_at(job)
                        m = MERGED2[:, 2 * i:2 * i + 2, :]
                        sg = SG[:, KD * j + 2 * i:KD * j + 2 * i + 2, :]
                        part = tmp[:, i % 2, :].rearrange("p (a n) -> p a n", a=2)
                        if j == 0:
                            tt(m, cat(job, 2, T), sg, ALU.mult).then_inc(*free(job))
                        else:
                            tt(part, cat(job, 2, T), sg, ALU.mult).then_inc(*free(job))
                            ve.drain()
                            tt(m, m, part, ALU.add)
                ve.drain().then_inc(merged2_ready, 1)

                def residual(i, J):
                    for half in range(2):
                        cut = slice(half * BANK, half * BANK + BANK)
                        for t in range(2):
                            job = J(half, t)
                            full_at(job)
                            stt(X[:, t, cut], X[:, t, cut], ALPHA, PS[job[0]][:, :], ALU.mult, ALU.add).then_inc(*free(job))
                    ve.drain().then_inc(r_ready, 1)
                    ve.wait_ge(ln_rstd_ready, L * 2 + i + 1)
                    for t in range(2):
                        ts(X[:, t, :], X[:, t, :], rs[:, 8, t:t + 1], rs[:, 9, t:t + 1], ALU.add, ALU.mult)
                    ve.drain()
                    if i == 0:
                        ve.wait_ge(layer_loaded, L * 96 + 96)
                    tt(X[:, 0:2, :], X[:, 0:2, :], G[:, 2 * i:2 * i + 1, :].to_broadcast([P, 2, D]), ALU.mult)
                    ve.drain()
                    tt(X[:, 0:2, :], X[:, 0:2, :], G[:, 2 * i + 1:2 * i + 2, :].to_broadcast([P, 2, D]),
                       ALU.add).then_inc(ln_done, 1)

                residual(0, lambda half, t: J_OUT2[half * 2 + t])

                emptied(ve, at(L, J_ROUTE[0]))
                ts(ROUTE, ROUTE, 1.0, None, ALU.add)
                ve.drain()
                nc.vector.reciprocal(ROUTE, ROUTE)
                ve.drain()
                scores2 = ROUTE.rearrange("p (g e) -> p g e", e=4)
                tt(BIASED.rearrange("p (t g) e -> p t (g e)", t=2), ROUTE.rearrange("p (t e) -> p t e", t=2),
                   router_bias[:, :].rearrange("p (o e) -> p o e", o=1).to_broadcast([P, 2, EXPERTS]), ALU.add)
                ve.drain()
                n = 0
                for i in range(4):
                    for j in range(i + 1, 4):
                        tt(PAIR[:, :, n:n + 1], BIASED[:, :, i:i + 1], BIASED[:, :, j:j + 1], ALU.add)
                        n += 1
                mine = BIASED.rearrange("p g (j o) -> p g j o", o=1).to_broadcast([P, 16, 4, 4])
                other = BIASED.rearrange("p g (o i) -> p g o i", o=1).to_broadcast([P, 16, 4, 4])
                tt(CMP, other, mine, ALU.is_gt)
                tt(CMP2, other, mine, ALU.is_equal)
                ve.drain()
                nc.vector.reduce_max(GROUP, PAIR[:, :, 0:6], X_AXIS)
                tri = col("tri", 0, 16).rearrange("p (o j i) -> p o j i", o=1, j=4).to_broadcast([P, 16, 4, 4])
                tt(CMP2, CMP2, tri, ALU.mult)
                ve.drain()
                tt(CMP, CMP, CMP2, ALU.add)
                groups = GROUP.rearrange("p (t g) -> p t g", t=2)
                nc.vector.reduce_max(GMAX[:, 0:2], groups, X_AXIS)
                ve.drain()
                nc.vector.reduce_sum(RANK, CMP, X_AXIS)
                picks = PICK.rearrange("p (t g) -> p t g", t=2)
                top = GMAX[:, 0:2].rearrange("p (t o) -> p t o", o=1).to_broadcast([P, 2, 8])
                tt(picks, groups, top, ALU.is_equal)
                ve.drain()
                rev8 = col("rev8", 0, 8).rearrange("p (o g) -> p o g", o=1).to_broadcast([P, 2, 8])
                tt(picks, picks, rev8, ALU.mult)
                ts(RANK, RANK, 1.5, None, ALU.is_lt)
                ve.drain()
                nc.vector.reduce_max(GMAX[:, 2:4], picks, X_AXIS)
                tt(RANK, RANK, scores2, ALU.mult)
                ve.drain()
                top = GMAX[:, 2:4].rearrange("p (t o) -> p t o", o=1).to_broadcast([P, 2, 8])
                tt(picks, picks, top, ALU.is_equal)
                ve.drain()
                tt(RANK, RANK, PICK.rearrange("p (g o) -> p g o", o=1).to_broadcast([P, 16, 4]), ALU.mult)
                ve.drain()
                rank = RANK.rearrange("p (t g) e -> p t (g e)", t=2)
                nc.vector.reduce_sum(GMAX[:, 4:6], rank, X_AXIS)
                ve.drain()
                nc.vector.reciprocal(GMAX[:, 4:6], GMAX[:, 4:6])
                ve.drain()
                for t in range(2):
                    ts(GW[:, t, :], rank[:, t, :], GMAX[:, 4 + t:5 + t], 0.5, ALU.mult, ALU.mult)
                ve.drain()

                def expert(e, first):
                    for t in range(2):
                        job = J_EXP(e, t)
                        ps = PS[job[0]]
                        ve.wait_ge(moe_th_ready, L * (2 * EXPERTS) + e * 2 + (t + 1))
                        stt(tmp[:, t, 0:T], th[:, t, 0:T], 1.0, ps[:, 0:T], ALU.add, ALU.mult)
                        ve.drain()
                        if t == 0 and not first:
                            full_at(J_EXP(e - 1, 2))
                        gate = GW[:, t, e:e + 1] if isinstance(e, int) else GW[:, t, bass.ds(e, 1)]
                        stt(HIDG[:, t, :], tmp[:, t, 0:T], gate, ps[:, T:2 * T], ALU.mult, ALU.mult).then_inc(*free(job))

                expert(0, True)
                expert(1, False)
                with ve.Fori(0, EXPERTS // 2 - 1) as g:
                    for r in range(2):
                        expert(g * 2 + (2 + r), False)
                residual(1, lambda half, t: J_Y[t * 2 + half])

        @block.tensor
        def _(pe):
            pe.wait_ge(silu_c_ready, 1)
            for u in range(18):
                w = loaded(pe, U_ADA + u).rearrange("p (k n) -> p k n", k=KD)
                if (u // 2) % 3 != 2:
                    job = J_ADA[u][0]
                    ps = acquire(pe, job)
                    for c in range(4):
                        for k in range(KD):
                            last = mm(ps[:, 2 * c:2 * c + 2], w[:, k, c * P:c * P + P], sc[:, k, :],
                                      start=k == 0, stop=k == KD - 1)
                    last.then_inc(*full(job))
                else:
                    for who, job in enumerate(J_ADA[u]):
                        ps = acquire(pe, job)
                        for k in range(KD):
                            last = mm(ps[:, :], sc[:, k, who:who + 1].to_broadcast([P, P]), w[:, k, :],
                                      start=k == 0, stop=k == KD - 1)
                        last.then_inc(*full(job))
                release(U_ADA + u)

            def to_features(J, n, tiles):
                pe.wait_ge(xn_ready, n)
                for k in range(KD):
                    ps = acquire(pe, J[k])
                    for t in range(tiles):
                        last = tr(ps[:, t * P:t * P + P], XN[:, t, k * P:k * P + P], ident[:, :])
                    last.then_inc(*full(J[k]))
                for job in J:
                    emptied(pe, job)

            def project(job, out, w, c0, rhs, k0=0, kn=KD, start=True):
                for k in range(kn):
                    last = mm(out, w[:, k0 + k, c0:c0 + P], rhs(k), start=k == 0, stop=k == kn - 1)
                return last

            def ffn_in(first, J, width):
                def body(i, r, g):
                    w = loaded(pe, first + r, g).rearrange("p (a k n) -> p a k n", a=2, k=KD)
                    for j in range(2):
                        for part in range(2):
                            job = J(i, 2 * j + part)
                            ps = acquire(pe, job)
                            project(job, ps[:, 0:width], w[:, part, :, :], j * P,
                                    lambda k: HT[:, k, 0:width]).then_inc(*full(job))
                    release(first + r)
                repeat(pe, 11, body)
                emptied(pe, J(10, 3))

            def ffn_out(first, J, tiles):
                for half in range(2):
                    for part in range(3):
                        w = loaded(pe, first + half * 3 + part).rearrange("p (k n) -> p k n", n=BANK)
                        for f in range(part * 8, min(part * 8 + 8, FT)):
                            for t in range(tiles):
                                job = J[half * tiles + t]
                                if f == 0:
                                    acquire(pe, job)
                                last = mm(PS[job[0]][:, :], HID[:, f, t * P:t * P + P], w[:, f - part * 8, :],
                                          start=f == 0, stop=f == FT - 1)
                                if f == FT - 1:
                                    last.then_inc(*full(job))
                        release(first + half * 3 + part)

            to_features(J_N1, 1, 4)
            ffn_in(U_FF1A, J_FF1A, 2 * T)
            ffn_out(U_FF1B, J_FF1B, 4)

            to_features(J_N2, 2, 4)

            def unit(name):
                u = U_MIX + MIX.index(name)
                return u, loaded(pe, u).rearrange("p (k n) -> p k n", k=KD)

            x_only = lambda k: HT[:, k, 0:T]
            both = lambda k: HT[:, k, :]

            def pairs(name, J):
                u, w = unit(name)
                for i in range(2):
                    ps = acquire(pe, J[i])
                    for a in range(2):
                        last = project(J[i], ps[:, a * T:(a + 1) * T], w, (2 * i + a) * P, x_only)
                    last.then_inc(*full(J[i]))
                release(u)

            def forget(name, J):
                u, w = unit(name)
                for h in range(HG_HEADS):
                    ps = acquire(pe, J[h])
                    project(J[h], ps[:, :], w, h * P, both).then_inc(*full(J[h]))
                release(u)

            pairs("hq", J_HQ)
            forget("hff", J_HF[0])
            u, w = unit("hi")
            for t in range(4):
                ps = acquire(pe, J_HI[t])
                for k in range(KD):
                    last = mm(ps[:, :], HT[:, k, t * P:t * P + P], w[:, k, :], start=k == 0, stop=k == KD - 1)
                last.then_inc(*full(J_HI[t]))
            release(u)
            u = U_MIX + MIX.index("ak")
            w = loaded(pe, u)[:, 0:KD * 256].rearrange("p (k n) -> p k n", k=KD)
            for i in range(2):
                ps = acquire(pe, J_AK[i])
                for a in range(2):
                    for k in range(KD):
                        t = 2 * i + a
                        last = mm(ps[:, a * 256:a * 256 + 256], HT[:, k, t * P:t * P + P], w[:, k, :],
                                  start=k == 0, stop=k == KD - 1)
                last.then_inc(*full(J_AK[i]))
            release(u)
            u, w = unit("aq")
            for t in range(2):
                ps = acquire(pe, J_AQ[t])
                for k in range(KD):
                    last = mm(ps[:, :], HT[:, k, t * P:t * P + P], w[:, k, :], start=k == 0, stop=k == KD - 1)
                last.then_inc(*full(J_AQ[t]))
            release(u)
            pairs("hg", J_HG)

            def recurrence(d):
                for i, tile in enumerate(TILES[d]):
                    n = d * 3 + i
                    pe.wait_ge(kdec_ready, n + 1)
                    job = J_KT[d][i]
                    ps = acquire(pe, job)
                    for h in range(HG_HEADS):
                        last = tr(ps[:, h * P:h * P + P], KDEC[:, h, :], ident[:, :])
                    last.then_inc(*full(job))
                    emptied(pe, job)
                    emptied(pe, J_HI[3])
                    job = J_KV[d][i]
                    ps = acquire(pe, job)
                    for h in range(HG_HEADS):
                        last = mm(ps[:, h * P:h * P + P], KDT[:, h, :], VHG[:, tile, h * P:h * P + P],
                                  start=True, stop=True)
                    last.then_inc(*full(job))

                def pair_scores(J, k_of, q_of):
                    for tile in range(2):
                        ps = acquire(pe, J[tile])
                        for h in range(HG_HEADS):
                            cut = slice(tile * P, tile * P + P)
                            last = mm(ps[:, h * P:h * P + P], k_of[:, h, cut], q_of[:, h, cut], start=True, stop=True)
                        last.then_inc(*full(J[tile]))

                names = (("ga", "ga2"), ("gh", "gh2"))[d]
                for li in range(len(LEVELS)):
                    n = d * len(LEVELS) + li
                    pe.wait_ge(qlev_ready, n + 1)
                    pe.wait_ge(klev_ready, n + 1)
                    pair_scores(J_LEV[d][li], KLEV, QLEV)
                    if li < 4:
                        u, w = unit(names[li // 2])
                        job = J_GATE[4 * d + li]
                        ps = acquire(pe, job)
                        for a in range(2):
                            last = project(job, ps[:, a * T:(a + 1) * T], w, (2 * (li % 2) + a) * P, x_only)
                        last.then_inc(*full(job))
                        if li % 2:
                            release(u)
                pair_scores(J_DIAG[d], KK, HQ)

            recurrence(0)
            forget("hfb", J_HF[1])
            recurrence(1)
            pe.wait_ge(state_ready, 1)
            for t in range(2):
                ps = acquire(pe, J_O[t])
                cut = slice(t * P, t * P + P)
                for h in range(HG_HEADS):
                    out = ps[:, h * P:h * P + P]
                    mm(out, SCORE[:, t, h, :], VHG[:, t, h * P:h * P + P], start=True, stop=False)
                    mm(out, QDEC[:, h, cut], STATE[:, t, h, :], start=False, stop=False)
                    last = mm(out, QDEC[:, 4 + h, cut], STATE[:, 2 + (1 - t), h, :], start=False, stop=True)
                last.then_inc(*full(J_O[t]))
            for t in range(2):
                emptied(pe, J_O[t])
                ps = acquire(pe, J_ORT[t])
                for m in range(4):
                    last = tr(ps[:, m * P:m * P + P], ONT[:, t, m * P:m * P + P], ident[:, :])
                last.then_inc(*full(J_ORT[t]))

            emptied(pe, J_AQ[1])
            for i in range(2):
                ps = acquire(pe, J_QT[i])
                for a in range(2):
                    for t in range(2):
                        m = 2 * i + a
                        src = QTOK[:, t, 2 * m:2 * m + 2, :].rearrange("p h n -> p (h n)")
                        last = tr(ps[:, a * T + t * P:a * T + t * P + P], src, ident[:, :])
                last.then_inc(*full(J_QT[i]))
            for g in range(2):
                ps = acquire(pe, J_KZ[g])
                for t in range(4):
                    src = KTOK[:, t, 2 * g:2 * g + 2, :].rearrange("p h n -> p (h n)")
                    last = tr(ps[:, t * P:t * P + P], src, ident[:, :])
                last.then_inc(*full(J_KZ[g]))
            for job in J_QT + J_KZ:
                emptied(pe, job)
            for b in range(2):
                for h in range(HEADS):
                    ps = acquire(pe, J_S[b][h])
                    mm(ps[:, :], QT[:, h // 2, b * P:b * P + P], KZ[:, 2 * (h // 4) + h % 2, :],
                       start=True, stop=True).then_inc(*full(J_S[b][h]))
                out = acquire(pe, J_PV[b])

                def to_keys(h):
                    pe.wait_ge(probs_ready, b * 8 + h + 1)
                    ps = acquire(pe, J_PT[b][h])
                    for t in range(4):
                        last = tr(ps[:, t * P:t * P + P], PROB[:, h, t * P:t * P + P], ident[:, :])
                    last.then_inc(*full(J_PT[b][h]))

                def weigh(h):
                    emptied(pe, J_PT[b][h])
                    g = h // 4
                    for t in range(4):
                        last = mm(out[:, h * HD:h * HD + HD], PT[:, h % 2, t * P:t * P + P],
                                  VTOK[:, t, g * HD:g * HD + HD], start=t == 0, stop=t == 3)
                    last.then_inc(*(full(J_PV[b]) if h == HEADS - 1 else (pv_done, 1)))

                to_keys(0)
                for h in range(1, HEADS):
                    to_keys(h)
                    weigh(h - 1)
                weigh(HEADS - 1)
                emptied(pe, J_PV[b])
                ps = acquire(pe, J_OT[b])
                for m in range(4):
                    last = tr(ps[:, m * P:m * P + P], OTOK[:, b, m * P:m * P + P], ident[:, :])
                last.then_inc(*full(J_OT[b]))
            emptied(pe, J_OT[1])
            emptied(pe, J_ORT[1])
            for u, J, src in ((U_WOA, J_WOA, OT), (U_WOH, J_WOH, ORT)):
                w = loaded(pe, u).rearrange("p (k n) -> p k n", k=4)
                for i in range(4):
                    ps = acquire(pe, J[i])
                    for a in range(2):
                        last = project(J[i], ps[:, a * T:(a + 1) * T], w, (2 * i + a) * P,
                                       lambda k: src[:, k, :], kn=4)
                    last.then_inc(*full(J[i]))
                release(u)
            pe.wait_ge(merged_ready, 1)
            for half in range(2):
                w = loaded(pe, U_WOUT + half).rearrange("p (k n) -> p k n", k=KD)
                for t in range(2):
                    job = J_WOUT[half * 2 + t]
                    ps = acquire(pe, job)
                    for k in range(KD):
                        last = mm(ps[:, :], MERGED[:, k, t * P:t * P + P], w[:, k, :], start=k == 0, stop=k == KD - 1)
                    last.then_inc(*full(job))
                release(U_WOUT + half)

            to_features(J_N3, 3, 2)
            ffn_in(U_FF2A, J_FF2A, T)
            ffn_out(U_FF2B, J_FF2B, 2)
            pe.wait_ge(consts2_loaded, 16 * 8)
            with pe.Fori(0, LAYERS) as L:
                def take(job):
                    return acquire(pe, at(L, job))

                def taken(job):
                    emptied(pe, at(L, job))

                def landed(u, g=0):
                    pe.wait_ge(slot_loaded[u % 4], L * LAYER_DMAS[u % 4] + g * (16 * units.dmas[u]) + units.loaded(u))
                    return ring[:, u % 4, :]

                def slot(u, width, k=KD, g=0):
                    return landed(u, g)[:, 0:k * width].rearrange("p (k n) -> p k n", k=k)

                xt = lambda k: HT[:, k, 0:T]

                def to_features(J, ready):
                    pe.wait_ge(*ready)
                    for i in range(4):
                        ps = take(J[i])
                        for a in range(2):
                            for t in range(2):
                                k = 2 * i + a
                                last = tr(ps[:, a * T + t * P:a * T + t * P + P], X[:, t, k * P:k * P + P], ident[:, :])
                        last.then_inc(*full(J[i]))
                    for job in J:
                        taken(job)

                def tokens(out, w, t, c0, n, src=None, kn=KD, k0=0):
                    for k in range(kn):
                        lhs = HT[:, k, t * P:t * P + P] if src is None else src[:, k, t * P:t * P + P]
                        last = mm(out, lhs, w[:, k0 + k, c0:c0 + n], start=k == 0, stop=k == kn - 1)
                    return last

                def features(job, w, c0, tiles=2):
                    ps = take(job)
                    for a in range(tiles):
                        last = project(job, ps[:, a * T:(a + 1) * T], w, c0 + a * P, xt)
                    last.then_inc(*full(job))

                pe.wait_ge(mtok_ready, L + 1)
                to_features(J_XT, (layer_start, L + 1))
                w = slot(U_IN, 416)
                for t in range(2):
                    ps = take(J_C[t])
                    tokens(ps[:, 0:416], w, t, 0, 416).then_inc(*full(J_C[t]))
                release(U_IN)
                w = slot(U_IN + 1, BANK)
                for i in range(2):
                    features(J_SBQK[i], w, i * 256)
                release(U_IN + 1)
                taken(J_C[1])
                ps = take(J_CT[0])
                for f in range(2):
                    for t in range(2):
                        last = tr(ps[:, f * T + t * P:f * T + t * P + P], CTOK[:, t, f * P:f * P + P], ident[:, :])
                last.then_inc(*full(J_CT[0]))
                ps = take(J_CT[1])
                for t in range(2):
                    last = tr(ps[:, t * P:t * P + P], CTOK[:, t, C_Q:C_Q + C_KV], ident[:, :])
                last.then_inc(*full(J_CT[1]))
                w = slot(U_IN + 2, 384)
                for t in range(2):
                    ps = take(J_VTOK[t])
                    tokens(ps[:, 0:384], w, t, 0, 384).then_inc(*full(J_VTOK[t]))
                release(U_IN + 2)
                taken(J_CT[0])
                taken(J_CT[1])
                pe.wait_ge(layer_loaded, L * 96 + 96)
                for t in range(2):
                    ps = take(J_MQ[t])
                    tokens(ps[:, 0:384], W_UQ, t, 0, 384, src=CT, kn=2).then_inc(*full(J_MQ[t]))
                for t in range(2):
                    ps = take(J_MKV[t])
                    mm(ps[:, :], CT[:, 2, t * P:t * P + P], W_UKV, start=True, stop=True).then_inc(*full(J_MKV[t]))
                w = slot(U_IN + 3, BANK)
                for i in range(2):
                    features(J_SWQ[i], w, i * 256)
                release(U_IN + 3)
                w = slot(U_IN4, BANK)
                features(J_SWK[0], w, 0)
                ps = take(J_DFV[0])
                for t in range(2):
                    last = tokens(ps[:, t * T:(t + 1) * T], w, t, 256, 256)
                last.then_inc(*full(J_DFV[0]))
                release(U_IN4)
                w = slot(U_IN5, BANK)
                for i in range(2):
                    features(J_DFQK[i], w, i * 256)
                release(U_IN5)
                taken(J_MQ[1])
                taken(J_MKV[1])
                for J, src in ((J_MQT, MQTOK), (J_MKT, MKTOK)):
                    for i in range(2):
                        ps = take(J[i])
                        for a in range(2):
                            for t in range(2):
                                last = tr(ps[0:MLA_DIM, a * T + t * P:a * T + t * P + P], src[:, t, 2 * i + a, :], ident[:, :])
                        last.then_inc(*full(J[i]))

                gates_done = [0]

                def gate(n):
                    for i in range(gates_done[0], gates_done[0] + n):
                        u = U_GATES + i // 2
                        features(J_G2[i], slot(u, BANK), (i % 2) * 256)
                        if i % 2:
                            release(u)
                    gates_done[0] += n

                taken(J_SBQK[0])
                taken(J_SBQK[1])
                for h in range(4):
                    ps = take(J_SBZ[h])
                    for kt in range(2):
                        last = mm(ps[:, kt * T:(kt + 1) * T], SBKZ[:, h, kt * P:kt * P + P], SBQT[:, h // 2, :],
                                  start=True, stop=True)
                    last.then_inc(*full(J_SBZ[h]))
                taken(J_MQT[1])
                taken(J_MKT[1])
                gate(4)
                pe.wait_ge(sb_l_ready, L + 1)
                for h in range(4):
                    ps = take(J_SBS[h])
                    l0, l1 = SB_L[:, 2 * h, :], SB_L[:, 2 * h + 1, :]
                    mm(ps[:, 0:T], later[:, :], l0, start=True, stop=False)
                    mm(ps[:, 0:T], ones[:, :], l1, start=False, stop=True)
                    mm(ps[:, T:2 * T], later[:, :], l1, start=True, stop=True).then_inc(*full(J_SBS[h]))
                gate(2)
                pe.wait_ge(sbo_ready, L + 1)
                taken(J_VTOK[0])
                taken(J_VTOK[1])
                ps = take(J_SBO[0])
                for b in range(2):
                    for h in range(4):
                        for kt in range(2):
                            last = mm(ps[:, b * T + h * HD:b * T + h * HD + HD], SB_E[:, 2 * h + kt, b * P:b * P + P],
                                      SBV[:, kt, h * HD:h * HD + HD], start=kt == 0, stop=kt == 1)
                last.then_inc(*full(J_SBO[0]))
                taken(J_SBO[0])
                ps = take(J_SBX[0])
                for f in range(2):
                    for b in range(2):
                        last = tr(ps[:, f * T + b * P:f * T + b * P + P], th[:, 0, b * T + f * P:b * T + f * P + P], ident[:, :])
                last.then_inc(*full(J_SBX[0]))

                def scores(n):
                    kind, b = SOFT[n]
                    cut = slice(b * P, b * P + P)
                    if n == 0:
                        taken(J_SWQ[1])
                        taken(J_DFQK[0])
                        taken(J_SWK[0])
                        taken(J_DFQK[1])
                    for i, job in enumerate(J_SM[n]):
                        ps = take(job)
                        for a in range(2):
                            m = 2 * i + a
                            if kind == "mla":
                                q, k = MQT[0:MLA_DIM, m, cut], MKT[0:MLA_DIM, m, :]
                            elif kind == "sw":
                                q, k = SWQT[:, m // 2, cut], SWKZ[:, 2 * (m // 4) + m % 2, :]
                            else:
                                q, k = DFQT[:, m // 4, cut], DFKZ[:, m, :]
                            last = mm(ps[:, a * T:(a + 1) * T], q, k, start=True, stop=True)
                        last.then_inc(*full(job))

                def outputs(n):
                    kind, b = SOFT[n]
                    side, heads = n % 2, OUT_HEADS[kind]
                    step = 2 if kind == "df" else 1

                    def to_keys(i):
                        if kind == "df":
                            pe.wait_ge(mixed_ready, L * 2 + b + 1)
                        else:
                            pe.wait_ge(probs2_ready, L * N_MAPS + maps_before(n) + 2 * i + 2)
                        ps = take(J_PB[n][i])
                        for a in range(2):
                            for kt in range(2):
                                c = (2 * a + kt) * P
                                last = tr(ps[:, c:c + P], PB[side][:, (2 * i + a) * step, kt * P:kt * P + P], ident[:, :])
                        last.then_inc(*full(J_PB[n][i]))

                    def weigh(out, i):
                        taken(J_PB[n][i])
                        for a in range(2):
                            h = 2 * i + a
                            for kt in range(2):
                                if kind == "mla":
                                    v = MV[:, kt, h, :]
                                elif kind == "sw":
                                    v = SWV[:, kt, h // 4 * HD:h // 4 * HD + HD]
                                else:
                                    v = DFV[:, kt, h * HD:h * HD + HD]
                                c = (2 * a + kt) * P
                                last = mm(out[:, h * HD:h * HD + HD], tmp[:, i % 2, c:c + P], v, start=kt == 0, stop=kt == 1)
                        return last

                    n_pairs = heads // 2
                    out = None
                    for i in range(n_pairs + 1):
                        if i < n_pairs:
                            to_keys(i)
                        if i:
                            if out is None:
                                out = take(J_OV[n])
                            last = weigh(out, i - 1)
                            if i < n_pairs:
                                last.then_inc(pv2_done, 1)
                    last.then_inc(*full(J_OV[n]))
                    nc.tensor.drain().then_inc(pv2_done, 1)
                    taken(J_OV[n])
                    ps = take(J_OX[n])
                    for f in range(heads // 2):
                        last = tr(ps[:, f * P:f * P + P], th[:, 0, f * P:f * P + P], ident[:, :])
                    last.then_inc(*full(J_OX[n]))

                scores(0)
                for n in range(6):
                    if n < 5:
                        gate(2)
                        scores(n + 1)
                    outputs(n)

                for j in range(4):
                    kn = BRANCH_TILES[j]
                    if j == 0:
                        taken(J_OX[1])
                        taken(J_OX[3])
                        taken(J_OX[5])
                    w = slot(U_BR + j, D, kn)
                    for i in range(4):
                        ps = take(J_BR[j][i])
                        for a in range(2):
                            last = project(J_BR[j][i], ps[:, a * T:(a + 1) * T], w, (2 * i + a) * P,
                                           lambda k: OTS[j][:, k, :], kn=kn)
                        last.then_inc(*full(J_BR[j][i]))
                    release(U_BR + j)
                pe.wait_ge(merged2_ready, L + 1)
                for half in range(2):
                    w = slot(U_OUT2 + half, BANK)
                    for t in range(2):
                        job = J_OUT2[half * 2 + t]
                        tokens(take(job)[:, :], w, t, 0, BANK, src=MERGED2).then_inc(*full(job))
                    release(U_OUT2 + half)

                to_features(J_XT2, (ln_done, L * 2 + 1))
                ps = take(J_ROUTE[0])
                for t in range(2):
                    last = tokens(ps[:, t * EXPERTS:(t + 1) * EXPERTS], w_router, t, 0, EXPERTS)
                last.then_inc(*full(J_ROUTE[0]))

                def hidden(e, t, w):
                    job = J_EXP(e, t)
                    tokens(take(job)[:, :], w, t, 0, BANK).then_inc(*full(job))

                def turn(e):
                    job = J_EXP(e, 2)
                    taken(J_EXP(e, 1))
                    ps = take(job)
                    for f in range(2):
                        for t in range(2):
                            last = tr(ps[:, f * T + t * P:f * T + t * P + P], HIDG[:, t, f * P:f * P + P], ident[:, :])
                    last.then_inc(*full(job))

                def down(e, r, g, first=False, end=False):
                    u = U_MOE + 2 * r + 1
                    w = slot(u, D, 2, g)
                    taken(J_EXP(e, 2))
                    for t in range(2):
                        for half in range(2):
                            job = J_Y[2 * t + half]
                            ps = take(job) if first else PS[job[0]]
                            for f in range(2):
                                last = mm(ps[:, :], HIDT[:, f, t * P:t * P + P], w[:, f, half * BANK:half * BANK + BANK],
                                          start=first and f == 0, stop=end and f == 1)
                            if end:
                                last.then_inc(*full(job))
                    release(u)

                def expert(e, r, g, last_e, last_r, last_g, second=False):
                    u = U_MOE + 2 * r
                    w = slot(u, BANK, KD, g)
                    hidden(e, 0, w)
                    turn(last_e)
                    hidden(e, 1, w)
                    release(u)
                    down(last_e, last_r, last_g, first=second)

                w = slot(U_MOE, BANK)
                hidden(0, 0, w)
                hidden(0, 1, w)
                release(U_MOE)
                expert(1, 1, 0, 0, 0, 0, second=True)
                with pe.Fori(0, EXPERTS // 2 - 1) as g:
                    for r in range(2):
                        expert(g * 2 + (2 + r), r, g + 1, g * 2 + (1 + r), 1 - r, g + r)
                turn(EXPERTS - 1)
                down(EXPERTS - 1, 1, EXPERTS // 2 - 1, end=True)


def vector_pack(a):
    parts = [a["c"], a["c_ctx"], a["b_ada"], a["norm_pre"], a["hgrn_lb_fwd"], a["hgrn_lb_bwd"], a["hgrn_norm"]]
    pack = np.concatenate([np.asarray(p).reshape(-1, P) for p in parts]).T
    return pack


_LAYER_WEIGHTS = ("w_in", "w_gate", "w_br_a", "w_br_b", "w_br_c", "w_br_d", "w_out", "moe_w1", "moe_w3", "moe_w2",
                  "w_uq", "w_ukv")
_LAYER_VECTORS = ("ln1_g", "ln1_b", "ln2_g", "ln2_b", "df_lq1", "df_lk1", "df_lq2", "df_lk2", "sw_sinks")
_WEIGHTS = ("w_ada", "ffn1_w_in", "ffn1_w_out", "ffn2_w_in", "ffn2_w_out", "mix_w_in", "w_o_attn", "w_o_hgrn", "w_out")
_VECTORS = ("norm_post", "b_ada", "attn_sink")


def kernel(**inputs):
    from concourse import bacc
    from concourse.bass_utils import run_bass_kernel_spmd

    a = {k: np.asarray(v) for k, v in inputs.items()}
    k = shape_constants()
    data = {n: a[n][0] for n in _WEIGHTS + _VECTORS}
    data["x"], data["ctx"] = a["x"][0], a["ctx"][0]
    for n in _LAYER_WEIGHTS:
        data["l_" + n] = a[n + "_2"].reshape(-1, a[n + "_2"].shape[-1])
    for n in _LAYER_VECTORS:
        data[n] = a[n + "_2"]
    data["w_router"], data["router_bias"] = a["w_router_2"], a["router_bias_2"]
    positions = a["positions_2"]
    data["pos_cols"], data["pos_row"] = positions.reshape(2, P).T, positions
    layer_cols = []
    for l in range(LAYERS):
        layer_cols += [a["b_gate_2"][l].reshape(32, P), a["mla_q_norm_2"][l].reshape(2, P),
                       a["mla_kv_norm_2"][l].reshape(1, P), np.tile(a["df_subln_2"][l], 2).reshape(1, P)]
    data["cols"] = np.ascontiguousarray(np.concatenate(
        [vector_pack(a), k["halves"], k["quarters"], k["rev8"], k["tri"], np.concatenate(layer_cols).T], axis=1))
    for n in ("pair_masks", "ident", "reset", "window", "rope", "causal", "slide", "later", "sb_mask", "inv_freq", "lam_init"):
        data[n] = k[n]
    data = {n: np.ascontiguousarray(v) for n, v in data.items()}

    nc = bacc.Bacc("TRN2", target_bir_lowering=False, num_devices=1,
                   dynamic_dma_scratch_size=1024)
    io = {n: nc.dram_tensor(f"in_{n}", v.shape, mybir.dt.from_np(v.dtype), kind="ExternalInput").ap()
          for n, v in data.items()}
    io["out"] = nc.dram_tensor("out", (T, D), mybir.dt.float32, kind="ExternalOutput").ap()
    build_program(nc, io)
    r = run_bass_kernel_spmd(nc, [{f"in_{n}": v for n, v in data.items()}], core_ids=[0])
    return r.results[0]["out"].reshape(1, T, D)
```

```python
from contextlib import ExitStack

import concourse.bass as bass
import numpy as np
from concourse import mybir

P = 128
D = 1024
KD = D // P
T = 256
D_FF = 2816
FT = D_FF // P
EPS = 1e-6
LN_EPS = 1e-5
BANK = 512

HEADS, HD = 8, 64
HG_HEADS = 4
WINDOW = 128
GRID_W = 64
IN1 = dict(aq=0, ak=512, hq=768, hff=1280, hfb=1792, hi=2304, hg=2816, ga=3328, gh=4352)
LEVELS = [64, 32, 16, 8, 4, 2, 1]
NEG = -1e30

LAYERS = 2
ALPHA = (2 * LAYERS) ** 0.25
EXPERTS, GROUPS, PER_GROUP, D_EXPERT = 32, 8, 4, 256
PASSES = GROUPS + 1
MLA_HEADS, MLA_DIM = 4, 96
IN2_WIDTH = 2720
IN2 = dict(c=0, sbqk=416, sbv=928, swq=1184, swk=1696, swv=1824, dfqk=1952, dfv=2464)
BRANCH_TILES = (2, 2, 4, 2)
C_Q, C_KV, C_ROPE = 256, 128, 32
TWO_PI_PARTS = (6.28125, 0.0019350051879882812, 3.019916050561733e-07)
ROUND = 1.5 * 2.0 ** 23

COLS = {}
_at = 0
for _name, _n in (("c", 8), ("c_ctx", 8), ("b_ada", 72), ("norm_pre", 24), ("lb_f0", 4), ("lb_f1", 4),
                  ("lb_b0", 4), ("lb_b1", 4), ("hgrn_norm", 4), ("halves", 2), ("quarters", 4),
                  ("rev8", 8), ("tri", 16), ("layers", 72)):
    COLS[_name] = (_at, _n)
    _at += _n
N_COLS = _at
PER_LAYER_COLS = 36


class Jobs:

    def __init__(self, used):
        self.used = list(used)

    def take(self, *banks):
        jobs = []
        for b in banks:
            jobs.append((b, self.used[b]))
            self.used[b] += 1
        return jobs


class Units:

    SLOTS = 4

    def __init__(self):
        self.dmas = []

    def add(self, n, dmas=1):
        first = len(self.dmas)
        self.dmas += [dmas] * n
        return first

    def loaded(self, u):
        return 16 * sum(self.dmas[v] for v in range(u % self.SLOTS, u + 1, self.SLOTS))


def shape_constants():
    f32 = np.float32
    i = np.arange(P)
    s, t = i[:, None], i[None, :]
    masks = []
    for m in LEVELS:
        masks.append((s // (2 * m) == t // (2 * m)) & (s % (2 * m) < m) & (t % (2 * m) >= m))
    masks += [x.T for x in masks]
    masks.append(s == t)
    pair_masks = np.stack(masks, 1).astype(f32)
    q = np.arange(T)
    gap = q[:, None] - q[None, :]
    tok = lambda a: np.ascontiguousarray(a.reshape(2, P, -1).transpose(1, 0, 2).astype(f32))
    window = np.zeros((T, 2 * T), f32)
    window[:, :T] = np.where(np.abs(gap) <= WINDOW, 0.0, NEG)
    causal = tok(np.where(gap >= 0, 0.0, NEG))
    slide = tok(np.where((gap >= 0) & (gap < P), 0.0, NEG))
    freqs = f32(10000.0) ** (-np.arange(16, dtype=f32) / f32(16))
    row, col = q // GRID_W, q % GRID_W
    ang = np.concatenate([row[:, None].astype(f32) * freqs, col[:, None].astype(f32) * freqs], 1)
    rope = tok(np.concatenate([np.cos(ang), np.sin(ang)], 1))
    reset = np.ones((P, 4 * P), f32)
    reset[:, ::P] = 0.0
    keys_first = np.stack([(q[:, None] < q[None, :])[k * P:(k + 1) * P] for k in range(2)], 1)
    halves = np.stack([i < 64, i >= 64], 1)
    quarters = np.stack([i // 32 == n for n in range(4)], 1)
    rev8 = np.tile(8.0 - np.arange(8), (P, 1))
    pick_row = np.stack([np.tile(s % 32 == w, (1, P)) for w in range(2)], 1)
    tri = np.tile(np.tril(np.ones((4, 4)), -1).reshape(1, 16), (P, 1))
    lam_init = np.array([0.8 - 0.6 * np.exp(-0.3 * l) for l in range(LAYERS)], f32)
    return dict(
        pair_masks=pair_masks, window=tok(window), causal=causal, slide=slide, rope=rope, reset=reset,
        pick_row=pick_row.astype(f32), ident=np.eye(P, dtype=f32), later=(s > t).astype(f32), sb_mask=keys_first.astype(f32),
        halves=halves.astype(f32), quarters=quarters.astype(f32),
        inv_freq=np.tile(freqs, (P, 1)), lam_init=np.tile(lam_init, (P, 1)),
        iota=np.tile(np.arange(P), (P, 1)).astype(f32), rev8=rev8.astype(f32), tri=tri.astype(f32),
    )


def build_program(nc, io, stop=None):
    fp32 = mybir.dt.float32
    fp32r = mybir.dt.float32r
    u8 = mybir.dt.uint8
    i32 = mybir.dt.int32
    ALU = mybir.AluOpType
    ACT = mybir.ActivationFunctionType
    X_AXIS = mybir.AxisListType.X
    mm = nc.tensor.matmul
    tr = nc.tensor.transpose
    act = nc.scalar.activation
    tt = nc.vector.tensor_tensor
    ts = nc.vector.tensor_scalar
    stt = nc.vector.scalar_tensor_tensor
    copy = nc.vector.tensor_copy

    with ExitStack() as ctx:
        def sb(name, shape, dt=fp32):
            return ctx.enter_context(nc.sbuf_tensor(name, shape, dt))

        def sem(name):
            return ctx.enter_context(nc.semaphore(name))

        ring = sb("ring", [P, 4, 4096])
        X = sb("X", [P, 4, D])
        G = sb("G", [P, 4, D])
        cols = sb("cols", [P, N_COLS])
        ident = sb("ident", [P, P])
        pair_mask = sb("pair_mask", [P, 2 * len(LEVELS) + 1, P], u8)
        masks = sb("masks", [P, 4, 2 * T])
        reset = masks[:, 0, :]
        window = masks[:, 1:3, :]
        causal = masks[:, 0, :].rearrange("p (t n) -> p t n", t=2)
        slide_gap = masks[:, 1, :].rearrange("p (t n) -> p t n", t=2)
        causal_gap = masks[:, 2, :].rearrange("p (t n) -> p t n", t=2)
        sb_mask = masks[:, 3, :].rearrange("p (t n) -> p t n", t=2)
        rope1 = sb("rope1", [P, 2, 2, 32])
        th = sb("th", [P, 2, BANK])
        tmp = sb("tmp", [P, 2, BANK])
        junk = sb("junk", [P, BANK])
        sc = sb("sc", [P, KD, 2])
        mod = sb("mod", [P, 9, KD, 2])
        gain = sb("gain", [P, 3, KD, 2])
        lbs = sb("lbs", [P, 2, 2, 4])
        lbt = sb("lbt", [P, 3, 8])
        ss = sb("ss", [P, 16, 8])
        rs = sb("rs", [P, 16, 8])
        neghalf = sb("neghalf", [P, 8])
        inv_width = sb("inv_width", [P, 8])
        neg_inv_d = sb("neg_inv_d", [P, 2])
        tot = sb("tot", [P, 2, 4, 4])
        dec = sb("dec", [P, 2, 4, 4])
        mx = sb("mx", [P, 16])
        negmx = sb("negmx", [P, 16])
        den = sb("den", [P, 16])
        sinkx = sb("sinkx", [P, 16])
        sink1 = sb("sink1", [P, HEADS])
        later = sb("later", [P, P])
        ones = sb("ones", [P, P])
        iota = sb("iota", [P, P])
        over_group = sb("over_group", [P, 1], i32)
        w_router = sb("w_router", [P, KD, EXPERTS])
        router_bias = sb("router_bias", [P, EXPERTS])
        rope2 = sb("rope2", [P, 2, 2, 16])
        inv_freq = sb("inv_freq", [P, 16])
        pos_i = sb("pos_i", [P, 2], i32)
        pos = sb("pos", [P, 2])
        lam_init = sb("lam_init", [P, LAYERS])
        lam_sum = sb("lam_sum", [P, 2, LAYERS])
        neg_lam = sb("neg_lam", [P, LAYERS])
        sub_gain = sb("sub_gain", [P, LAYERS])
        half_bias = sb("half_bias", [P, LAYERS, 32])
        sink2 = sb("sink2", [P, LAYERS, 8])
        mx2 = sb("mx2", [P, 2, 8])
        neg2 = sb("neg2", [P, 2, 8])
        den2 = sb("den2", [P, 2, 8])
        sinkx2 = sb("sinkx2", [P, 2, 8])
        row_sum = sb("row_sum", [P, 2, 4])
        row_rs = sb("row_rs", [P, 4, 4])

        with ExitStack() as shared:
            HT = shared.enter_context(nc.sbuf_tensor("HT", [P, KD, 2 * T], fp32))
            arena = shared.enter_context(nc.sbuf_tensor("arena", [P, 20992], fp32))

        X_PARTS = sb("X_PARTS", [P, 2, 2, D], fp32r)
        sb("experts_arena", [P, 4864])
        W_PARTS = sb("W_PARTS", [P, 2, 2, KD // 2, BANK], fp32r)
        TOKEN_PARTS = sb("TOKEN_PARTS", [P, 2, 2, KD, P], fp32r)
        DOWN_PARTS = sb("DOWN_PARTS", [P, 2, D], fp32r)
        PLACE_ONE = sb("PLACE_ONE", [P, 2, P], fp32r)
        PLACE_T = sb("PLACE_T", [P, 2, T], fp32r)

        def region(start, *dims):
            n = int(np.prod(dims))
            v = arena[:, start:start + n]
            if len(dims) == 1:
                return v
            names = "abcd"[:len(dims)]
            return v.rearrange(f"p ({' '.join(names)}) -> p {' '.join(names)}", **dict(zip(names, dims)))

        PS = [ctx.enter_context(nc.psum_tensor(f"bank{b}", [P, BANK], fp32)) for b in range(8)]

        bank_full = [sem(f"bank_full{b}") for b in range(8)]
        bank_free = [sem(f"bank_free{b}") for b in range(8)]
        slot_loaded = [sem(f"slot_loaded{s}") for s in range(4)]
        slot_free = [sem(f"slot_free{s}") for s in range(4)]
        cols_loaded = sem("cols_loaded")
        consts_loaded = sem("consts_loaded")
        c_tanh_ready = sem("c_tanh_ready")
        silu_c_ready = sem("silu_c_ready")
        sumsq_ready = sem("sumsq_ready")
        rstd_ready = sem("rstd_ready")
        xn_ready = sem("xn_ready")
        x_ready = sem("x_ready")
        th_ready = sem("th_ready")
        gain_ready = sem("gain_ready")
        f_ready = sem("f_ready")
        lf_ready = sem("lf_ready")
        cum_ready = sem("cum_ready")
        kexp_ready = sem("kexp_ready")
        kdec_ready = sem("kdec_ready")
        state_ready = sem("state_ready")
        qexp_ready = sem("qexp_ready")
        qdec_ready = sem("qdec_ready")
        gap_ready = sem("gap_ready")
        decay_ready = sem("decay_ready")
        qlev_ready = sem("qlev_ready")
        klev_ready = sem("klev_ready")
        negmax_ready = sem("negmax_ready")
        probs_ready = sem("probs_ready")
        pv_done = sem("pv_done")
        merged_ready = sem("merged_ready")
        out_stored = sem("out_stored")
        lb_max_ready = sem("lb_max_ready")
        lb_exp_ready = sem("lb_exp_ready")
        silu_ready = sem("silu_ready")
        gate_ready = sem("gate_ready")
        gate_tanh_ready = sem("gate_tanh_ready")
        lam_ready = sem("lam_ready")
        lam_exp_ready = sem("lam_exp_ready")
        consts2_loaded = sem("consts2_loaded")
        angle_ready = sem("angle_ready")
        rope2_ready = sem("rope2_ready")
        layer_loaded = sem("layer_loaded")
        c_squares_ready = sem("c_squares_ready")
        c_rstd_ready = sem("c_rstd_ready")
        df_squares_ready = sem("df_squares_ready")
        df_rstd_ready = sem("df_rstd_ready")
        neg2_ready = sem("neg2_ready")
        probs2_ready = sem("probs2_ready")
        mixed_ready = sem("mixed_ready")
        pv2_done = sem("pv2_done")
        r_ready = sem("r_ready")
        sum_ready = sem("sum_ready")
        mean_ready = sem("mean_ready")
        square_ready = sem("square_ready")
        ln_rstd_ready = sem("ln_rstd_ready")
        merged2_ready = sem("merged2_ready")
        moe_th_ready = sem("moe_th_ready")
        picks_ready = sem("picks_ready")
        over_ready = sem("over_ready")
        places_ready = sem("places_ready")
        half_free = [sem(f"half_free{h}") for h in range(2)]
        half_rounded = sem("half_rounded")
        half_split = sem("half_split")
        x_rounded = sem("x_rounded")
        tokens_rounded = sem("tokens_rounded")
        down_rounded = sem("down_rounded")
        sb_log_ready = sem("sb_log_ready")
        sb_l_ready = sem("sb_l_ready")
        sb_a_ready = sem("sb_a_ready")
        sb_exp_ready = sem("sb_exp_ready")
        mtok_ready = sem("mtok_ready")
        sbo_ready = sem("sbo_ready")
        ln_done = sem("ln_done")
        layer_start = sem("layer_start")

        def acquire(eng, job):
            bank, use = job
            if not (isinstance(use, int) and use == 0):
                eng.wait_ge(bank_free[bank], use)
            return PS[bank]

        def filled(eng, job):
            bank, use = job
            eng.wait_ge(bank_full[bank], use + 1)
            return PS[bank]

        def emptied(eng, job):
            bank, use = job
            eng.wait_ge(bank_free[bank], use + 1)

        def full(job):
            return bank_full[job[0]], 1

        def free(job):
            return bank_free[job[0]], 1

        def cat(job, a, b):
            return PS[job[0]][:, :].rearrange("p (a b) -> p a b", a=a)

        units = Units()
        ADA_FIRST = 4
        U_ADA = [units.add(1) for _ in range(ADA_FIRST)]
        U_FF1A = units.add(11, 2)
        U_FF1B, ADA_AFTER = [], []
        for part in range(6):
            U_FF1B.append(units.add(1))
            more = list(range(len(U_ADA), len(U_ADA) + (5, 5, 4, 0, 0, 0)[part]))
            U_ADA += [units.add(1) for _ in more]
            ADA_AFTER.append(more)
        MIX = ["hq", "hff", "hi", "ak", "aq", "hg", "ga", "ga2", "hfb", "gh", "gh2"]
        U_MIX = units.add(11)
        U_WOA = units.add(1)
        U_WOH = units.add(1)
        U_WOUT = units.add(2)
        U_FF2A = units.add(11, 2)
        U_FF2B = [units.add(1) for _ in range(6)]
        U_LAYERS = len(units.dmas)

        jobs = Jobs([0] * 8)
        J_ADA = []

        def ada_jobs(n):
            for u in range(len(J_ADA), len(J_ADA) + n):
                J_ADA.append(jobs.take(*([u % 2, 2 + u % 2] if u // 2 != 2 else [u % 2, 2, 3])))

        ada_jobs(ADA_FIRST)

        def norm_jobs():
            return [jobs.take(k % 8)[0] for k in range(KD)]

        class Loop:

            def __init__(self, n, banks):
                self.first = [jobs.used[b] for b in banks]
                self.banks = banks
                for _ in range(n):
                    jobs.take(*banks)

            def __call__(self, i, k):
                return self.banks[k], self.first[k] + i

        J_N1 = norm_jobs()
        J_FF1A = Loop(11, [0, 1, 2, 3])
        J_FF1B = jobs.take(4, 5, 6, 7)
        ada_jobs(18 - ADA_FIRST)
        J_FF1B += jobs.take(0, 1, 2, 3)
        J_N2 = norm_jobs()
        J_HQ = jobs.take(0, 1)
        J_HF = [jobs.take(2, 3, 4, 5)]
        J_HI = jobs.take(6, 7, 0, 1)
        J_AK = jobs.take(2, 3)
        J_AQ = jobs.take(4, 5)
        J_HG = jobs.take(6, 7)
        J_KT, J_KV, J_LEV, J_DIAG, J_GATE = [], [], [], [], []
        for d in range(2):
            if d == 1:
                J_HF.append(jobs.take(2, 3, 4, 5))
            J_KT.append([])
            J_KV.append([])
            for i in range(3):
                J_KT[d].append(jobs.take(2 * (i % 2))[0])
                J_KV[d].append(jobs.take(2 * (i % 2) + 1)[0])
            J_LEV.append([])
            for li in range(len(LEVELS)):
                J_LEV[d].append(jobs.take(*((0, 1) if li % 2 == 0 else (2, 3))))
                if li < 4:
                    J_GATE.append(jobs.take(4 + li)[0])
            J_DIAG.append(jobs.take(4, 5))
        J_O = jobs.take(0, 1)
        J_ORT = jobs.take(2, 3)
        J_QT = jobs.take(4, 5)
        J_KZ = jobs.take(6, 7)
        J_S, J_PT, J_PV, J_OT = [], [], [], []
        for b in range(2):
            J_S.append([jobs.take(h % 4)[0] for h in range(HEADS)])
            J_PV.append(jobs.take(6)[0])
            J_PT.append([jobs.take(4 + h % 2)[0] for h in range(HEADS)])
            J_OT.append(jobs.take(7)[0])
        J_WOA = jobs.take(0, 1, 2, 3)
        J_WOH = jobs.take(4, 5, 6, 7)
        J_WOUT = jobs.take(0, 1, 2, 3)
        J_N3 = norm_jobs()
        J_FF2A = Loop(11, [0, 1, 2, 3])
        J_FF2B = jobs.take(4, 5, 6, 7)

        U_IN = units.add(4)
        units.dmas[U_IN + 2] = 2
        U_IN4 = units.add(1, 5)
        U_IN5 = units.add(1)
        U_GATES = units.add(8)
        U_BR = units.add(4)
        U_OUT2 = units.add(2)
        U_MOE = len(units.dmas)
        units.add(1, 2)
        for _ in range(PASSES * PER_GROUP - 1):
            units.add(1, 2)
            units.add(1)
        units.add(1)

        def unit_in(p, i):
            if i:
                return U_MOE + 2 * i - 1, p * 2
            return (U_MOE, 0) if isinstance(p, int) and p == 0 else (U_MOE + 2 * PER_GROUP - 1, p * 2 - 2)

        def unit_out(p, i):
            if isinstance(p, int) and (p, i) == (PASSES - 1, PER_GROUP - 1):
                return len(units.dmas) - 1, 0
            return U_MOE + 2 * i + 2, p * 2

        LAYER_TURNS = (len(units.dmas) - U_LAYERS) // 4
        assert (len(units.dmas) - U_LAYERS) % 4 == 0
        LAYER_DMAS = [16 * sum(units.dmas[u] for u in range(U_LAYERS, len(units.dmas)) if u % 4 == s) for s in range(4)]

        before_layers = list(jobs.used)
        J_XT = jobs.take(0, 1, 2, 3)
        J_C = jobs.take(4, 5)
        J_CT = jobs.take(6, 7)
        J_SBQK = jobs.take(0, 1)
        J_MQ = jobs.take(2, 3)
        J_MKV = jobs.take(4, 5)
        J_VTOK = jobs.take(6, 7)
        J_SWQ = jobs.take(0, 1)
        J_SWK = jobs.take(2)
        J_DFV = jobs.take(3)
        J_DFQK = jobs.take(4, 5)
        J_MQT = jobs.take(6, 7)
        J_MKT = jobs.take(0, 1)
        J_SBZ = jobs.take(2, 3, 4, 5)
        J_G2 = jobs.take(6, 7, 6, 7)
        J_SBS = jobs.take(2, 3, 4, 5)
        J_G2 += jobs.take(6, 7)
        J_SM, J_PB, J_OV, J_OX = [], [], [], []
        J_SBO = jobs.take(6)
        J_SBX = jobs.take(6)
        for n, (kind, _) in enumerate((("mla", 0), ("mla", 1), ("sw", 0), ("sw", 1), ("df", 0), ("df", 1))):
            J_SM.append(jobs.take(*range({"mla": 2}.get(kind, 4))))
            J_G2 += jobs.take(7, 7)[:2 if n < 5 else 0] if n < 5 else []
            J_PB.append(jobs.take(*[4 + i % 2 for i in range(4 if kind == "sw" else 2)]))
            J_OV.append(jobs.take(6)[0])
            J_OX.append(jobs.take(6)[0])
        J_BR = [jobs.take(*((0, 1, 2, 3) if j % 2 == 0 else (4, 5, 6, 7))) for j in range(4)]
        J_OUT2 = jobs.take(0, 1, 2, 3)
        J_XT2 = jobs.take(4, 5, 6, 7)
        J_ROUTE = jobs.take(3)
        J_PLACE = jobs.take(3)
        first_use = list(jobs.used)
        HALVES = 2 * PASSES * PER_GROUP

        def halves_before(L, p, i):
            return L * HALVES + (p * (2 * PER_GROUP) + 2 * i)

        def next_expert(p, i):
            return (p, i + 1) if i < PER_GROUP - 1 else (p + 1, 0)

        def half_of(u, h):
            return ring[:, u % 4, h * 2048:h * 2048 + 2048].rearrange("p (k n) -> p k n", n=BANK)


        def j_hidden(p, i):
            return i % 2, first_use[i % 2] + p * 2 + i // 2

        def j_turn(p, i):
            return 2, first_use[2] + p * 4 + i

        def j_slots(p):
            return 3, first_use[3] + p

        def j_down(p, half):
            return 4 + half, first_use[4 + half] + p

        def j_gather(p, half, first=False):
            return 6 + half, first_use[6 + half] + (0 if first else p * 3 - 2)

        def j_scatter(p, t, half, last=False):
            return 6 + half, first_use[6 + half] + (p * 3 + (t + (1 if last else 2)))

        for n, uses in enumerate((2, 2, 4, 1, 1, 1, 3, 3)):
            jobs.take(*[n] * (uses * PASSES))
        LAYER_USES = [n - m for n, m in zip(jobs.used, before_layers)]

        def at(L, job):
            bank, use = job
            return bank, L * LAYER_USES[bank] + use

        def repeat(eng, n, body):
            turns = n // 4
            with eng.Fori(0, turns) as g:
                for r in range(4):
                    body(g * 4 + r, r, g)
            for r in range(n - 4 * turns):
                body(4 * turns + r, 4 * turns + r, 0)

        def loaded(eng, u, g=0):
            value = units.loaded(u)
            if not isinstance(g, int):
                value = g * (16 * units.dmas[u]) + value
            eng.wait_ge(slot_loaded[u % 4], value)
            return ring[:, u % 4, :]

        def released(eng, u, g=0):
            value = u // 4 + g
            if not (isinstance(value, int) and value == 0):
                eng.wait_ge(slot_free[u % 4], value)
            return ring[:, u % 4, :]

        def release(u):
            nc.tensor.drain().then_inc(slot_free[u % 4], 1)

        XN = region(0, 4, D)
        NORM_POST = region(11264, 3, D)
        PICK_ROW = region(14336, 2, P)
        SC = region(14592, KD, 32)
        MASK_F = region(8192, 15, P)
        HID = region(0, FT, 2 * T)
        HQ = region(0, 4, T)
        BB = region(1024, 4, 4 * P)
        KK = region(3072, 4, 4 * P)
        VHG = region(5120, 4, 4 * P)
        STATE = region(7168, 4, 4, P)
        KDEC = region(9216, 4, P)
        KDT = region(9728, 4, P)
        EB = region(10240, 4, T)
        QLEV = region(11264, 4, T)
        KLEV = region(12288, 4, T)
        SHIFT = region(10240, 4, 4, P)
        QDEC = region(13312, 8, T)
        SCORE = region(15360, 2, 4, P)
        HGT = region(16384, 4, T)
        ORT = region(17408, 4, T)
        VTOK = region(18432, 4, P)
        QTOK = region(18944, 2, 8, HD)
        KTOK = region(19968, 4, 4, HD)
        ROPE_T = region(10240, 4, 256)
        ONT = region(10240, 2, 4 * P)
        SGA = X[:, 2:4, :].rearrange("p t (a n) -> p (t a) n", n=T)
        SGH = G[:, 0:2, :].rearrange("p t (a n) -> p (t a) n", n=T)
        PROB = region(0, HEADS, 4 * P)
        PT = region(4096, 2, 4 * P)
        OTOK = region(5120, 2, 4 * P)
        OT = region(6144, 4, T)
        QT = region(7168, 4, T)
        KZ = region(8192, 4, 4 * P)
        MERGED = region(10240, KD, T)
        YT2 = region(13312, 2, D)

        def col(name, i=0, n=1):
            first = COLS[name][0] + i
            return cols[:, first:first + n]

        N_CONSTS = 25
        TILES = ((2, 3, 0), (3, 2, 1))

        block = ctx.enter_context(nc.Block())

        SG = region(0, 4 * KD, T)
        CTOK = region(0, 2, C_Q + C_KV + C_ROPE)
        CT = region(1024, 3, T)
        W_UQ = region(2048, 2, MLA_HEADS * MLA_DIM)
        W_UKV = region(3072, MLA_HEADS * P)
        MQTOK = region(4096, 2, MLA_HEADS, MLA_DIM)
        MKTOK = region(5120, 2, MLA_HEADS, MLA_DIM)
        ROT = region(6144, 4, P)
        OTS = [region(8192, 2, T), region(8704, 2, T), region(9216, 4, T), region(10240, 2, T)]
        MQT = region(10752, MLA_HEADS, T)
        MKT = region(11776, MLA_HEADS, T)
        MV = region(12800, 2, MLA_HEADS, HD)
        SBV = region(13312, 2, T)
        SWV = region(13824, 2, P)
        DFV = region(14080, 2, T)
        SBQT = region(14592, 2, T)
        SBKZ = region(15104, 4, T)
        SWQT = region(16128, 4, T)
        SWKZ = region(17152, 4, T)
        DFQT = region(18176, 2, T)
        DFKZ = region(18688, 8, T)
        LCOLS = region(20736, PER_LAYER_COLS)
        HBIAS = region(20800, 32)
        SINK2 = region(20864, 8)
        SUBG = region(20880, 1)
        NEG_LAM = region(20884, 1)
        POS_ROW_I = region(0, T).bitcast(i32)
        POS_ROW = region(512, T)
        POS_ROW_GAP = region(1024, 2, T)
        LAMS = region(2048, 4, LAYERS, 32)
        angle = region(2560, 2, 2, 16)
        turns = region(2688, 2, 2, 16)
        PB = [X[:, 2:4, :].rearrange("p t (a n) -> p (t a) n", n=T), HT[:, :, T:2 * T]]
        SB_E, SB_L = PB
        MERGED2 = region(10752, KD, T)
        SQ = PB[0]
        HIDG = region(0, 2, T)
        HIDT = region(512, 2, T)
        ROUTE = region(1024, 64)
        BIASED = region(1152, 16, 4)
        PAIR = region(1280, 16, 8)
        GROUP = region(1408, 16)
        GMAX = region(1440, 8)
        PICK = region(1472, 16)
        CMP = region(1536, 16, 4, 4)
        CMP2 = region(1792, 16, 4, 4)
        RANK = region(2048, 16, 4)
        GW = region(2176, 2, EXPERTS + PER_GROUP)
        SLOT = region(2304, 2, PASSES)
        COUNT = region(2336, 2, GROUPS)
        PLACE = region(2368, 2, P + PER_GROUP)
        GATES = region(2688, 2, PER_GROUP)
        SUM = region(2700, 2, D)

        SOFT = [("mla", 0), ("mla", 1), ("sw", 0), ("sw", 1), ("df", 0), ("df", 1)]
        MAPS = dict(mla=4, sw=8, df=8)
        OUT_HEADS = dict(mla=4, sw=8, df=4)
        SCALE = dict(mla=MLA_DIM ** -0.5, sw=HD ** -0.5, df=32.0 ** -0.5)
        BRANCH = dict(mla=0, sb=1, sw=2, df=3)

        def probs_before(n):
            return sum(OUT_HEADS[kind] // 2 for kind, _ in SOFT[:n])

        def maps_before(n):
            return sum(MAPS[kind] for kind, _ in SOFT[:n])

        N_MAPS, N_PAIRS = maps_before(6), probs_before(6)

        @block.sync
        def _(sp):
            def columns(w, first, n):
                return w[:, first:first + n].rearrange("(k p) n -> p k n", p=P)

            def load(u, dst, src, g=0):
                sp.dma_start(dst, src).then_inc(slot_loaded[u % 4], 16)

            def slot(v, k, n):
                return v[:, 0:k * n].rearrange("p (k n) -> p k n", k=k)

            def ada(u):
                load(U_ADA[u], slot(released(sp, U_ADA[u]), KD, BANK), columns(io["w_ada"], u * BANK, BANK))

            for u in range(ADA_FIRST):
                ada(u)

            def ffn_in(first, w):
                def body(i, r, g):
                    v = released(sp, first + r, g).rearrange("p (a k n) -> p a k n", a=2, k=KD)
                    for part in range(2):
                        src = w[:, bass.ds(i * 256 + part * D_FF, 256)]
                        load(first + r, v[:, part, :, :], src.rearrange("(k p) n -> p k n", p=P))
                repeat(sp, 11, body)

            def ffn_out(own, w, after=((),) * 6):
                for half in range(2):
                    for part in range(3):
                        f0, f1 = part * 8, min(part * 8 + 8, FT)
                        u = own[half * 3 + part]
                        v = released(sp, u)
                        load(u, slot(v, f1 - f0, BANK),
                             w[f0 * P:f1 * P, half * BANK:half * BANK + BANK].rearrange("(k p) n -> p k n", p=P))
                        for a in after[half * 3 + part]:
                            ada(a)

            ffn_in(U_FF1A, io["ffn1_w_in"])
            ffn_out(U_FF1B, io["ffn1_w_out"], ADA_AFTER)
            for n, name in enumerate(MIX):
                first = IN1[name[:2] if name.endswith("2") else name] + (BANK if name.endswith("2") else 0)
                width = 256 if name == "ak" else BANK
                v = released(sp, U_MIX + n)
                load(U_MIX + n, slot(v, KD, width), columns(io["mix_w_in"], first, width))
            for u, w in ((U_WOA, io["w_o_attn"]), (U_WOH, io["w_o_hgrn"])):
                v = released(sp, u)
                load(u, slot(v, 4, D), w.rearrange("(k p) n -> p k n", p=P))
            for half in range(2):
                v = released(sp, U_WOUT + half)
                load(U_WOUT + half, slot(v, KD, BANK), columns(io["w_out"], half * BANK, BANK))
            ffn_in(U_FF2A, io["ffn2_w_in"])
            ffn_out(U_FF2B, io["ffn2_w_out"])
            with sp.Fori(0, LAYERS) as L:
                def free_slot(u, g=0):
                    sp.wait_ge(slot_free[u % 4], L * LAYER_TURNS + g + u // 4)
                    return ring[:, u % 4, :]

                def rows(name, n):
                    return io["l_" + name][bass.ds(L * n, n), :]

                def cut(name, n, first, width):
                    return io["l_" + name][bass.ds(L * n, n), first:first + width].rearrange("(k p) n -> p k n", p=P)

                for i, (name, width) in enumerate((("c", 416), ("sbqk", BANK), ("sbv", 384), ("swq", BANK))):
                    v = slot(free_slot(U_IN + i), KD, width)
                    if name == "sbv":
                        load(U_IN + i, v[:, :, 0:256], cut("w_in", D, IN2["sbv"], 256))
                        load(U_IN + i, v[:, :, 256:384], cut("w_in", D, IN2["swv"], P))
                    else:
                        load(U_IN + i, v, cut("w_in", D, IN2[name], width))
                v = slot(free_slot(U_IN4), KD, BANK)
                for i in range(4):
                    load(U_IN4, v[:, :, i * HD:i * HD + HD], cut("w_in", D, IN2["swk"] + i // 2 * HD, HD))
                load(U_IN4, v[:, :, 256:BANK], cut("w_in", D, IN2["dfv"], 256))
                load(U_IN5, slot(free_slot(U_IN5), KD, BANK), cut("w_in", D, IN2["dfqk"], BANK))
                for i in range(8):
                    load(U_GATES + i, slot(free_slot(U_GATES + i), KD, BANK), cut("w_gate", D, i * BANK, BANK))
                for j, name in enumerate(("w_br_a", "w_br_b", "w_br_c", "w_br_d")):
                    n = BRANCH_TILES[j]
                    load(U_BR + j, slot(free_slot(U_BR + j), n, D), cut(name, n * P, 0, D))
                for half in range(2):
                    load(U_OUT2 + half, slot(free_slot(U_OUT2 + half), KD, BANK), cut("w_out", D, half * BANK, BANK))

                def load_in(p, i, first, await_over=False):
                    u, turns = unit_in(p, i)
                    v = slot(free_slot(u, turns), KD, BANK)
                    for n, name in enumerate(("moe_w1", "moe_w3")):
                        src = io["l_" + name][bass.ds(L * (EXPERTS * D) + first * D + i * D, D), :]
                        if n and await_over:
                            sp.wait_ge(over_ready, L + 1)
                        load(u, v[:, :, n * 256:n * 256 + 256], src.rearrange("(k p) n -> p k n", p=P))

                def load_out(p, i, first):
                    u, turns = unit_out(p, i)
                    v = slot(free_slot(u, turns), 2, D)
                    src = io["l_moe_w2"][bass.ds(L * (EXPERTS * D_EXPERT) + first * D_EXPERT + i * D_EXPERT, D_EXPERT), :]
                    load(u, v, src.rearrange("(k p) n -> p k n", p=P))

                load_in(0, 0, 0)
                with sp.Fori(0, GROUPS - 1) as p:
                    for i in range(PER_GROUP):
                        load_in(*next_expert(p, i), (p + (i + 1) // PER_GROUP) * PER_GROUP)
                        load_out(p, i, p * PER_GROUP)
                first = (GROUPS - 1) * PER_GROUP
                load_in(GROUPS - 1, 1, first, await_over=True)
                load_out(GROUPS - 1, 0, first)
                over = sp.value_load(over_group[0:1, 0:1], min_val=0, max_val=EXPERTS - PER_GROUP)
                for i in range(1, PER_GROUP):
                    load_in(*next_expert(GROUPS - 1, i), first if i < PER_GROUP - 1 else over)
                    load_out(GROUPS - 1, i, first)
                for i in range(PER_GROUP):
                    if i < PER_GROUP - 1:
                        load_in(GROUPS, i + 1, over)
                    load_out(GROUPS, i, over)
            sp.wait_ge(ln_done, 2 * LAYERS)
            sp.dma_start(io["out"].rearrange("(t p) n -> p t n", p=P), X[:, 0:2, :]).then_inc(out_stored, 16)
            sp.wait_ge(out_stored, 16)

        @block.scalar
        def _(se):
            def const(dst, src):
                se.dma_start(dst, src).then_inc(consts_loaded, 16)

            se.dma_start(cols[:, :], io["cols"]).then_inc(cols_loaded, 16)
            const(ident[:, :], io["ident"])
            const(X[:, 0:2, :], io["x"].rearrange("(t p) n -> p t n", p=P))
            const(X[:, 2:4, :], io["ctx"].rearrange("(t p) n -> p t n", p=P))
            const(MASK_F, io["pair_masks"])
            const(PICK_ROW, io["pick_row"])
            const(reset[:, :], io["reset"])
            const(window[:, :, :], io["window"])
            const(rope1[:, :, :, :], io["rope"].rearrange("p t (a n) -> p t a n", a=2))
            for g, j in enumerate((2, 2, 5, 8)):
                const(G[:, g, :], io["b_ada"][j * D:(j + 1) * D].partition_broadcast(P))
            for n in range(3):
                const(NORM_POST[:, n, :], io["norm_post"][n, :].partition_broadcast(P))
            const(sink1[:, :], io["attn_sink"].partition_broadcast(P))
            const(later[:, :], io["later"])
            const(iota[:, :], io["iota"])
            const(w_router[:, :, :], io["w_router"].rearrange("(k p) n -> p k n", p=P))
            const(router_bias[:, :], io["router_bias"].partition_broadcast(P))
            const(inv_freq[:, :], io["inv_freq"])
            const(lam_init[:, :], io["lam_init"])
            for l in range(LAYERS):
                const(sink2[:, l, :], io["sw_sinks"][l, :].partition_broadcast(P))
            const(pos_i[:, :], io["pos_cols"])
            se.wait_ge(cols_loaded, 16)
            act(sc[:, :, :], cols[:, 0:16].rearrange("p (w k) -> p k w", w=2), ACT.Tanh, scale=0.5).then_inc(c_tanh_ready, 1)
            se.wait_ge(lb_max_ready, 1)
            act(lbt[:, 0:2, :], lbt[:, 0:2, :], ACT.Exp).then_inc(lb_exp_ready, 1)
            se.wait_ge(consts_loaded, 16 * N_CONSTS)

            def sum_squares(ev, tiles, src, dst):
                for t in range(tiles):
                    last = act(dst(t), src(t), ACT.Square, accum_out=ss[:, ev, t:t + 1])
                last.then_inc(sumsq_ready, 1)

            def transposed(n, tiles, J):
                for k in range(1, KD, 2):
                    ps = filled(se, J[k])
                    for w in range(tiles // 2):
                        last = act(HT[:, k, w * T:(w + 1) * T], ps[:, w * T:(w + 1) * T], ACT.Identity,
                                   scale=gain[:, n, k, w:w + 1], bias=mod[:, 3 * n, k, w:w + 1])
                    last.then_inc(*free(J[k]))

            def ffn_in(J, width):
                def body(i, r, g):
                    for j in range(2):
                        ps = filled(se, J(i, 2 * j))
                        act(th[:, j, 0:width], ps[:, 0:width], ACT.Tanh, scale=0.5).then_inc(th_ready, 1)
                repeat(se, 11, body)

            def post_squares(ev, tiles, J):
                for half in range(2):
                    for t in range(tiles):
                        ps = filled(se, J[half * tiles + t])
                        if half or t:
                            se.drain()
                        last = act(junk[:, :], ps[:, :], ACT.Square, accum_out=ss[:, ev, half * tiles + t:half * tiles + t + 1])
                last.then_inc(sumsq_ready, 1)

            sum_squares(0, 4, lambda t: X[:, t, :], lambda t: XN[:, t, :])
            se.wait_ge(gain_ready, 1)
            transposed(0, 4, J_N1)
            ffn_in(J_FF1A, 2 * T)
            post_squares(1, 4, J_FF1B)

            se.wait_ge(x_ready, 1)
            sum_squares(2, 4, lambda t: X[:, t, :], lambda t: XN[:, t, :])
            transposed(1, 4, J_N2)
            for i in range(2):
                ps = filled(se, J_HQ[i])
                act(th[:, i, :], ps[:, :], ACT.Tanh, scale=0.5).then_inc(gate_tanh_ready, 1)

            def forget_exp(d):
                if d:
                    filled(se, J_DIAG[0][1])
                for h in range(HG_HEADS):
                    ps = filled(se, J_HF[d][h])
                    act(KK[:, h, :], ps[:, :], ACT.Exp, scale=-1.0).then_inc(*free(J_HF[d][h]))

            def recurrence(d):
                se.wait_ge(f_ready, d + 1)
                act(BB, KK, ACT.Ln).then_inc(lf_ready, 1)
                se.wait_ge(cum_ready, d + 1)
                act(dec[:, d, :, :], tot[:, d, :, :], ACT.Exp)
                for i, tile in enumerate(TILES[d]):
                    if i:
                        filled(se, J_KT[d][i - 1])
                    cut = slice(tile * P, tile * P + P)
                    if d == 0:
                        for h in range(HG_HEADS):
                            last = act(KDEC[:, h, :], BB[:, h, cut], ACT.Exp, scale=-1.0,
                                       bias=tot[:, d, h, tile:tile + 1])
                    else:
                        last = act(KDEC, BB[:, :, cut], ACT.Exp)
                    last.then_inc(kexp_ready, 1)
                    ps = filled(se, J_KT[d][i])
                    if i:
                        filled(se, J_KV[d][i - 1])
                    act(KDT, cat(J_KT[d][i], 4, P), ACT.Copy).then_inc(*free(J_KT[d][i]))
                if d == 0:
                    last = act(EB, BB[:, :, 0:T], ACT.Exp)
                else:
                    for h in range(HG_HEADS):
                        for tile in range(2):
                            cut = slice(tile * P, tile * P + P)
                            last = act(EB[:, h, cut], BB[:, h, cut], ACT.Exp, scale=-1.0,
                                       bias=tot[:, d, h, tile:tile + 1])
                last.then_inc(qexp_ready, 1)
                for li in range(len(LEVELS)):
                    n = d * len(LEVELS) + li
                    se.wait_ge(gap_ready, n + 1)
                    act(EB, EB, ACT.Abs)
                    se.drain()
                    act(EB, EB, ACT.Exp, scale=-1.0).then_inc(decay_ready, 1)
                    if 1 <= li <= 4:
                        gate(d * 4 + li - 1)

            def gate(i):
                sg, job = (SGA, SGH)[i // 4], J_GATE[i]
                filled(se, job)
                act(sg[:, 2 * (i % 4):2 * (i % 4) + 2, :], cat(job, 2, T), ACT.Tanh, scale=0.5).then_inc(*free(job))

            forget_exp(0)
            for t in range(4):
                ps = filled(se, J_HI[t])
                act(VHG[:, t, :], ps[:, :], ACT.Copy).then_inc(*free(J_HI[t]))
            se.wait_ge(silu_ready, 1)
            for i in range(2):
                ps = filled(se, J_HG[i])
                act(th[:, i, :], ps[:, :], ACT.Tanh, scale=0.5).then_inc(gate_tanh_ready, 1)
            recurrence(0)
            forget_exp(1)
            recurrence(1)
            for t in range(2):
                ps = filled(se, J_O[t])
                if t:
                    se.drain()
                last = act(junk[:, :], ps[:, :], ACT.Square, accum_out=ss[:, 3, t:t + 1])
            last.then_inc(sumsq_ready, 1)

            emptied(se, J_ORT[1])
            for i in range(2):
                filled(se, J_QT[i])
                act(QT[:, 2 * i:2 * i + 2, :], cat(J_QT[i], 2, T), ACT.Copy).then_inc(*free(J_QT[i]))
            for b in range(2):
                se.wait_ge(negmax_ready, b + 1)
                act(sinkx[:, b * 8:b * 8 + 8], sinkx[:, b * 8:b * 8 + 8], ACT.Exp)
                for h in range(HEADS):
                    act(PROB[:, h, :], PROB[:, h, :], ACT.Exp, bias=negmx[:, b * 8 + h:b * 8 + h + 1],
                        scale=HD ** -0.5, accum_out=den[:, b * 8 + h:b * 8 + h + 1]).then_inc(probs_ready, 1)
                for h in range(0, HEADS, 2):
                    ps = filled(se, J_PT[b][h])
                    if h >= 2:
                        se.wait_ge(pv_done, b * 7 + h - 1)
                    elif b:
                        filled(se, J_PV[b - 1])
                    act(PT[:, 0, :], ps[:, :], ACT.Copy).then_inc(*free(J_PT[b][h]))
                filled(se, J_OT[b])
                act(OT[:, :, b * P:b * P + P], cat(J_OT[b], 4, P), ACT.Copy).then_inc(*free(J_OT[b]))
            post_squares(4, 2, J_WOUT)

            se.wait_ge(x_ready, 2)
            sum_squares(5, 2, lambda t: X[:, t, :], lambda t: XN[:, t, :])
            transposed(2, 2, J_N3)
            ffn_in(J_FF2A, T)
            post_squares(6, 2, J_FF2B)
            se.wait_ge(x_ready, 3)

            def const2(dst, src):
                se.dma_start(dst, src).then_inc(consts2_loaded, 16)

            const2(causal, io["causal"])
            const2(slide_gap, io["slide"])
            const2(sb_mask, io["sb_mask"])
            for i, n in enumerate(("df_lq1", "df_lk1", "df_lq2", "df_lk2")):
                const2(LAMS[:, i, :, :].rearrange("p l n -> p (l n)"), io[n].rearrange("l n -> (l n)").partition_broadcast(P))
            const2(POS_ROW_I, io["pos_row"].partition_broadcast(P))
            se.wait_ge(lam_ready, 1)
            act(lam_sum[:, :, :], lam_sum[:, :, :], ACT.Exp).then_inc(lam_exp_ready, 1)
            se.wait_ge(angle_ready, 1)
            act(rope2[:, :, :, :], angle[:, :, :, :], ACT.Sin).then_inc(rope2_ready, 1)

            with se.Fori(0, LAYERS) as L:
                se.wait_ge(layer_start, L + 1)
                se.dma_start(W_UQ, io["l_w_uq"][bass.ds(L * C_Q, C_Q), :].rearrange("(k p) n -> p k n", p=P)).then_inc(layer_loaded, 16)
                se.dma_start(W_UKV, io["l_w_ukv"][bass.ds(L * C_KV, C_KV), :]).then_inc(layer_loaded, 16)
                for i, n in enumerate(("ln1_g", "ln1_b", "ln2_g", "ln2_b")):
                    se.dma_start(G[:, i, :], io[n][bass.ds(L, 1), :].partition_broadcast(P)).then_inc(layer_loaded, 16)

                def evac(dst, job, src=None, func=ACT.Copy, **kw):
                    filled(se, at(L, job))
                    act(dst, src if src is not None else PS[job[0]][:, :], func, **kw).then_inc(*free(job))

                def to_features(J):
                    for i in range(4):
                        evac(HT[:, 2 * i:2 * i + 2, 0:T], J[i], cat(J[i], 2, T))

                to_features(J_XT)
                for t in range(2):
                    ps = filled(se, at(L, J_C[t]))
                    act(junk[:, 0:C_Q], ps[:, 0:C_Q], ACT.Square, accum_out=ss[:, 7, t:t + 1])
                    last = act(junk[:, C_Q:C_Q + C_KV], ps[:, C_Q:C_Q + C_KV], ACT.Square, accum_out=ss[:, 7, 2 + t:3 + t])
                    se.drain()
                se.drain().then_inc(c_squares_ready, 1)
                evac(SBQT, J_SBQK[0], cat(J_SBQK[0], 2, T))
                for t in range(2):
                    filled(se, at(L, J_VTOK[t]))
                    ps = PS[J_VTOK[t][0]]
                    act(SBV[:, t, :], ps[:, 0:256], ACT.Copy)
                    act(SWV[:, t, :], ps[:, 256:384], ACT.Copy).then_inc(*free(J_VTOK[t]))
                for i in range(2):
                    evac(SWQT[:, 2 * i:2 * i + 2, :], J_SWQ[i], cat(J_SWQ[i], 2, T))
                evac(DFV, J_DFV[0], cat(J_DFV[0], 2, T))
                evac(DFQT, J_DFQK[0], cat(J_DFQK[0], 2, T))
                for i in range(2):
                    evac(MQT[0:MLA_DIM, 2 * i:2 * i + 2, :], J_MQT[i], cat(J_MQT[i], 2, T)[0:MLA_DIM])
                for i in range(2):
                    evac(MKT[0:MLA_DIM, 2 * i:2 * i + 2, :], J_MKT[i], cat(J_MKT[i], 2, T)[0:MLA_DIM])

                def gate(i):
                    job = at(L, J_G2[i])
                    ps = filled(se, job)
                    for a in range(2):
                        last = act(SG[:, 2 * i + a, :], ps[:, a * T:(a + 1) * T], ACT.Tanh, scale=0.5,
                                   bias=HBIAS[:, 2 * i + a:2 * i + a + 1])
                    last.then_inc(*free(job))

                for h in range(4):
                    ps = filled(se, at(L, J_SBZ[h]))
                    act(SB_E[:, 2 * h:2 * h + 2, :], cat(J_SBZ[h], 2, T), ACT.Abs, scale=HD ** -0.5)
                se.drain()
                act(SB_E, SB_E, ACT.Exp, scale=-1.0)
                se.drain()
                act(SB_E, SB_E, ACT.Ln, bias=1.0).then_inc(sb_log_ready, 1)
                for i in range(4):
                    gate(i)
                se.wait_ge(sb_a_ready, L + 1)
                act(SB_E, SB_E, ACT.Exp).then_inc(sb_exp_ready, 1)
                for i in range(4, 6):
                    gate(i)

                def exps(n):
                    kind, b = SOFT[n]
                    maps = MAPS[kind]
                    se.wait_ge(neg2_ready, L * 6 + n + 1)
                    if kind == "sw":
                        act(sinkx2[:, n % 2, :], sinkx2[:, n % 2, :], ACT.Exp)
                    for h in range(maps):
                        act(PB[n % 2][:, h, :], PB[n % 2][:, h, :], ACT.Exp, scale=SCALE[kind],
                            bias=neg2[:, n % 2, h:h + 1], accum_out=den2[:, n % 2, h:h + 1]).then_inc(probs2_ready, 1)

                def outputs(n):
                    kind, b = SOFT[n]
                    for i in range(0, OUT_HEADS[kind] // 2, 2):
                        pair = probs_before(n) + i
                        if pair >= 2:
                            se.wait_ge(pv2_done, L * N_PAIRS + pair - 1)
                        evac(tmp[:, 0, :], J_PB[n][i])
                    tiles = OUT_HEADS[kind] // 2
                    dst = OTS[BRANCH[kind]][:, :, b * P:b * P + P]
                    src = PS[J_OX[n][0]][:, 0:tiles * P].rearrange("p (a n) -> p a n", a=tiles)
                    if kind == "df":
                        evac(dst, J_OX[n], src, ACT.Copy, scale=SUBG)
                    else:
                        evac(dst, J_OX[n], src)

                evac(OTS[1], J_SBX[0], cat(J_SBX[0], 2, T))
                exps(0)
                for n in range(6):
                    if n < 5:
                        gate(6 + 2 * n)
                        gate(7 + 2 * n)
                    outputs(n)
                    if n < 5:
                        exps(n + 1)

                def moments(i):
                    se.wait_ge(r_ready, L * 2 + i + 1)
                    for t in range(2):
                        last = act(SQ[:, 4 * t:4 * t + 4, :], X[:, t, :].rearrange("p (a n) -> p a n", a=4), ACT.Copy,
                                   accum_out=ss[:, 8, t:t + 1])
                    last.then_inc(sum_ready, 1)
                    se.wait_ge(mean_ready, L * 2 + i + 1)
                    for t in range(2):
                        last = act(SQ[:, 4 * t:4 * t + 4, :], X[:, t, :].rearrange("p (a n) -> p a n", a=4), ACT.Square,
                                   bias=rs[:, 8, t:t + 1], accum_out=ss[:, 9, t:t + 1])
                    last.then_inc(square_ready, 1)

                moments(0)
                to_features(J_XT2)
                filled(se, at(L, J_ROUTE[0]))
                act(ROUTE, PS[J_ROUTE[0][0]][:, 0:64], ACT.Exp, scale=-1.0).then_inc(*free(J_ROUTE[0]))

                def round_half(p, i, h):
                    u, turns = unit_in(p, i)
                    if h == 0:
                        se.wait_ge(slot_loaded[u % 4], L * LAYER_DMAS[u % 4] + turns * (16 * units.dmas[u]) + units.loaded(u))
                    se.wait_ge(half_free[h], L * (HALVES // 2) + p * PER_GROUP + (i + 1))
                    act(W_PARTS[:, h, 0, :, :], half_of(u, h), ACT.Copy).then_inc(half_rounded, 1)

                def gather(p, side, first=False):
                    for half in range(2):
                        job = j_gather(p, half, first)
                        filled(se, at(L, job))
                        act(TOKEN_PARTS[:, side, 0, 4 * half:4 * half + 4, :], cat(job, 4, P), ACT.Copy).then_inc(tokens_rounded, 1)
                    filled(se, at(L, j_slots(p)))
                    act(PLACE_T[:, side, :], PS[3][:, 0:T], ACT.Copy)
                    act(GATES[:, side, :], PS[3][:, T:T + PER_GROUP], ACT.Copy).then_inc(*free(j_slots(p)))

                def turn(p, i):
                    evac(HIDT[:, i % 2, :], j_turn(p, i), PS[2][:, 0:T])

                def experts(p, side, first=False, last=False):
                    for i in range(PER_GROUP):
                        more = not (last and i == PER_GROUP - 1)
                        if i:
                            turn(p, i - 1)
                        elif not first:
                            turn(p - 1, PER_GROUP - 1)
                        if more:
                            round_half(*next_expert(p, i), 0)
                        ps = filled(se, at(L, j_hidden(p, i)))
                        act(th[:, i % 2, 0:T], ps[:, 0:T], ACT.Tanh, scale=0.5).then_inc(moe_th_ready, 1)
                        if more:
                            round_half(*next_expert(p, i), 1)
                        if i == 0 and not first:
                            down(p - 1)
                        if i == 2 and not last:
                            gather(p + 1, 1 - side)

                def down(p):
                    for half in range(2):
                        job = j_down(p, half)
                        ps = filled(se, at(L, job))
                        act(DOWN_PARTS[:, 0, half * BANK:half * BANK + BANK], ps[:, :], ACT.Copy).then_inc(down_rounded, 1)

                for t in range(2):
                    last = act(X_PARTS[:, 0, t, :], X[:, t, :], ACT.Copy)
                last.then_inc(x_rounded, 1)
                round_half(0, 0, 0)
                round_half(0, 0, 1)
                gather(0, 0, True)
                experts(0, 0, first=True)
                with se.Fori(0, (PASSES - 3) // 2) as g:
                    experts(g * 2 + 1, 1)
                    experts(g * 2 + 2, 0)
                experts(PASSES - 2, 1)
                experts(PASSES - 1, 0, last=True)
                turn(PASSES - 1, PER_GROUP - 1)
                down(PASSES - 1)
                moments(1)

        @block.gpsimd
        def _(po):
            po.memset(neghalf[:, :], -0.5)
            po.memset(inv_width[:, 0:2], 1.0 / C_Q)
            po.memset(inv_width[:, 2:4], 1.0 / C_KV)
            po.memset(inv_width[:, 4:8], 1.0 / HD)
            po.memset(neg_inv_d[:, :], -1.0 / D)
            po.drain()

            def rstd(ev, n, width, halves):
                po.wait_ge(sumsq_ready, ev + 1)
                if halves:
                    po.tensor_tensor(ss[:, ev, 0:n], ss[:, ev, 0:n], ss[:, ev, n:2 * n], ALU.add)
                    po.drain()
                po.tensor_scalar(ss[:, ev, 0:n], ss[:, ev, 0:n], 1.0 / width, EPS, ALU.mult, ALU.add)
                po.drain()
                po.tensor_tensor(rs[:, ev, 0:n], ss[:, ev, 0:n], neghalf[:, 0:n], ALU.pow).then_inc(rstd_ready, 1)

            rstd(0, 4, D, False)
            rstd(1, 4, D, True)
            rstd(2, 4, D, False)
            for d in range(2):
                for li in range(len(LEVELS)):
                    n = d * len(LEVELS) + li
                    po.wait_ge(decay_ready, n + 1)
                    if li:
                        filled(po, J_LEV[d][li - 1][1])
                    po.tensor_tensor(QLEV, HQ, EB, ALU.mult).then_inc(qlev_ready, 1)
                    if 1 <= li <= 4:
                        i = d * 4 + li - 1
                        sg = (SGA, SGH)[i // 4][:, 2 * (i % 4):2 * (i % 4) + 2, :]
                        emptied(po, J_GATE[i])
                        po.tensor_scalar(sg, sg, 0.5, 0.5, ALU.mult, ALU.add).then_inc(gate_ready, 1)
            rstd(3, 2, 4 * P, False)
            rstd(4, 2, D, True)
            rstd(5, 2, D, False)
            rstd(6, 2, D, True)
            with po.Fori(0, LAYERS) as L:
                po.wait_ge(c_squares_ready, L + 1)
                po.tensor_tensor(row_rs[:, 0, :], ss[:, 7, 0:4], inv_width[:, 0:4], ALU.mult)
                po.drain()
                po.tensor_scalar(row_rs[:, 0, :], row_rs[:, 0, :], 1.0, EPS, ALU.mult, ALU.add)
                po.drain()
                po.tensor_tensor(row_rs[:, 1, :], row_rs[:, 0, :], neghalf[:, 0:4], ALU.pow).then_inc(c_rstd_ready, 1)
                for b in range(2):
                    po.wait_ge(df_squares_ready, L * 2 + b + 1)
                    po.tensor_tensor(row_rs[:, 0, :], row_sum[:, b, :], inv_width[:, 4:8], ALU.mult)
                    po.drain()
                    po.tensor_scalar(row_rs[:, 0, :], row_rs[:, 0, :], 1.0, EPS, ALU.mult, ALU.add)
                    po.drain()
                    po.tensor_tensor(row_rs[:, 2 + b, :], row_rs[:, 0, :], neghalf[:, 0:4], ALU.pow).then_inc(df_rstd_ready, 1)
                for i in range(2):
                    po.wait_ge(sum_ready, L * 2 + i + 1)
                    po.tensor_tensor(rs[:, 8, 0:2], ss[:, 8, 0:2], neg_inv_d[:, 0:2], ALU.mult).then_inc(mean_ready, 1)
                    po.wait_ge(square_ready, L * 2 + i + 1)
                    po.tensor_tensor(ss[:, 9, 0:2], ss[:, 9, 0:2], neg_inv_d[:, 0:2], ALU.mult)
                    po.drain()
                    po.tensor_scalar(ss[:, 9, 0:2], ss[:, 9, 0:2], -1.0, LN_EPS, ALU.mult, ALU.add)
                    po.drain()
                    po.tensor_tensor(rs[:, 9, 0:2], ss[:, 9, 0:2], neghalf[:, 0:2], ALU.pow).then_inc(ln_rstd_ready, 1)

        @block.vector
        def _(ve):
            ve.wait_ge(cols_loaded, 16)
            c_kw = cols[:, 0:16].rearrange("p (w k) -> p k w", w=2)
            ve.wait_ge(c_tanh_ready, 1)
            stt(sc[:, :, :], sc[:, :, :], 1.0, c_kw, ALU.add, ALU.mult)
            nc.vector.memset(SC, 0.0)
            ve.drain()
            ts(SC[:, :, 0:2], sc[:, :, :], 0.5, None, ALU.mult).then_inc(silu_c_ready, 1)
            for d, (a, b) in enumerate((("lb_f0", "lb_f1"), ("lb_b0", "lb_b1"))):
                tt(lbt[:, 2, 4 * d:4 * d + 4], col(a, 0, 4), col(b, 0, 4), ALU.max)
            ve.drain()
            for d, names in enumerate((("lb_f0", "lb_f1"), ("lb_b0", "lb_b1"))):
                for r in range(2):
                    last = tt(lbt[:, r, 4 * d:4 * d + 4], col(names[r], 0, 4), lbt[:, 2, 4 * d:4 * d + 4], ALU.subtract)
            last.then_inc(lb_max_ready, 1)
            ve.wait_ge(lb_exp_ready, 1)
            tt(lbt[:, 2, :], lbt[:, 0, :], lbt[:, 1, :], ALU.add)
            ve.drain()
            nc.vector.reciprocal(lbt[:, 2, :], lbt[:, 2, :])
            ve.drain()
            for d in range(2):
                tt(lbs[:, d, 0, :], lbt[:, 0, 4 * d:4 * d + 4], lbt[:, 2, 4 * d:4 * d + 4], ALU.mult)
            ve.drain()
            for d in range(2):
                ts(lbs[:, d, 1, :], lbs[:, d, 0, :], -1.0, 1.0, ALU.mult, ALU.add)

            ve.wait_ge(consts_loaded, 16 * N_CONSTS)
            copy(pair_mask[:, :, :], MASK_F)
            nc.vector.memset(ones[:, :], 1.0)
            def ada_rows(u):
                ps = filled(ve, J_ADA[u][0])
                copy(tmp[:, u % 2, :], ps[:, :]).then_inc(*free(J_ADA[u][0]))

            def ada_result(u):
                j, half = u // 2, u % 2
                if j % 3 != 2:
                    job = J_ADA[u][1]
                    ps = filled(ve, job)
                    bias = col("b_ada", 4 * u, 4).rearrange("p (k o) -> p k o", o=1).to_broadcast([P, 4, 2])
                    tt(mod[:, j, 4 * half:4 * half + 4, :], ps[:, 0:8].rearrange("p (k w) -> p k w", w=2),
                       bias, ALU.add).then_inc(*free(job))
                else:
                    for w, job in enumerate(J_ADA[u][1:]):
                        g = w if j == 2 else j // 3 + 1
                        ps = filled(ve, job)
                        part = G[:, g, half * BANK:half * BANK + BANK]
                        tt(part, part, ps[:, :], ALU.add).then_inc(*free(job))

            def ada(group):
                for n, u in enumerate(group):
                    ada_rows(u)
                    if n:
                        ada_result(group[n - 1])
                ada_result(group[-1])
                ve.drain()

            def norm_gain(n):
                pre = col("norm_pre", 8 * n, 8).rearrange("p (k o) -> p k o", o=1).to_broadcast([P, KD, 2])
                return stt(gain[:, n, :, :], mod[:, 3 * n + 1, :, :], 1.0, pre, ALU.add, ALU.mult)

            ada(list(range(ADA_FIRST)))
            norm_gain(0).then_inc(gain_ready, 1)

            def normalise(ev, tiles):
                ve.wait_ge(rstd_ready, ev + 1)
                for t in range(tiles):
                    last = ts(XN[:, t, :], X[:, t, :], rs[:, ev, t:t + 1], None, ALU.mult)
                last.then_inc(xn_ready, 1)

            def transposed(n, tiles, J):
                for k in range(0, KD, 2):
                    ps = filled(ve, J[k])
                    for w in range(tiles // 2):
                        last = ts(HT[:, k, w * T:(w + 1) * T], ps[:, w * T:(w + 1) * T],
                                  gain[:, n, k, w:w + 1], mod[:, 3 * n, k, w:w + 1], ALU.mult, ALU.add)
                    last.then_inc(*free(J[k]))

            def ffn_in(J, width, before):
                def body(i, r, g):
                    for j in range(2):
                        gate, up = J(i, 2 * j), J(i, 2 * j + 1)
                        ve.wait_ge(th_ready, i * 2 + (before + j + 1))
                        stt(tmp[:, j, 0:width], th[:, j, 0:width], 1.0, PS[gate[0]][:, 0:width],
                            ALU.add, ALU.mult).then_inc(*free(gate))
                        ve.drain()
                        ps = filled(ve, up)
                        stt(HID[:, i * 2 + j, 0:width], tmp[:, j, 0:width], 0.5, ps[:, 0:width],
                            ALU.mult, ALU.mult).then_inc(*free(up))
                repeat(ve, 11, body)

            def post(ev, tiles, J, gains, buf):
                ve.wait_ge(rstd_ready, ev + 1)
                for half in range(2):
                    cut = slice(half * BANK, half * BANK + BANK)
                    for t in range(tiles):
                        job = J[half * tiles + t]
                        ps = filled(ve, job)
                        stt(buf[:, t, cut], ps[:, :], rs[:, ev, t:t + 1], G[:, gains[t], cut],
                            ALU.mult, ALU.mult).then_inc(*free(job))
                ve.drain()
                tt(X[:, 0:tiles, :], X[:, 0:tiles, :], buf[:, 0:tiles, :], ALU.add).then_inc(x_ready, 1)

            normalise(0, 4)
            transposed(0, 4, J_N1)
            ffn_in(J_FF1A, 2 * T, 0)
            for group in ADA_AFTER[:3]:
                ada(group)
            for n in (1, 2):
                norm_gain(n)
            for g, (n, w) in enumerate(((0, 0.5), (0, 0.5), (1, 1.0), (2, 0.5))):
                stt(G[:, g, :], G[:, g, :], w, NORM_POST[:, n, :], ALU.mult, ALU.mult)
            ve.drain()
            post(1, 4, J_FF1B, (0, 0, 1, 1), XN)

            ve.drain()
            normalise(2, 4)
            transposed(1, 4, J_N2)

            for i in range(2):
                ve.wait_ge(gate_tanh_ready, i + 1)
                ps = PS[J_HQ[i][0]]
                stt(tmp[:, i, :], th[:, i, :], 1.0, ps[:, :], ALU.add, ALU.mult).then_inc(*free(J_HQ[i]))
                ve.drain()
                last = ts(HQ[:, 2 * i:2 * i + 2, :], tmp[:, i, :].rearrange("p (a n) -> p a n", a=2), 0.5, None, ALU.mult)
            last.then_inc(silu_ready, 1)

            def rope(dst, src, table, heads):
                v = src.rearrange("p h (r a n) -> p h r a n", r=2, a=2)
                w = dst.rearrange("p h (r a n) -> p h r a n", r=2, a=2)
                c = table[:, 0, :].rearrange("p (o r n) -> p o r n", o=1, r=2).to_broadcast([P, heads, 2, 16])
                s = table[:, 1, :].rearrange("p (o r n) -> p o r n", o=1, r=2).to_broadcast([P, heads, 2, 16])
                t = [ROPE_T[:, i, 0:heads * 32].rearrange("p (h r n) -> p h r n", h=heads, r=2) for i in range(4)]
                tt(t[0], v[:, :, :, 0, :], c, ALU.mult)
                tt(t[1], v[:, :, :, 1, :], s, ALU.mult)
                tt(t[2], v[:, :, :, 0, :], s, ALU.mult)
                last = tt(t[3], v[:, :, :, 1, :], c, ALU.mult)
                ve.drain()
                tt(w[:, :, :, 0, :], t[0], t[1], ALU.subtract)
                tt(w[:, :, :, 1, :], t[2], t[3], ALU.add)
                ve.drain()

            def forget(d):
                for h in range(HG_HEADS):
                    emptied(ve, J_HF[d][h])
                    ts(KK[:, h, :], KK[:, h, :], 1.0, None, ALU.add)
                    ve.drain()
                    nc.vector.reciprocal(KK[:, h, :], KK[:, h, :])
                    ve.drain()
                    last = ts(KK[:, h, :], KK[:, h, :], lbs[:, d, 1, h:h + 1], lbs[:, d, 0, h:h + 1], ALU.mult, ALU.add)
                last.then_inc(f_ready, 1)

            def cumulate(d):
                ve.wait_ge(lf_ready, d + 1)
                ts(KK, KK, -1.0, 1.0, ALU.mult, ALU.add)
                for h in range(HG_HEADS):
                    nc.vector.tensor_tensor_scan(BB[:, h, :], reset[:, :], BB[:, h, :], 0.0, ALU.mult, ALU.add)
                ve.drain()
                tiles = BB.rearrange("p h (t n) -> p h t n", n=P)
                last = copy(tot[:, d, :, :], tiles[:, :, :, P - 1])
                if d:
                    nc.vector.memset(SHIFT[:, :, :, 0:1], 0.0)
                    for h in range(HG_HEADS):
                        copy(SHIFT[:, h, :, 1:P], tiles[:, h, :, 0:P - 1])
                    ve.drain()
                    last = copy(tiles, SHIFT)
                last.then_inc(cum_ready, 1)

            def states(d):
                for i, tile in enumerate(TILES[d]):
                    n = d * 3 + i
                    ve.wait_ge(kexp_ready, n + 1)
                    tt(KDEC, KDEC, KK[:, :, tile * P:tile * P + P], ALU.mult).then_inc(kdec_ready, 1)
                    job = J_KV[d][i]
                    filled(ve, job)
                    ps = cat(job, 4, P)
                    src, dst = STATE[:, 2 * d, :, :], STATE[:, 2 * d + (i == 2), :, :]
                    if i == 0:
                        dst = STATE[:, 2 * d:2 * d + 1, :, :]
                        copy(STATE[:, 2 * d, :, :], ps).then_inc(*free(job))
                    else:
                        ve.drain()
                        for h in range(HG_HEADS):
                            last = stt(dst[:, h, :], src[:, h, :], dec[:, d, h, tile:tile + 1], ps[:, h, :],
                                       ALU.mult, ALU.add)
                        last.then_inc(*free(job))

            def levels(d):
                ve.wait_ge(qexp_ready, d + 1)
                tt(QDEC[:, 4 * d:4 * d + 4, :], HQ, EB, ALU.mult).then_inc(qdec_ready, 1)

                def pick(li):
                    for tile in range(2):
                        job = J_LEV[d][li][tile]
                        filled(ve, job)
                        which = d * len(LEVELS) + li
                        nc.vector.copy_predicated(SCORE[:, tile, :, :],
                                                  pair_mask[:, which:which + 1, :].to_broadcast([P, 4, P]),
                                                  cat(job, 4, P)).then_inc(*free(job))

                for li, m in enumerate(LEVELS):
                    n = d * len(LEVELS) + li
                    ve.drain()
                    if n:
                        ve.wait_ge(qlev_ready, n)
                    for h in range(HG_HEADS):
                        b = BB[:, h, 0:T].rearrange("p (k n) -> p k n", n=2 * m)
                        e = EB[:, h, :].rearrange("p (k n) -> p k n", n=2 * m)
                        mid = b[:, :, m - 1:m].to_broadcast([P, T // (2 * m), 2 * m])
                        last = tt(e, b, mid, ALU.subtract)
                    last.then_inc(gap_ready, 1)
                    if li:
                        pick(li - 1)
                    ve.wait_ge(decay_ready, n + 1)
                    tt(KLEV, KK[:, :, 0:T], EB, ALU.mult).then_inc(klev_ready, 1)
                pick(len(LEVELS) - 1)
                ve.drain()
                for tile in range(2):
                    job = J_DIAG[d][tile]
                    filled(ve, job)
                    diag = pair_mask[:, 2 * len(LEVELS):, :].to_broadcast([P, 4, P])
                    if d == 0:
                        last = nc.vector.copy_predicated(SCORE[:, tile, :, :], diag, cat(job, 4, P))
                        last.then_inc(*free(job))
                    else:
                        e = EB[:, :, tile * P:tile * P + P]
                        tt(e, SCORE[:, tile, :, :], cat(job, 4, P), ALU.add)
                        ve.drain()
                        nc.vector.copy_predicated(SCORE[:, tile, :, :], diag, e).then_inc(*free(job))

            nc.vector.memset(SCORE, 0.0)
            forget(0)
            for i in range(2):
                job = J_AK[i]
                filled(ve, job)
                v = cat(job, 2, 256)
                for t in range(2):
                    k = v[:, t, 0:P].rearrange("p (h n) -> p h n", h=2)
                    dup = KTOK[:, 2 * i + t, :, :].rearrange("p (g c) n -> p g c n", c=2)
                    if i == 0:
                        rope(dup[:, :, 0, :], k, rope1[:, t, :, :], 2)
                        copy(dup[:, :, 1, :], dup[:, :, 0, :])
                    else:
                        copy(dup[:, :, 0, :], k)
                        copy(dup[:, :, 1, :], k)
                    last = copy(VTOK[:, 2 * i + t, :], v[:, t, P:2 * P])
                last.then_inc(*free(job))
            for t in range(2):
                filled(ve, J_AQ[t])
                rope(QTOK[:, t, :, :], cat(J_AQ[t], 8, HD), rope1[:, t, :, :], 8)
                ve.drain().then_inc(*free(J_AQ[t]))
            cumulate(0)
            for i in range(2):
                ve.wait_ge(gate_tanh_ready, 3 + i)
                ps = PS[J_HG[i][0]]
                stt(tmp[:, i, :], th[:, i, :], 1.0, ps[:, :], ALU.add, ALU.mult).then_inc(*free(J_HG[i]))
                ve.drain()
                for a in range(2):
                    ts(HGT[:, 2 * i + a, :], tmp[:, i, a * T:(a + 1) * T], col("hgrn_norm", 2 * i + a), 0.5, ALU.mult, ALU.mult)
            states(0)
            levels(0)
            forget(1)
            cumulate(1)
            states(1)
            levels(1)
            ve.drain().then_inc(state_ready, 1)
            ve.wait_ge(rstd_ready, 4)
            for t in range(2):
                ts(ONT[:, t, :], PS[J_O[t][0]][:, :], rs[:, 3, t:t + 1], None, ALU.mult).then_inc(*free(J_O[t]))
            for t in range(2):
                filled(ve, J_ORT[t])
                tt(ORT[:, :, t * P:t * P + P], cat(J_ORT[t], 4, P), HGT[:, :, t * P:t * P + P],
                   ALU.mult).then_inc(*free(J_ORT[t]))

            for g in range(2):
                ps = filled(ve, J_KZ[g])
                for half in range(2):
                    last = ts(KZ[:, 2 * g + half, :], ps[:, :], col("halves", half), None, ALU.mult)
                last.then_inc(*free(J_KZ[g]))
            for b in range(2):
                if b:
                    filled(ve, J_PT[0][HEADS - 1])
                for h in range(HEADS):
                    ps = filled(ve, J_S[b][h])
                    nc.vector.tensor_tensor_reduce(out=PROB[:, h, :], in0=ps[:, :], in1=window[:, b, :], scale=1.0,
                                                   scalar=-3e38, op0=ALU.add, op1=ALU.max,
                                                   accum_out=mx[:, b * 8 + h:b * 8 + h + 1]).then_inc(*free(J_S[b][h]))
                cut = slice(b * 8, b * 8 + 8)
                ve.drain()
                stt(negmx[:, cut], mx[:, cut], HD ** -0.5, sink1[:, :], ALU.mult, ALU.max)
                ve.drain()
                tt(sinkx[:, cut], sink1[:, :], negmx[:, cut], ALU.subtract)
                ve.drain()
                ts(negmx[:, cut], negmx[:, cut], -1.0, None, ALU.mult).then_inc(negmax_ready, 1)
                ve.wait_ge(probs_ready, 8 * (b + 1))
                tt(den[:, cut], den[:, cut], sinkx[:, cut], ALU.add)
                ve.drain()
                nc.vector.reciprocal(den[:, cut], den[:, cut])
                for h in range(1, HEADS, 2):
                    ps = filled(ve, J_PT[b][h])
                    if h >= 3:
                        ve.wait_ge(pv_done, b * 7 + h - 1)
                    copy(PT[:, 1, :], ps[:, :]).then_inc(*free(J_PT[b][h]))
                filled(ve, J_PV[b])
                ve.drain()
                tt(OTOK[:, b, :].rearrange("p (h n) -> p h n", h=HEADS), cat(J_PV[b], HEADS, HD),
                   den[:, cut].rearrange("p (h o) -> p h o", o=1).to_broadcast([P, HEADS, HD]),
                   ALU.mult).then_inc(*free(J_PV[b]))

            ve.wait_ge(gate_ready, 8)
            for i in range(4):
                filled(ve, J_WOA[i])
                tt(MERGED[:, 2 * i:2 * i + 2, :], cat(J_WOA[i], 2, T), SGA[:, 2 * i:2 * i + 2, :],
                   ALU.mult).then_inc(*free(J_WOA[i]))
            for i in range(4):
                filled(ve, J_WOH[i])
                part = tmp[:, i % 2, :].rearrange("p (a n) -> p a n", a=2)
                tt(part, cat(J_WOH[i], 2, T), SGH[:, 2 * i:2 * i + 2, :], ALU.mult).then_inc(*free(J_WOH[i]))
                ve.drain()
                last = tt(MERGED[:, 2 * i:2 * i + 2, :], MERGED[:, 2 * i:2 * i + 2, :], part, ALU.add)
            last.then_inc(merged_ready, 1)
            post(4, 2, J_WOUT, (2, 2), YT2)

            ve.drain()
            normalise(5, 2)
            transposed(2, 2, J_N3)
            ffn_in(J_FF2A, T, 22)
            post(6, 2, J_FF2B, (3, 3), XN)
            copy(pos[:, :], pos_i[:, :])
            ve.wait_ge(consts2_loaded, 16 * 8)
            copy(POS_ROW, POS_ROW_I)
            ve.drain()
            for t in range(2):
                ts(POS_ROW_GAP[:, t, :], POS_ROW, pos[:, t:t + 1], None, ALU.subtract)
            ve.drain()
            tt(slide_gap, slide_gap, POS_ROW_GAP, ALU.add)
            tt(causal_gap, causal, POS_ROW_GAP, ALU.add)
            for i in range(2):
                tt(LAMS[:, 2 * i, :, :], LAMS[:, 2 * i, :, :], LAMS[:, 2 * i + 1, :, :], ALU.mult)
            for t in range(2):
                for a in range(2):
                    ts(angle[:, t, a, :], inv_freq[:, :], pos[:, t:t + 1], None, ALU.mult)
            ve.drain()
            for i in range(2):
                last = nc.vector.reduce_sum(lam_sum[:, i, :], LAMS[:, 2 * i, :, :], X_AXIS)
            last.then_inc(lam_ready, 1)
            for a, quarter in ((0, 0.25), (1, 0.0)):
                ts(turns[:, :, a, :], angle[:, :, a, :], float(1 / (2 * np.pi)), quarter, ALU.mult, ALU.add)
            ve.drain()
            ts(turns[:, :, :, :], turns[:, :, :, :], ROUND, -ROUND, ALU.add, ALU.add)
            for part in TWO_PI_PARTS:
                ve.drain()
                stt(angle[:, :, :, :], turns[:, :, :, :], -part, angle[:, :, :, :], ALU.mult, ALU.add)
            ve.drain()
            ts(angle[:, :, 0, :], angle[:, :, 0, :], float(np.pi / 2), None, ALU.add)
            ve.drain()
            ts(angle[:, :, :, :], angle[:, :, :, :], 3.1415925, -3.1415925, ALU.min, ALU.max).then_inc(angle_ready, 1)
            ve.wait_ge(lam_exp_ready, 1)
            tt(neg_lam[:, :], lam_sum[:, 1, :], lam_sum[:, 0, :], ALU.subtract)
            ve.drain()
            ts(lam_sum[:, 0, :], lam_init[:, :], -1.0, 1.0, ALU.mult, ALU.add)
            ve.drain()
            tt(neg_lam[:, :], neg_lam[:, :], lam_init[:, :], ALU.subtract)
            for l in range(LAYERS):
                tt(sub_gain[:, l:l + 1], lam_sum[:, 0, l:l + 1], col("layers", l * PER_LAYER_COLS + 35), ALU.mult)
                ts(half_bias[:, l, :], col("layers", l * PER_LAYER_COLS, 32), 0.5, None, ALU.mult)
            ve.wait_ge(rope2_ready, 1)
            copy(turns[:, 0, 0, 0:1], rope2[:, 0, 0, 0:1])
            with ve.Fori(0, LAYERS) as L:
                ve.drain().then_inc(layer_start, 1)
                copy(LCOLS, cols[:, bass.ds(L * PER_LAYER_COLS + COLS["layers"][0], PER_LAYER_COLS)])
                copy(HBIAS, half_bias[:, bass.ds(L, 1), :])
                copy(SINK2, sink2[:, bass.ds(L, 1), :])
                copy(SUBG, sub_gain[:, bass.ds(L, 1)])
                copy(NEG_LAM, neg_lam[:, bass.ds(L, 1)])
                ve.drain().then_inc(mtok_ready, 1)

                def full_at(job):
                    return filled(ve, at(L, job))

                ve.wait_ge(c_rstd_ready, L + 1)
                for t in range(2):
                    ps = PS[J_C[t][0]]
                    ts(CTOK[:, t, 0:C_Q], ps[:, 0:C_Q], row_rs[:, 1, t:t + 1], None, ALU.mult)
                    ts(CTOK[:, t, C_Q:C_Q + C_KV], ps[:, C_Q:C_Q + C_KV], row_rs[:, 1, 2 + t:3 + t], None, ALU.mult)
                    copy(CTOK[:, t, C_Q + C_KV:], ps[:, C_Q + C_KV:C_Q + C_KV + C_ROPE]).then_inc(*free(J_C[t]))
                ve.drain()

                def rotate(dst, src, t, heads):
                    c = rope2[:, t, 0:1, :].to_broadcast([P, heads, 16])
                    s = rope2[:, t, 1:2, :].to_broadcast([P, heads, 16])
                    a, b = src[:, :, 0:16], src[:, :, 16:32]
                    r = [ROT[:, i, 0:heads * 16].rearrange("p (h n) -> p h n", h=heads) for i in range(4)]
                    tt(r[0], a, c, ALU.mult)
                    tt(r[1], b, s, ALU.mult)
                    tt(r[2], a, s, ALU.mult)
                    tt(r[3], b, c, ALU.mult)
                    ve.drain()
                    tt(dst[:, :, 0:16], r[0], r[1], ALU.subtract)
                    tt(dst[:, :, 16:32], r[2], r[3], ALU.add)
                    ve.drain()

                for t in range(2):
                    rotate(MKTOK[:, t, 0:1, HD:], CTOK[:, t:t + 1, C_Q + C_KV:], t, 1)
                    for h in range(1, MLA_HEADS):
                        copy(MKTOK[:, t, h, HD:], MKTOK[:, t, 0, HD:])
                ps = full_at(J_CT[0])
                for f in range(2):
                    last = ts(CT[:, f, :], ps[:, f * T:(f + 1) * T], LCOLS[:, 32 + f:33 + f], None, ALU.mult)
                last.then_inc(*free(J_CT[0]))
                ps = full_at(J_CT[1])
                ts(CT[:, 2, :], ps[:, 0:T], LCOLS[:, 34:35], None, ALU.mult).then_inc(*free(J_CT[1]))
                ps = full_at(J_SBQK[1])
                for h in range(4):
                    last = ts(SBKZ[:, h, :], ps[:, h // 2 * T:(h // 2 + 1) * T], col("halves", h % 2), None, ALU.mult)
                last.then_inc(*free(J_SBQK[1]))
                for t in range(2):
                    full_at(J_MQ[t])
                    q = PS[J_MQ[t][0]][:, 0:MLA_HEADS * MLA_DIM].rearrange("p (h n) -> p h n", h=MLA_HEADS)
                    copy(MQTOK[:, t, :, 0:HD], q[:, :, 0:HD])
                    rotate(MQTOK[:, t, :, HD:], q[:, :, HD:], t, MLA_HEADS)
                    ve.drain().then_inc(*free(J_MQ[t]))
                for t in range(2):
                    full_at(J_MKV[t])
                    kv = cat(J_MKV[t], MLA_HEADS, P)
                    copy(MKTOK[:, t, :, 0:HD], kv[:, :, 0:HD])
                    copy(MV[:, t, :, :], kv[:, :, HD:]).then_inc(*free(J_MKV[t]))
                ps = full_at(J_SWK[0])
                for g in range(2):
                    for half in range(2):
                        last = ts(SWKZ[:, 2 * g + half, :], ps[:, g * T:(g + 1) * T], col("halves", half), None, ALU.mult)
                last.then_inc(*free(J_SWK[0]))
                ps = full_at(J_DFQK[1])
                for m in range(8):
                    last = ts(DFKZ[:, m, :], ps[:, m // 4 * T:(m // 4 + 1) * T], col("quarters", m % 4), None, ALU.mult)
                last.then_inc(*free(J_DFQK[1]))

                ve.wait_ge(sb_log_ready, L + 1)
                for h in range(4):
                    e, l = SB_E[:, 2 * h:2 * h + 2, :], SB_L[:, 2 * h:2 * h + 2, :]
                    z = cat(J_SBZ[h], 2, T)
                    ts(l, z, HD ** -0.5, None, ALU.mult).then_inc(*free(J_SBZ[h]))
                    ve.drain()
                    stt(e, l, 0.0, e, ALU.min, ALU.subtract)
                    ve.drain()
                    tt(l, e, l, ALU.subtract)
                    ve.drain()
                    last = tt(l, l, sb_mask, ALU.mult)
                last.then_inc(sb_l_ready, 1)
                for h in range(4):
                    full_at(J_SBS[h])
                    e = SB_E[:, 2 * h:2 * h + 2, :]
                    tt(e, e, cat(J_SBS[h], 2, T), ALU.add).then_inc(*free(J_SBS[h]))
                ve.drain().then_inc(sb_a_ready, 1)
                ve.wait_ge(sb_exp_ready, L + 1)
                for h in range(4):
                    e = SB_E[:, 2 * h:2 * h + 2, :]
                    last = tt(e, e, sb_mask, ALU.mult)
                last.then_inc(sbo_ready, 1)
                full_at(J_SBO[0])
                copy(th[:, 0, :], PS[J_SBO[0][0]][:, :]).then_inc(*free(J_SBO[0]))

                def scores(n):
                    kind, b = SOFT[n]
                    buf, side = PB[n % 2], n % 2
                    if n == 1:
                        full_at(J_SBS[3])
                    elif n >= 2:
                        full_at(J_PB[n - 2][-1])
                    for i, job in enumerate(J_SM[n]):
                        full_at(job)
                        ps = cat(job, 2, T)
                        if kind == "mla":
                            tt(buf[:, 2 * i:2 * i + 2, :], ps, causal[:, b:b + 1, :].to_broadcast([P, 2, T]),
                               ALU.add).then_inc(*free(job))
                        else:
                            for a in range(2):
                                m = 2 * i + a
                                slope = 2.0 ** -(m + 1) if kind == "sw" else 2.0 ** (-2.0 * (m // 2 + 1))
                                gap = (slide_gap if kind == "sw" else causal_gap)[:, b, :]
                                last = stt(buf[:, m, :], gap, slope / SCALE[kind], ps[:, a, :], ALU.mult, ALU.add)
                            last.then_inc(*free(job))
                    ve.drain()
                    m = MAPS[kind]
                    nc.vector.reduce_max(mx2[:, side, 0:m], buf[:, 0:m, :], X_AXIS)
                    ve.drain()
                    if kind == "sw":
                        stt(mx2[:, side, :], mx2[:, side, :], SCALE[kind], SINK2, ALU.mult, ALU.max)
                        ve.drain()
                        tt(sinkx2[:, side, :], SINK2, mx2[:, side, :], ALU.subtract)
                        ts(neg2[:, side, :], mx2[:, side, :], -1.0, None, ALU.mult)
                    else:
                        ts(neg2[:, side, 0:m], mx2[:, side, 0:m], -SCALE[kind], None, ALU.mult)
                    ve.drain().then_inc(neg2_ready, 1)

                def weights(n):
                    kind, b = SOFT[n]
                    side, m = n % 2, MAPS[kind]
                    ve.wait_ge(probs2_ready, L * N_MAPS + maps_before(n) + m)
                    if kind == "sw":
                        tt(den2[:, side, :], den2[:, side, :], sinkx2[:, side, :], ALU.add)
                        ve.drain()
                    nc.vector.reciprocal(den2[:, side, 0:m], den2[:, side, 0:m])
                    ve.drain()
                    if kind == "df":
                        for h in range(4):
                            ts(den2[:, side, 2 * h + 1:2 * h + 2], den2[:, side, 2 * h + 1:2 * h + 2], NEG_LAM, None, ALU.mult)
                            p = PB[side][:, 2 * h, :]
                            ts(p, p, den2[:, side, 2 * h:2 * h + 1], None, ALU.mult)
                        ve.drain()
                        for h in range(4):
                            p = PB[side][:, 2 * h, :]
                            stt(p, PB[side][:, 2 * h + 1, :], den2[:, side, 2 * h + 1:2 * h + 2], p, ALU.mult, ALU.add)
                        ve.drain().then_inc(mixed_ready, 1)

                def outputs(n):
                    kind, b = SOFT[n]
                    side, heads = n % 2, OUT_HEADS[kind]
                    for i in range(1, heads // 2, 2):
                        pair = probs_before(n) + i
                        if pair >= 2:
                            ve.wait_ge(pv2_done, L * N_PAIRS + pair - 1)
                        full_at(J_PB[n][i])
                        copy(tmp[:, 1, :], PS[J_PB[n][i][0]][:, :]).then_inc(*free(J_PB[n][i]))
                    if n:
                        full_at(J_OX[n - 1])
                    else:
                        full_at(J_SBX[0])
                    full_at(J_OV[n])
                    out = PS[J_OV[n][0]][:, 0:heads * HD].rearrange("p (h n) -> p h n", h=heads)
                    o = th[:, 0, 0:heads * HD].rearrange("p (h n) -> p h n", h=heads)
                    if kind != "df":
                        r = den2[:, side, 0:heads].rearrange("p (h o) -> p h o", o=1).to_broadcast([P, heads, HD])
                        tt(o, out, r, ALU.mult).then_inc(*free(J_OV[n]))
                    else:
                        copy(o, out)
                        ve.drain()
                        q = th[:, 1, 0:heads * HD].rearrange("p (h n) -> p h n", h=heads)
                        tt(q, o, o, ALU.mult)
                        ve.drain()
                        nc.vector.reduce_sum(row_sum[:, b, :], q, X_AXIS).then_inc(df_squares_ready, 1)
                        ve.wait_ge(df_rstd_ready, L * 2 + b + 1)
                        r = row_rs[:, 2 + b, :].rearrange("p (h o) -> p h o", o=1).to_broadcast([P, heads, HD])
                        tt(o, o, r, ALU.mult).then_inc(*free(J_OV[n]))

                scores(0)
                weights(0)
                for n in range(6):
                    outputs(n)
                    if n < 5:
                        scores(n + 1)
                        weights(n + 1)

                for i in range(16):
                    ve.wait_ge(bank_free[J_G2[i][0]], at(L, J_G2[i])[1] + 1)
                    sg = SG[:, 2 * i:2 * i + 2, :]
                    ts(sg, sg, 0.5, 0.5, ALU.mult, ALU.add)
                ve.drain()
                for j in range(4):
                    for i in range(4):
                        job = J_BR[j][i]
                        full_at(job)
                        m = MERGED2[:, 2 * i:2 * i + 2, :]
                        sg = SG[:, KD * j + 2 * i:KD * j + 2 * i + 2, :]
                        part = tmp[:, i % 2, :].rearrange("p (a n) -> p a n", a=2)
                        if j == 0:
                            tt(m, cat(job, 2, T), sg, ALU.mult).then_inc(*free(job))
                        else:
                            tt(part, cat(job, 2, T), sg, ALU.mult).then_inc(*free(job))
                            ve.drain()
                            tt(m, m, part, ALU.add)
                ve.drain().then_inc(merged2_ready, 1)

                def residual(J):
                    for half in range(2):
                        cut = slice(half * BANK, half * BANK + BANK)
                        for t in range(2):
                            job = J(half, t)
                            full_at(job)
                            stt(X[:, t, cut], X[:, t, cut], ALPHA, PS[job[0]][:, :], ALU.mult, ALU.add).then_inc(*free(job))

                def layer_norm(i):
                    ve.drain().then_inc(r_ready, 1)
                    ve.wait_ge(ln_rstd_ready, L * 2 + i + 1)
                    for t in range(2):
                        ts(X[:, t, :], X[:, t, :], rs[:, 8, t:t + 1], rs[:, 9, t:t + 1], ALU.add, ALU.mult)
                    ve.drain()
                    if i == 0:
                        ve.wait_ge(layer_loaded, L * 96 + 96)
                    tt(X[:, 0:2, :], X[:, 0:2, :], G[:, 2 * i:2 * i + 1, :].to_broadcast([P, 2, D]), ALU.mult)
                    ve.drain()
                    tt(X[:, 0:2, :], X[:, 0:2, :], G[:, 2 * i + 1:2 * i + 2, :].to_broadcast([P, 2, D]),
                       ALU.add).then_inc(ln_done, 1)

                residual(lambda half, t: J_OUT2[half * 2 + t])
                layer_norm(0)

                emptied(ve, at(L, J_ROUTE[0]))
                ve.wait_ge(x_rounded, L + 1)
                tt(X_PARTS[:, 1, :, :], X[:, 0:2, :], X_PARTS[:, 0, :, :], ALU.subtract)
                ts(ROUTE, ROUTE, 1.0, None, ALU.add)
                ve.drain()
                nc.vector.reciprocal(ROUTE, ROUTE)
                ve.drain()
                scores2 = ROUTE.rearrange("p (g e) -> p g e", e=4)
                tt(BIASED.rearrange("p (t g) e -> p t (g e)", t=2), ROUTE.rearrange("p (t e) -> p t e", t=2),
                   router_bias[:, :].rearrange("p (o e) -> p o e", o=1).to_broadcast([P, 2, EXPERTS]), ALU.add)
                ve.drain()
                n = 0
                for i in range(4):
                    for j in range(i + 1, 4):
                        tt(PAIR[:, :, n:n + 1], BIASED[:, :, i:i + 1], BIASED[:, :, j:j + 1], ALU.add)
                        n += 1
                mine = BIASED.rearrange("p g (j o) -> p g j o", o=1).to_broadcast([P, 16, 4, 4])
                other = BIASED.rearrange("p g (o i) -> p g o i", o=1).to_broadcast([P, 16, 4, 4])
                tt(CMP, other, mine, ALU.is_gt)
                tt(CMP2, other, mine, ALU.is_equal)
                ve.drain()
                nc.vector.reduce_max(GROUP, PAIR[:, :, 0:6], X_AXIS)
                tri = col("tri", 0, 16).rearrange("p (o j i) -> p o j i", o=1, j=4).to_broadcast([P, 16, 4, 4])
                tt(CMP2, CMP2, tri, ALU.mult)
                ve.drain()
                tt(CMP, CMP, CMP2, ALU.add)
                groups = GROUP.rearrange("p (t g) -> p t g", t=2)
                nc.vector.reduce_max(GMAX[:, 0:2], groups, X_AXIS)
                ve.drain()
                nc.vector.reduce_sum(RANK, CMP, X_AXIS)
                picks = PICK.rearrange("p (t g) -> p t g", t=2)
                top = GMAX[:, 0:2].rearrange("p (t o) -> p t o", o=1).to_broadcast([P, 2, 8])
                tt(picks, groups, top, ALU.is_equal)
                ve.drain()
                rev8 = col("rev8", 0, 8).rearrange("p (o g) -> p o g", o=1).to_broadcast([P, 2, 8])
                tt(picks, picks, rev8, ALU.mult)
                ts(RANK, RANK, 1.5, None, ALU.is_lt)
                ve.drain()
                nc.vector.reduce_max(GMAX[:, 2:4], picks, X_AXIS)
                tt(RANK, RANK, scores2, ALU.mult)
                ve.drain()
                top = GMAX[:, 2:4].rearrange("p (t o) -> p t o", o=1).to_broadcast([P, 2, 8])
                tt(picks, picks, top, ALU.is_equal)
                ve.drain().then_inc(picks_ready, 1)
                tt(RANK, RANK, PICK.rearrange("p (g o) -> p g o", o=1).to_broadcast([P, 16, 4]), ALU.mult)
                ve.drain()
                rank = RANK.rearrange("p (t g) e -> p t (g e)", t=2)
                nc.vector.reduce_sum(GMAX[:, 4:6], rank, X_AXIS)
                ve.drain()
                nc.vector.reciprocal(GMAX[:, 4:6], GMAX[:, 4:6])
                ve.drain()
                for t in range(2):
                    ts(GW[:, t, 0:EXPERTS], rank[:, t, :], GMAX[:, 4 + t:5 + t], 0.5, ALU.mult, ALU.mult)
                ve.drain()
                own = GW[:, :, 0:EXPERTS].rearrange("p t (g e) -> p t e g", e=PER_GROUP)
                nc.vector.reduce_sum(GW[:, :, EXPERTS:], own, X_AXIS)
                full_at(J_PLACE[0])
                behind = PS[J_PLACE[0][0]][:, 0:2 * GROUPS].rearrange("p (t g) -> p t g", t=2)
                stt(SLOT[:, :, 0:GROUPS], behind, 1.0, picks, ALU.add, ALU.mult)
                ts(COUNT[:, 0, :], PS[J_PLACE[0][0]][:, 2 * GROUPS:3 * GROUPS], P + 0.5, float(-PER_GROUP), ALU.is_gt,
                   ALU.mult).then_inc(*free(J_PLACE[0]))
                ve.drain()
                nc.vector.reduce_sum(SLOT[:, :, GROUPS:], SLOT[:, :, 0:GROUPS], X_AXIS)
                ts(COUNT[:, 1, :], col("rev8", 0, 8), -float(GROUPS), None, ALU.add)
                ve.drain()
                ts(SLOT[:, :, 0:GROUPS], SLOT[:, :, 0:GROUPS], -1.0, None, ALU.add)
                ts(SLOT[:, :, GROUPS:], SLOT[:, :, GROUPS:], -1.0 - P, None, ALU.add)
                tt(COUNT[:, 0, :], COUNT[:, 0, :], COUNT[:, 1, :], ALU.mult)
                ve.drain()
                nc.vector.reduce_sum(COUNT[:, 1, 0:1], COUNT[:, 0, :], X_AXIS)
                ve.drain()
                copy(over_group[:, :], COUNT[:, 1, 0:1]).then_inc(over_ready, 1)

                def place(p, first=False):
                    if not first:
                        full_at(j_slots(p - 1))
                    for t in range(2):
                        slot = SLOT[:, t, p:p + 1] if isinstance(p, int) else SLOT[:, t, bass.ds(p, 1)]
                        ts(PLACE[:, t, 0:P], iota[:, :], slot, None, ALU.is_equal)
                        ts(PLACE_ONE[:, t, :], iota[:, :], slot, None, ALU.is_equal)
                        gates = slice(p * PER_GROUP, p * PER_GROUP + PER_GROUP) if isinstance(p, int) else \
                            bass.ds(p * PER_GROUP, PER_GROUP)
                        copy(PLACE[:, t, P:], GW[:, t, gates])
                    ve.drain().then_inc(places_ready, 1)

                def scatter(p, last=False):
                    for t in range(2):
                        for half in range(2):
                            cut = slice(half * BANK, half * BANK + BANK)
                            job = j_scatter(p, t, half, last)
                            full_at(job)
                            dst = X if last else SUM
                            tt(dst[:, t, cut], SUM[:, t, cut], PS[job[0]][:, :], ALU.add).then_inc(*free(job))

                def split_half(p, i, h):
                    u, _ = unit_in(p, i)
                    ve.wait_ge(half_rounded, halves_before(L, p, i) + h + 1)
                    tt(W_PARTS[:, h, 1, :, :], half_of(u, h), W_PARTS[:, h, 0, :, :], ALU.subtract).then_inc(half_split, 1)
                    if h == 1:
                        ve.drain().then_inc(slot_free[u % 4], 1)

                def gather(p, side, first=False):
                    for half in range(2):
                        job = j_gather(p, half, first)
                        ve.wait_ge(tokens_rounded, L * (2 * PASSES) + p * 2 + (half + 1))
                        cut = slice(4 * half, 4 * half + 4)
                        tt(TOKEN_PARTS[:, side, 1, cut, :], cat(job, 4, P), TOKEN_PARTS[:, side, 0, cut, :],
                           ALU.subtract).then_inc(*free(job))

                def down(p):
                    for half in range(2):
                        job = j_down(p, half)
                        ve.wait_ge(down_rounded, L * (2 * PASSES) + p * 2 + (half + 1))
                        cut = slice(half * BANK, half * BANK + BANK)
                        tt(DOWN_PARTS[:, 1, cut], PS[job[0]][:, :], DOWN_PARTS[:, 0, cut], ALU.subtract).then_inc(*free(job))

                def experts(p, side, first=False, last=False):
                    if not last:
                        place(p + 1)
                    emptied(ve, at(L, j_slots(p)))
                    for i in range(PER_GROUP):
                        more = not (last and i == PER_GROUP - 1)
                        if more:
                            split_half(*next_expert(p, i), 0)
                        job = j_hidden(p, i)
                        ve.wait_ge(moe_th_ready, L * (PASSES * PER_GROUP) + p * PER_GROUP + (i + 1))
                        ps = PS[job[0]]
                        stt(tmp[:, i % 2, 0:T], th[:, i % 2, 0:T], 1.0, ps[:, 0:T], ALU.add, ALU.mult)
                        ve.drain()
                        stt(HIDG[:, i % 2, :], tmp[:, i % 2, 0:T], GATES[:, side, i:i + 1],
                            ps[:, T:2 * T], ALU.mult, ALU.mult).then_inc(*free(job))
                        if more:
                            split_half(*next_expert(p, i), 1)
                        if i == 0 and not first:
                            down(p - 1)
                        if i == 1 and not first:
                            scatter(p - 1)
                        if i == 2 and not last:
                            gather(p + 1, 1 - side)

                place(0, True)
                split_half(0, 0, 0)
                split_half(0, 0, 1)
                gather(0, 0, True)
                experts(0, 0, first=True)
                for t in range(2):
                    ts(SUM[:, t, :], X[:, t, :], ALPHA, None, ALU.mult)
                ve.drain()
                with ve.Fori(0, (PASSES - 3) // 2) as g:
                    experts(g * 2 + 1, 1)
                    experts(g * 2 + 2, 0)
                experts(PASSES - 2, 1)
                experts(PASSES - 1, 0, last=True)
                down(PASSES - 1)
                scatter(PASSES - 1, last=True)
                layer_norm(1)

        @block.tensor
        def _(pe):
            def ada_rows(u):
                w = loaded(pe, U_ADA[u]).rearrange("p (k n) -> p k n", k=KD)
                ps = acquire(pe, J_ADA[u][0])
                for k in range(KD):
                    q = 32 * (k % 4)
                    last = mm(ps[q:q + 32, :], SC[:, k, :], w[:, k, :], start=k < 4, stop=k >= 4, tile_position=(0, q))
                last.then_inc(*full(J_ADA[u][0]))
                release(U_ADA[u])

            def ada_result(u):
                emptied(pe, J_ADA[u][0])
                rows = tmp[:, u % 2, :]
                if u // 2 % 3 != 2:
                    job = J_ADA[u][1]
                    ps = acquire(pe, job)
                    for c in range(4):
                        last = mm(ps[:, 2 * c:2 * c + 2], rows[:, c * P:c * P + P],
                                  PICK_ROW[:, :, 0:1].rearrange("p w o -> p (w o)"), start=True, stop=True)
                    last.then_inc(*full(job))
                else:
                    for w, job in enumerate(J_ADA[u][1:]):
                        ps = acquire(pe, job)
                        mm(ps[:, :], PICK_ROW[:, w, :], rows, start=True, stop=True).then_inc(*full(job))

            def ada(group):
                for n, u in enumerate(group):
                    ada_rows(u)
                    if n:
                        ada_result(group[n - 1])
                ada_result(group[-1])

            pe.wait_ge(silu_c_ready, 1)
            pe.wait_ge(consts_loaded, 16 * N_CONSTS)
            ada(list(range(ADA_FIRST)))

            def to_features(J, n, tiles):
                pe.wait_ge(xn_ready, n)
                for k in range(KD):
                    ps = acquire(pe, J[k])
                    for t in range(tiles):
                        last = tr(ps[:, t * P:t * P + P], XN[:, t, k * P:k * P + P], ident[:, :])
                    last.then_inc(*full(J[k]))
                for job in J:
                    emptied(pe, job)

            def project(job, out, w, c0, rhs, k0=0, kn=KD, start=True):
                for k in range(kn):
                    last = mm(out, w[:, k0 + k, c0:c0 + P], rhs(k), start=k == 0, stop=k == kn - 1)
                return last

            def ffn_in(first, J, width):
                def body(i, r, g):
                    w = loaded(pe, first + r, g).rearrange("p (a k n) -> p a k n", a=2, k=KD)
                    for j in range(2):
                        for part in range(2):
                            job = J(i, 2 * j + part)
                            ps = acquire(pe, job)
                            project(job, ps[:, 0:width], w[:, part, :, :], j * P,
                                    lambda k: HT[:, k, 0:width]).then_inc(*full(job))
                    release(first + r)
                repeat(pe, 11, body)
                emptied(pe, J(10, 3))

            def ffn_out(own, J, tiles, after=((),) * 6):
                for half in range(2):
                    for part in range(3):
                        n = half * 3 + part
                        w = loaded(pe, own[n]).rearrange("p (k n) -> p k n", n=BANK)
                        for f in range(part * 8, min(part * 8 + 8, FT)):
                            for t in range(tiles):
                                job = J[half * tiles + t]
                                if f == 0:
                                    acquire(pe, job)
                                last = mm(PS[job[0]][:, :], HID[:, f, t * P:t * P + P], w[:, f - part * 8, :],
                                          start=f == 0, stop=f == FT - 1)
                                if f == FT - 1:
                                    last.then_inc(*full(job))
                        release(own[n])
                        if after[n]:
                            ada(after[n])

            to_features(J_N1, 1, 4)
            ffn_in(U_FF1A, J_FF1A, 2 * T)
            ffn_out(U_FF1B, J_FF1B, 4, ADA_AFTER)

            to_features(J_N2, 2, 4)

            def unit(name):
                u = U_MIX + MIX.index(name)
                return u, loaded(pe, u).rearrange("p (k n) -> p k n", k=KD)

            x_only = lambda k: HT[:, k, 0:T]
            both = lambda k: HT[:, k, :]

            def pairs(name, J):
                u, w = unit(name)
                for i in range(2):
                    ps = acquire(pe, J[i])
                    for a in range(2):
                        last = project(J[i], ps[:, a * T:(a + 1) * T], w, (2 * i + a) * P, x_only)
                    last.then_inc(*full(J[i]))
                release(u)

            def forget(name, J):
                u, w = unit(name)
                for h in range(HG_HEADS):
                    ps = acquire(pe, J[h])
                    project(J[h], ps[:, :], w, h * P, both).then_inc(*full(J[h]))
                release(u)

            pairs("hq", J_HQ)
            forget("hff", J_HF[0])
            u, w = unit("hi")
            for t in range(4):
                ps = acquire(pe, J_HI[t])
                for k in range(KD):
                    last = mm(ps[:, :], HT[:, k, t * P:t * P + P], w[:, k, :], start=k == 0, stop=k == KD - 1)
                last.then_inc(*full(J_HI[t]))
            release(u)
            u = U_MIX + MIX.index("ak")
            w = loaded(pe, u)[:, 0:KD * 256].rearrange("p (k n) -> p k n", k=KD)
            for i in range(2):
                ps = acquire(pe, J_AK[i])
                for a in range(2):
                    for k in range(KD):
                        t = 2 * i + a
                        last = mm(ps[:, a * 256:a * 256 + 256], HT[:, k, t * P:t * P + P], w[:, k, :],
                                  start=k == 0, stop=k == KD - 1)
                last.then_inc(*full(J_AK[i]))
            release(u)
            u, w = unit("aq")
            for t in range(2):
                ps = acquire(pe, J_AQ[t])
                for k in range(KD):
                    last = mm(ps[:, :], HT[:, k, t * P:t * P + P], w[:, k, :], start=k == 0, stop=k == KD - 1)
                last.then_inc(*full(J_AQ[t]))
            release(u)
            pairs("hg", J_HG)

            def recurrence(d):
                for i, tile in enumerate(TILES[d]):
                    n = d * 3 + i
                    pe.wait_ge(kdec_ready, n + 1)
                    job = J_KT[d][i]
                    ps = acquire(pe, job)
                    for h in range(HG_HEADS):
                        last = tr(ps[:, h * P:h * P + P], KDEC[:, h, :], ident[:, :])
                    last.then_inc(*full(job))
                    emptied(pe, job)
                    emptied(pe, J_HI[3])
                    job = J_KV[d][i]
                    ps = acquire(pe, job)
                    for h in range(HG_HEADS):
                        last = mm(ps[:, h * P:h * P + P], KDT[:, h, :], VHG[:, tile, h * P:h * P + P],
                                  start=True, stop=True)
                    last.then_inc(*full(job))

                def pair_scores(J, k_of, q_of):
                    for tile in range(2):
                        ps = acquire(pe, J[tile])
                        for h in range(HG_HEADS):
                            cut = slice(tile * P, tile * P + P)
                            last = mm(ps[:, h * P:h * P + P], k_of[:, h, cut], q_of[:, h, cut], start=True, stop=True)
                        last.then_inc(*full(J[tile]))

                names = (("ga", "ga2"), ("gh", "gh2"))[d]
                for li in range(len(LEVELS)):
                    n = d * len(LEVELS) + li
                    pe.wait_ge(qlev_ready, n + 1)
                    pe.wait_ge(klev_ready, n + 1)
                    pair_scores(J_LEV[d][li], KLEV, QLEV)
                    if li < 4:
                        u, w = unit(names[li // 2])
                        job = J_GATE[4 * d + li]
                        ps = acquire(pe, job)
                        for a in range(2):
                            last = project(job, ps[:, a * T:(a + 1) * T], w, (2 * (li % 2) + a) * P, x_only)
                        last.then_inc(*full(job))
                        if li % 2:
                            release(u)
                pair_scores(J_DIAG[d], KK, HQ)

            recurrence(0)
            forget("hfb", J_HF[1])
            recurrence(1)
            pe.wait_ge(state_ready, 1)
            for t in range(2):
                ps = acquire(pe, J_O[t])
                cut = slice(t * P, t * P + P)
                for h in range(HG_HEADS):
                    out = ps[:, h * P:h * P + P]
                    mm(out, SCORE[:, t, h, :], VHG[:, t, h * P:h * P + P], start=True, stop=False)
                    mm(out, QDEC[:, h, cut], STATE[:, t, h, :], start=False, stop=False)
                    last = mm(out, QDEC[:, 4 + h, cut], STATE[:, 2 + (1 - t), h, :], start=False, stop=True)
                last.then_inc(*full(J_O[t]))
            for t in range(2):
                emptied(pe, J_O[t])
                ps = acquire(pe, J_ORT[t])
                for m in range(4):
                    last = tr(ps[:, m * P:m * P + P], ONT[:, t, m * P:m * P + P], ident[:, :])
                last.then_inc(*full(J_ORT[t]))

            emptied(pe, J_AQ[1])
            for i in range(2):
                ps = acquire(pe, J_QT[i])
                for a in range(2):
                    for t in range(2):
                        m = 2 * i + a
                        src = QTOK[:, t, 2 * m:2 * m + 2, :].rearrange("p h n -> p (h n)")
                        last = tr(ps[:, a * T + t * P:a * T + t * P + P], src, ident[:, :])
                last.then_inc(*full(J_QT[i]))
            for g in range(2):
                ps = acquire(pe, J_KZ[g])
                for t in range(4):
                    src = KTOK[:, t, 2 * g:2 * g + 2, :].rearrange("p h n -> p (h n)")
                    last = tr(ps[:, t * P:t * P + P], src, ident[:, :])
                last.then_inc(*full(J_KZ[g]))
            for job in J_QT + J_KZ:
                emptied(pe, job)
            for b in range(2):
                for h in range(HEADS):
                    ps = acquire(pe, J_S[b][h])
                    mm(ps[:, :], QT[:, h // 2, b * P:b * P + P], KZ[:, 2 * (h // 4) + h % 2, :],
                       start=True, stop=True).then_inc(*full(J_S[b][h]))
                out = acquire(pe, J_PV[b])

                def to_keys(h):
                    pe.wait_ge(probs_ready, b * 8 + h + 1)
                    ps = acquire(pe, J_PT[b][h])
                    for t in range(4):
                        last = tr(ps[:, t * P:t * P + P], PROB[:, h, t * P:t * P + P], ident[:, :])
                    last.then_inc(*full(J_PT[b][h]))

                def weigh(h):
                    emptied(pe, J_PT[b][h])
                    g = h // 4
                    for t in range(4):
                        last = mm(out[:, h * HD:h * HD + HD], PT[:, h % 2, t * P:t * P + P],
                                  VTOK[:, t, g * HD:g * HD + HD], start=t == 0, stop=t == 3)
                    last.then_inc(*(full(J_PV[b]) if h == HEADS - 1 else (pv_done, 1)))

                to_keys(0)
                for h in range(1, HEADS):
                    to_keys(h)
                    weigh(h - 1)
                weigh(HEADS - 1)
                emptied(pe, J_PV[b])
                ps = acquire(pe, J_OT[b])
                for m in range(4):
                    last = tr(ps[:, m * P:m * P + P], OTOK[:, b, m * P:m * P + P], ident[:, :])
                last.then_inc(*full(J_OT[b]))
            emptied(pe, J_OT[1])
            emptied(pe, J_ORT[1])
            for u, J, src in ((U_WOA, J_WOA, OT), (U_WOH, J_WOH, ORT)):
                w = loaded(pe, u).rearrange("p (k n) -> p k n", k=4)
                for i in range(4):
                    ps = acquire(pe, J[i])
                    for a in range(2):
                        last = project(J[i], ps[:, a * T:(a + 1) * T], w, (2 * i + a) * P,
                                       lambda k: src[:, k, :], kn=4)
                    last.then_inc(*full(J[i]))
                release(u)
            pe.wait_ge(merged_ready, 1)
            for half in range(2):
                w = loaded(pe, U_WOUT + half).rearrange("p (k n) -> p k n", k=KD)
                for t in range(2):
                    job = J_WOUT[half * 2 + t]
                    ps = acquire(pe, job)
                    for k in range(KD):
                        last = mm(ps[:, :], MERGED[:, k, t * P:t * P + P], w[:, k, :], start=k == 0, stop=k == KD - 1)
                    last.then_inc(*full(job))
                release(U_WOUT + half)

            to_features(J_N3, 3, 2)
            ffn_in(U_FF2A, J_FF2A, T)
            ffn_out(U_FF2B, J_FF2B, 2)
            pe.wait_ge(consts2_loaded, 16 * 8)
            for h in range(2):
                pe.drain().then_inc(half_free[h], 1)
            with pe.Fori(0, LAYERS) as L:
                def take(job):
                    return acquire(pe, at(L, job))

                def taken(job):
                    emptied(pe, at(L, job))

                def landed(u, g=0):
                    pe.wait_ge(slot_loaded[u % 4], L * LAYER_DMAS[u % 4] + g * (16 * units.dmas[u]) + units.loaded(u))
                    return ring[:, u % 4, :]

                def slot(u, width, k=KD, g=0):
                    return landed(u, g)[:, 0:k * width].rearrange("p (k n) -> p k n", k=k)

                xt = lambda k: HT[:, k, 0:T]

                def to_features(J, ready):
                    pe.wait_ge(*ready)
                    for i in range(4):
                        ps = take(J[i])
                        for a in range(2):
                            for t in range(2):
                                k = 2 * i + a
                                last = tr(ps[:, a * T + t * P:a * T + t * P + P], X[:, t, k * P:k * P + P], ident[:, :])
                        last.then_inc(*full(J[i]))
                    for job in J:
                        taken(job)

                def tokens(out, w, t, c0, n, src=None, kn=KD, k0=0):
                    for k in range(kn):
                        lhs = HT[:, k, t * P:t * P + P] if src is None else src[:, k, t * P:t * P + P]
                        last = mm(out, lhs, w[:, k0 + k, c0:c0 + n], start=k == 0, stop=k == kn - 1)
                    return last

                def features(job, w, c0, tiles=2):
                    ps = take(job)
                    for a in range(tiles):
                        last = project(job, ps[:, a * T:(a + 1) * T], w, c0 + a * P, xt)
                    last.then_inc(*full(job))

                pe.wait_ge(mtok_ready, L + 1)
                to_features(J_XT, (layer_start, L + 1))
                w = slot(U_IN, 416)
                for t in range(2):
                    ps = take(J_C[t])
                    tokens(ps[:, 0:416], w, t, 0, 416).then_inc(*full(J_C[t]))
                release(U_IN)
                w = slot(U_IN + 1, BANK)
                for i in range(2):
                    features(J_SBQK[i], w, i * 256)
                release(U_IN + 1)
                taken(J_C[1])
                ps = take(J_CT[0])
                for f in range(2):
                    for t in range(2):
                        last = tr(ps[:, f * T + t * P:f * T + t * P + P], CTOK[:, t, f * P:f * P + P], ident[:, :])
                last.then_inc(*full(J_CT[0]))
                ps = take(J_CT[1])
                for t in range(2):
                    last = tr(ps[:, t * P:t * P + P], CTOK[:, t, C_Q:C_Q + C_KV], ident[:, :])
                last.then_inc(*full(J_CT[1]))
                w = slot(U_IN + 2, 384)
                for t in range(2):
                    ps = take(J_VTOK[t])
                    tokens(ps[:, 0:384], w, t, 0, 384).then_inc(*full(J_VTOK[t]))
                release(U_IN + 2)
                taken(J_CT[0])
                taken(J_CT[1])
                pe.wait_ge(layer_loaded, L * 96 + 96)
                for t in range(2):
                    ps = take(J_MQ[t])
                    tokens(ps[:, 0:384], W_UQ, t, 0, 384, src=CT, kn=2).then_inc(*full(J_MQ[t]))
                for t in range(2):
                    ps = take(J_MKV[t])
                    mm(ps[:, :], CT[:, 2, t * P:t * P + P], W_UKV, start=True, stop=True).then_inc(*full(J_MKV[t]))
                w = slot(U_IN + 3, BANK)
                for i in range(2):
                    features(J_SWQ[i], w, i * 256)
                release(U_IN + 3)
                w = slot(U_IN4, BANK)
                features(J_SWK[0], w, 0)
                ps = take(J_DFV[0])
                for t in range(2):
                    last = tokens(ps[:, t * T:(t + 1) * T], w, t, 256, 256)
                last.then_inc(*full(J_DFV[0]))
                release(U_IN4)
                w = slot(U_IN5, BANK)
                for i in range(2):
                    features(J_DFQK[i], w, i * 256)
                release(U_IN5)
                taken(J_MQ[1])
                taken(J_MKV[1])
                for J, src in ((J_MQT, MQTOK), (J_MKT, MKTOK)):
                    for i in range(2):
                        ps = take(J[i])
                        for a in range(2):
                            for t in range(2):
                                last = tr(ps[0:MLA_DIM, a * T + t * P:a * T + t * P + P], src[:, t, 2 * i + a, :], ident[:, :])
                        last.then_inc(*full(J[i]))

                gates_done = [0]

                def gate(n):
                    for i in range(gates_done[0], gates_done[0] + n):
                        u = U_GATES + i // 2
                        features(J_G2[i], slot(u, BANK), (i % 2) * 256)
                        if i % 2:
                            release(u)
                    gates_done[0] += n

                taken(J_SBQK[0])
                taken(J_SBQK[1])
                for h in range(4):
                    ps = take(J_SBZ[h])
                    for kt in range(2):
                        last = mm(ps[:, kt * T:(kt + 1) * T], SBKZ[:, h, kt * P:kt * P + P], SBQT[:, h // 2, :],
                                  start=True, stop=True)
                    last.then_inc(*full(J_SBZ[h]))
                taken(J_MQT[1])
                taken(J_MKT[1])
                gate(4)
                pe.wait_ge(sb_l_ready, L + 1)
                for h in range(4):
                    ps = take(J_SBS[h])
                    l0, l1 = SB_L[:, 2 * h, :], SB_L[:, 2 * h + 1, :]
                    mm(ps[:, 0:T], later[:, :], l0, start=True, stop=False)
                    mm(ps[:, 0:T], ones[:, :], l1, start=False, stop=True)
                    mm(ps[:, T:2 * T], later[:, :], l1, start=True, stop=True).then_inc(*full(J_SBS[h]))
                gate(2)
                pe.wait_ge(sbo_ready, L + 1)
                taken(J_VTOK[0])
                taken(J_VTOK[1])
                ps = take(J_SBO[0])
                for b in range(2):
                    for h in range(4):
                        for kt in range(2):
                            last = mm(ps[:, b * T + h * HD:b * T + h * HD + HD], SB_E[:, 2 * h + kt, b * P:b * P + P],
                                      SBV[:, kt, h * HD:h * HD + HD], start=kt == 0, stop=kt == 1)
                last.then_inc(*full(J_SBO[0]))
                taken(J_SBO[0])
                ps = take(J_SBX[0])
                for f in range(2):
                    for b in range(2):
                        last = tr(ps[:, f * T + b * P:f * T + b * P + P], th[:, 0, b * T + f * P:b * T + f * P + P], ident[:, :])
                last.then_inc(*full(J_SBX[0]))

                def scores(n):
                    kind, b = SOFT[n]
                    cut = slice(b * P, b * P + P)
                    if n == 0:
                        taken(J_SWQ[1])
                        taken(J_DFQK[0])
                        taken(J_SWK[0])
                        taken(J_DFQK[1])
                    for i, job in enumerate(J_SM[n]):
                        ps = take(job)
                        for a in range(2):
                            m = 2 * i + a
                            if kind == "mla":
                                q, k = MQT[0:MLA_DIM, m, cut], MKT[0:MLA_DIM, m, :]
                            elif kind == "sw":
                                q, k = SWQT[:, m // 2, cut], SWKZ[:, 2 * (m // 4) + m % 2, :]
                            else:
                                q, k = DFQT[:, m // 4, cut], DFKZ[:, m, :]
                            last = mm(ps[:, a * T:(a + 1) * T], q, k, start=True, stop=True)
                        last.then_inc(*full(job))

                def outputs(n):
                    kind, b = SOFT[n]
                    side, heads = n % 2, OUT_HEADS[kind]
                    step = 2 if kind == "df" else 1

                    def to_keys(i):
                        if kind == "df":
                            pe.wait_ge(mixed_ready, L * 2 + b + 1)
                        else:
                            pe.wait_ge(probs2_ready, L * N_MAPS + maps_before(n) + 2 * i + 2)
                        ps = take(J_PB[n][i])
                        for a in range(2):
                            for kt in range(2):
                                c = (2 * a + kt) * P
                                last = tr(ps[:, c:c + P], PB[side][:, (2 * i + a) * step, kt * P:kt * P + P], ident[:, :])
                        last.then_inc(*full(J_PB[n][i]))

                    def weigh(out, i):
                        taken(J_PB[n][i])
                        for a in range(2):
                            h = 2 * i + a
                            for kt in range(2):
                                if kind == "mla":
                                    v = MV[:, kt, h, :]
                                elif kind == "sw":
                                    v = SWV[:, kt, h // 4 * HD:h // 4 * HD + HD]
                                else:
                                    v = DFV[:, kt, h * HD:h * HD + HD]
                                c = (2 * a + kt) * P
                                last = mm(out[:, h * HD:h * HD + HD], tmp[:, i % 2, c:c + P], v, start=kt == 0, stop=kt == 1)
                        return last

                    n_pairs = heads // 2
                    out = None
                    for i in range(n_pairs + 1):
                        if i < n_pairs:
                            to_keys(i)
                        if i:
                            if out is None:
                                out = take(J_OV[n])
                            last = weigh(out, i - 1)
                            if i < n_pairs:
                                last.then_inc(pv2_done, 1)
                    last.then_inc(*full(J_OV[n]))
                    nc.tensor.drain().then_inc(pv2_done, 1)
                    taken(J_OV[n])
                    ps = take(J_OX[n])
                    for f in range(heads // 2):
                        last = tr(ps[:, f * P:f * P + P], th[:, 0, f * P:f * P + P], ident[:, :])
                    last.then_inc(*full(J_OX[n]))

                scores(0)
                for n in range(6):
                    if n < 5:
                        gate(2)
                        scores(n + 1)
                    outputs(n)

                for j in range(4):
                    kn = BRANCH_TILES[j]
                    if j == 0:
                        taken(J_OX[1])
                        taken(J_OX[3])
                        taken(J_OX[5])
                    w = slot(U_BR + j, D, kn)
                    for i in range(4):
                        ps = take(J_BR[j][i])
                        for a in range(2):
                            last = project(J_BR[j][i], ps[:, a * T:(a + 1) * T], w, (2 * i + a) * P,
                                           lambda k: OTS[j][:, k, :], kn=kn)
                        last.then_inc(*full(J_BR[j][i]))
                    release(U_BR + j)
                pe.wait_ge(merged2_ready, L + 1)
                for half in range(2):
                    w = slot(U_OUT2 + half, BANK)
                    for t in range(2):
                        job = J_OUT2[half * 2 + t]
                        tokens(take(job)[:, :], w, t, 0, BANK, src=MERGED2).then_inc(*full(job))
                    release(U_OUT2 + half)

                to_features(J_XT2, (ln_done, L * 2 + 1))
                ps = take(J_ROUTE[0])
                for t in range(2):
                    last = tokens(ps[:, t * EXPERTS:(t + 1) * EXPERTS], w_router, t, 0, EXPERTS)
                last.then_inc(*full(J_ROUTE[0]))

                pe.wait_ge(picks_ready, L + 1)
                ps = take(J_PLACE[0])
                picks = [PICK[:, t * GROUPS:(t + 1) * GROUPS] for t in range(2)]
                mm(ps[:, 0:GROUPS], later[:, :], picks[0], start=True, stop=False)
                mm(ps[:, 0:GROUPS], ones[:, :], picks[1], start=False, stop=True)
                mm(ps[:, GROUPS:2 * GROUPS], later[:, :], picks[1], start=True, stop=True)
                mm(ps[:, 2 * GROUPS:3 * GROUPS], ones[:, :], picks[0], start=True, stop=False)
                mm(ps[:, 2 * GROUPS:3 * GROUPS], ones[:, :], picks[1], start=False, stop=True).then_inc(*full(J_PLACE[0]))

                def gather(p, first=False):
                    pe.wait_ge(places_ready, L * PASSES + p + 1)
                    for half in range(2):
                        job = j_gather(p, half, first)
                        ps = take(job)
                        for a in range(4):
                            k = 4 * half + a
                            for t in range(2):
                                for part in range(2):
                                    last = mm(ps[:, a * P:a * P + P], X_PARTS[:, part, t, k * P:k * P + P], PLACE_ONE[:, t, :],
                                              start=t == part == 0, stop=t == part == 1)
                        last.then_inc(*full(job))
                    ps = take(j_slots(p))
                    for t in range(2):
                        tr(ps[:, t * P:t * P + P], PLACE[:, t, 0:P], ident[:, :])
                    for t in range(2):
                        last = mm(ps[:, 2 * P:2 * P + PER_GROUP], PLACE[:, t, 0:P], PLACE[:, t, P:], start=t == 0, stop=t == 1)
                    last.then_inc(*full(j_slots(p)))

                def turn(p, i, first=False):
                    job = j_turn(p, i)
                    taken(j_hidden(p, i))
                    ps = take(job) if first and i == 0 else PS[job[0]]
                    for f in range(2):
                        last = tr(ps[:, f * P:f * P + P], HIDG[:, i % 2, f * P:f * P + P], ident[:, :])
                    last.then_inc(*full(job))

                def down(p, i, first=False):
                    u, turns = unit_out(p, i)
                    w = slot(u, D, 2, turns)
                    taken(j_turn(p, i))
                    for half in range(2):
                        job = j_down(p, half)
                        ps = take(job) if first and i == 0 else PS[job[0]]
                        for f in range(2):
                            last = mm(ps[:, :], HIDT[:, i % 2, f * P:f * P + P], w[:, f, half * BANK:half * BANK + BANK],
                                      start=i == 0 and f == 0, stop=i == PER_GROUP - 1 and f == 1)
                        if i == PER_GROUP - 1:
                            last.then_inc(*full(job))
                    release(u)

                def scatter(p, side, last=False):
                    taken(j_down(p, 1))
                    for t in range(2):
                        for half in range(2):
                            job = j_scatter(p, t, half, last)
                            ps = take(job)
                            for part in range(2):
                                done = mm(ps[:, :], PLACE_T[:, side, t * P:t * P + P],
                                          DOWN_PARTS[:, part, half * BANK:half * BANK + BANK], start=part == 0, stop=part == 1)
                            done.then_inc(*full(job))

                def experts(p, side, first=False, last=False):
                    taken(j_gather(p, 1, first))
                    for i in range(PER_GROUP):
                        job = j_hidden(p, i)
                        ps = take(job) if first and i < 2 else PS[job[0]]
                        for h in range(2):
                            if h and i:
                                turn(p, i - 1, first)
                            elif h and not first:
                                turn(p - 1, PER_GROUP - 1)
                            pe.wait_ge(half_split, halves_before(L, p, i) + h + 1)
                            for k in range(KD // 2):
                                for n, (x, w) in enumerate(((0, 0), (0, 1), (1, 0))):
                                    done = mm(ps[:, :], TOKEN_PARTS[:, side, x, h * 4 + k, :], W_PARTS[:, h, w, k, :],
                                              start=h == k == n == 0, stop=h == 1 and k == 3 and n == 2)
                            if h == 1:
                                done.then_inc(*full(job))
                            pe.drain().then_inc(half_free[h], 1)
                        if i == 1 and not first:
                            scatter(p - 1, 1 - side)
                        if i:
                            down(p, i - 1, first)
                        elif not first:
                            down(p - 1, PER_GROUP - 1)
                        if i == 2 and not last:
                            gather(p + 1)

                gather(0, True)
                experts(0, 0, first=True)
                with pe.Fori(0, (PASSES - 3) // 2) as g:
                    experts(g * 2 + 1, 1)
                    experts(g * 2 + 2, 0)
                experts(PASSES - 2, 1)
                experts(PASSES - 1, 0, last=True)
                turn(PASSES - 1, PER_GROUP - 1)
                down(PASSES - 1, PER_GROUP - 1)
                scatter(PASSES - 1, 0, last=True)


def vector_pack(a):
    parts = [a["c"], a["c_ctx"], a["b_ada"], a["norm_pre"], a["hgrn_lb_fwd"], a["hgrn_lb_bwd"], a["hgrn_norm"]]
    pack = np.concatenate([np.asarray(p).reshape(-1, P) for p in parts]).T
    return pack


_LAYER_WEIGHTS = ("w_in", "w_gate", "w_br_a", "w_br_b", "w_br_c", "w_br_d", "w_out", "moe_w1", "moe_w3", "moe_w2",
                  "w_uq", "w_ukv")
_LAYER_VECTORS = ("ln1_g", "ln1_b", "ln2_g", "ln2_b", "df_lq1", "df_lk1", "df_lq2", "df_lk2", "sw_sinks")
_WEIGHTS = ("w_ada", "ffn1_w_in", "ffn1_w_out", "ffn2_w_in", "ffn2_w_out", "mix_w_in", "w_o_attn", "w_o_hgrn", "w_out")
_VECTORS = ("norm_post", "b_ada", "attn_sink")


def kernel(**inputs):
    from concourse import bacc
    from concourse.bass_utils import run_bass_kernel_spmd

    a = {k: np.asarray(v) for k, v in inputs.items()}
    k = shape_constants()
    data = {n: a[n][0] for n in _WEIGHTS + _VECTORS}
    data["x"], data["ctx"] = a["x"][0], a["ctx"][0]
    for n in _LAYER_WEIGHTS:
        data["l_" + n] = a[n + "_2"].reshape(-1, a[n + "_2"].shape[-1])
    for n in _LAYER_VECTORS:
        data[n] = a[n + "_2"]
    data["w_router"], data["router_bias"] = a["w_router_2"], a["router_bias_2"]
    positions = a["positions_2"]
    data["pos_cols"], data["pos_row"] = positions.reshape(2, P).T, positions
    layer_cols = []
    for l in range(LAYERS):
        layer_cols += [a["b_gate_2"][l].reshape(32, P), a["mla_q_norm_2"][l].reshape(2, P),
                       a["mla_kv_norm_2"][l].reshape(1, P), np.tile(a["df_subln_2"][l], 2).reshape(1, P)]
    data["cols"] = np.ascontiguousarray(np.concatenate(
        [vector_pack(a), k["halves"], k["quarters"], k["rev8"], k["tri"], np.concatenate(layer_cols).T], axis=1))
    for n in ("pick_row", "pair_masks", "ident", "reset", "window", "rope", "causal", "slide", "later", "iota", "sb_mask", "inv_freq", "lam_init"):
        data[n] = k[n]
    data = {n: np.ascontiguousarray(v) for n, v in data.items()}

    nc = bacc.Bacc("TRN2", target_bir_lowering=False, num_devices=1,
                   dynamic_dma_scratch_size=1024)
    io = {n: nc.dram_tensor(f"in_{n}", v.shape, mybir.dt.from_np(v.dtype), kind="ExternalInput").ap()
          for n, v in data.items()}
    io["out"] = nc.dram_tensor("out", (T, D), mybir.dt.float32, kind="ExternalOutput").ap()
    build_program(nc, io)
    r = run_bass_kernel_spmd(nc, [{f"in_{n}": v for n, v in data.items()}], core_ids=[0])
    return r.results[0]["out"].reshape(1, T, D)
```
